# Optimizing a Trainium2 kernel written in Bass

```python
import jax, jax.numpy as jnp
from jax import lax
import numpy as np
import math
import jax
import jax.numpy as jnp

D_MODEL = 1024
BATCH = 1
SEQ = 256
DEPTH = 2

HEAD_DIM = 64
ROT_DIM = HEAD_DIM // 4
ROPE_THETA = 500000.0
NORM_EPS = 1e-6
NEG_INF = -1e30

MOBA_HEADS = 8
MOBA_BLOCK = 256
MOBA_TOPK = 3
MOBA_Q_CHUNK = 32

NSA_HEADS = 8
NSA_KV_HEADS = 2
NSA_GROUP = NSA_HEADS // NSA_KV_HEADS
NSA_CMP_LEN = 32
NSA_CMP_STRIDE = 16
NSA_CMP_HIDDEN = 256
NSA_SEL_BLOCK = 64
NSA_SEL_TOPK = 16
NSA_WINDOW = 512
NSA_Q_CHUNK = 32
NSA_FORCE = 1e4

DIFF_HEADS = 8
DIFF_QK_DIM = HEAD_DIM
DIFF_V_DIM = 2 * HEAD_DIM
DIFF_Q_CHUNK = 128

FFN_HIDDEN = -(-8 * D_MODEL // (3 * 256)) * 256

MOBA_W = MOBA_HEADS * HEAD_DIM
NSA_Q_W = NSA_HEADS * HEAD_DIM
NSA_KV_W = 3 * 2 * NSA_KV_HEADS * HEAD_DIM
NSA_GATE_W = 3 * NSA_HEADS
SPARSE_IN = 3 * MOBA_W + NSA_Q_W + NSA_KV_W + NSA_GATE_W
SPARSE_SPLITS = [MOBA_W, 2 * MOBA_W, 3 * MOBA_W, 3 * MOBA_W + NSA_Q_W, 3 * MOBA_W + NSA_Q_W + NSA_KV_W]
SPARSE_OUT = MOBA_W + NSA_Q_W
DIFF_IN = 2 * DIFF_HEADS * 2 * DIFF_QK_DIM + DIFF_HEADS * DIFF_V_DIM
DIFF_OUT = DIFF_HEADS * DIFF_V_DIM


def rms_norm(t, gain):
    tf = t.astype(jnp.float32)
    y = tf * lax.rsqrt(jnp.mean(tf * tf, axis=-1, keepdims=True) + NORM_EPS)
    return (y * gain.astype(jnp.float32)).astype(t.dtype)

def rope_tables(positions):
    inv_freq = 1.0 / (ROPE_THETA ** (jnp.arange(0, ROT_DIM, 2, dtype=jnp.float32) / ROT_DIM))
    ang = positions.astype(jnp.float32)[:, None, :, None] * inv_freq
    return jnp.cos(ang), jnp.sin(ang)

def partial_rope(t, cos, sin):
    half = ROT_DIM // 2
    cos = cos.astype(t.dtype)
    sin = sin.astype(t.dtype)
    t1, t2, rest = t[..., :half], t[..., half:ROT_DIM], t[..., ROT_DIM:]
    return jnp.concatenate([t1 * cos - t2 * sin, t2 * cos + t1 * sin, rest], axis=-1)

def masked_softmax(s, valid):
    s = jnp.where(valid, s.astype(jnp.float32), NEG_INF)
    return jax.nn.softmax(s, axis=-1) * valid

def moba_attention(q, k, v):
    B, H, S, dh = q.shape
    Qc = MOBA_Q_CHUNK
    nb = -(-S // MOBA_BLOCK)
    pad = nb * MOBA_BLOCK - S
    kb = jnp.pad(k, ((0, 0), (0, 0), (0, pad), (0, 0))).reshape(B, H, nb, MOBA_BLOCK, dh)
    vb = jnp.pad(v, ((0, 0), (0, 0), (0, pad), (0, 0))).reshape(B, H, nb, MOBA_BLOCK, dh)
    kmean = jnp.mean(kb.astype(jnp.float32), axis=3)
    topk = min(MOBA_TOPK, nb)
    scale = dh ** -0.5
    bi = jnp.arange(B)[:, None, None, None]
    hi = jnp.arange(H)[None, :, None, None]
    blk = jnp.arange(nb)
    off = jnp.arange(MOBA_BLOCK)

    def one_chunk(ci):
        t0 = ci * Qc
        pos = t0 + jnp.arange(Qc)
        own = t0 // MOBA_BLOCK
        qc = lax.dynamic_slice_in_dim(q, t0, Qc, axis=2)
        gate = jnp.einsum('bhqd,bhnd->bhqn', qc.astype(jnp.float32), kmean)
        gate = jnp.where(blk < own, gate, NEG_INF)
        gval, idx = lax.top_k(gate, topk)
        sel_ok = gval > 0.5 * NEG_INF
        k_sel = kb[bi, hi, idx]
        v_sel = vb[bi, hi, idx]
        k_own = lax.dynamic_index_in_dim(kb, own, axis=2, keepdims=False)
        v_own = lax.dynamic_index_in_dim(vb, own, axis=2, keepdims=False)
        s_sel = jnp.einsum('bhqd,bhqnjd->bhqnj', qc, k_sel).reshape(B, H, Qc, topk * MOBA_BLOCK)
        s_own = jnp.einsum('bhqd,bhjd->bhqj', qc, k_own)
        ok_sel = jnp.broadcast_to(sel_ok[..., None], (B, H, Qc, topk, MOBA_BLOCK)).reshape(B, H, Qc, topk * MOBA_BLOCK)
        ok_own = jnp.broadcast_to((own * MOBA_BLOCK + off)[None, :] <= pos[:, None], (B, H, Qc, MOBA_BLOCK))
        p = masked_softmax(jnp.concatenate([s_sel, s_own], axis=-1) * scale,
                           jnp.concatenate([ok_sel, ok_own], axis=-1)).astype(v.dtype)
        p_sel = p[..., :topk * MOBA_BLOCK].reshape(B, H, Qc, topk, MOBA_BLOCK)
        p_own = p[..., topk * MOBA_BLOCK:]
        return (jnp.einsum('bhqnj,bhqnjd->bhqd', p_sel, v_sel)
                + jnp.einsum('bhqj,bhjd->bhqd', p_own, v_own))

    out = lax.map(one_chunk, jnp.arange(S // Qc))
    return out.transpose(1, 2, 0, 3, 4).reshape(B, H, S, dh)

def nsa_compress(t, pos_emb, w1, w2):
    S = t.shape[2]
    ncmp = (S - NSA_CMP_LEN) // NSA_CMP_STRIDE + 1
    idx = np.arange(ncmp)[:, None] * NSA_CMP_STRIDE + np.arange(NSA_CMP_LEN)[None, :]
    blocks = t[:, :, idx] + pos_emb
    hid = jax.nn.silu(jnp.einsum('bgnld,lde->bgne', blocks, w1))
    return jnp.einsum('bgne,ed->bgnd', hid, w2)

def nsa_overlap(ncmp, nsel):
    cs = np.arange(ncmp) * NSA_CMP_STRIDE
    ss = np.arange(nsel) * NSA_SEL_BLOCK
    ov = np.minimum(cs[:, None] + NSA_CMP_LEN, ss[None, :] + NSA_SEL_BLOCK) - np.maximum(cs[:, None], ss[None, :])
    return jnp.asarray(np.clip(ov, 0, None) / NSA_CMP_LEN, dtype=jnp.float32)

def nsa_attention(q, kc, vc, ks, vs, kw, vw, gates):
    B, H, S, dh = q.shape
    G, R, Qc, SB, W = NSA_KV_HEADS, NSA_GROUP, NSA_Q_CHUNK, NSA_SEL_BLOCK, NSA_WINDOW
    ncmp = kc.shape[2]
    nsel = S // SB
    topk = min(NSA_SEL_TOPK, nsel)
    scale = dh ** -0.5
    cmp_end = jnp.arange(ncmp) * NSA_CMP_STRIDE + NSA_CMP_LEN - 1
    overlap = nsa_overlap(ncmp, nsel)
    ksb = ks.reshape(B, G, nsel, SB, dh)
    vsb = vs.reshape(B, G, nsel, SB, dh)
    kwp = jnp.pad(kw, ((0, 0), (0, 0), (W, 0), (0, 0)))
    vwp = jnp.pad(vw, ((0, 0), (0, 0), (W, 0), (0, 0)))
    bi = jnp.arange(B)[:, None, None, None]
    gi = jnp.arange(G)[None, :, None, None]
    sel_blk = jnp.arange(nsel)
    sel_off = jnp.arange(SB)
    win_off = jnp.arange(W + Qc)

    def one_chunk(ci):
        t0 = ci * Qc
        pos = t0 + jnp.arange(Qc)
        qg = lax.dynamic_slice_in_dim(q, t0, Qc, axis=2).reshape(B, G, R, Qc, dh)
        g = lax.dynamic_slice_in_dim(gates, t0, Qc, axis=2).reshape(B, G, R, Qc, 3)
        ok_c = cmp_end[None, :] <= pos[:, None]
        p_c = masked_softmax(jnp.einsum('bgrqd,bgnd->bgrqn', qg, kc) * scale, ok_c)
        o_c = jnp.einsum('bgrqn,bgnd->bgrqd', p_c.astype(vc.dtype), vc)
        imp = jnp.einsum('bgqn,nm->bgqm', p_c.sum(axis=2), overlap)
        cur = pos // SB
        ok_blk = sel_blk[None, :] <= cur[:, None]
        forced = ok_blk & ((sel_blk[None, :] == 0) | (sel_blk[None, :] >= cur[:, None] - 1))
        score = jnp.where(ok_blk, jnp.where(forced, NSA_FORCE, imp), NEG_INF)
        sval, idx = lax.top_k(score, topk)
        sel_ok = sval > 0.5 * NEG_INF
        k_sel = ksb[bi, gi, idx]
        v_sel = vsb[bi, gi, idx]
        tok = idx[..., None] * SB + sel_off
        ok_s = (sel_ok[..., None] & (tok <= pos[None, None, :, None, None])).reshape(B, G, 1, Qc, topk * SB)
        s_s = jnp.einsum('bgrqd,bgqnjd->bgrqnj', qg, k_sel).reshape(B, G, R, Qc, topk * SB) * scale
        p_s = masked_softmax(s_s, ok_s).astype(vs.dtype).reshape(B, G, R, Qc, topk, SB)
        o_s = jnp.einsum('bgrqnj,bgqnjd->bgrqd', p_s, v_sel)
        k_w = lax.dynamic_slice_in_dim(kwp, t0, W + Qc, axis=2)
        v_w = lax.dynamic_slice_in_dim(vwp, t0, W + Qc, axis=2)
        kpos = t0 - W + win_off
        ok_w = (kpos[None, :] <= pos[:, None]) & (kpos[None, :] > pos[:, None] - W) & (kpos[None, :] >= 0)
        p_w = masked_softmax(jnp.einsum('bgrqd,bgkd->bgrqk', qg, k_w) * scale, ok_w)
        o_w = jnp.einsum('bgrqk,bgkd->bgrqd', p_w.astype(vw.dtype), v_w)
        o = g[..., 0:1] * o_c + g[..., 1:2] * o_s + g[..., 2:3] * o_w
        return o.reshape(B, H, Qc, dh)

    out = lax.map(one_chunk, jnp.arange(S // Qc))
    return out.transpose(1, 2, 0, 3, 4).reshape(B, H, S, dh)

def to_heads(t, n_heads):
    B, S, _ = t.shape
    return t.reshape(B, S, n_heads, HEAD_DIM).transpose(0, 2, 1, 3)

def qk_prep(t, gain, cos, sin):
    return partial_rope(rms_norm(t, gain), cos, sin)

def sparse_mixer(h, cos, sin, w_in, w_out, moba_qn, moba_kn, nsa_qn, nsa_kn, cmp_pos, cmp_w1, cmp_w2):
    B, S, _ = h.shape
    mq, mk, mv, nq, nkv, ng = jnp.split(h @ w_in, SPARSE_SPLITS, axis=-1)
    o_moba = moba_attention(qk_prep(to_heads(mq, MOBA_HEADS), moba_qn, cos, sin),
                            qk_prep(to_heads(mk, MOBA_HEADS), moba_kn, cos, sin),
                            to_heads(mv, MOBA_HEADS))
    kv = nkv.reshape(B, S, 3, 2, NSA_KV_HEADS, HEAD_DIM).transpose(2, 3, 0, 4, 1, 5)
    kc = nsa_compress(qk_prep(kv[0, 0], nsa_kn[0], cos, sin), cmp_pos[0], cmp_w1[0], cmp_w2[0])
    vc = nsa_compress(kv[0, 1], cmp_pos[1], cmp_w1[1], cmp_w2[1])
    gates = jax.nn.sigmoid(ng).reshape(B, S, 3, NSA_HEADS).transpose(0, 3, 1, 2)
    o_nsa = nsa_attention(qk_prep(to_heads(nq, NSA_HEADS), nsa_qn, cos, sin), kc, vc,
                          qk_prep(kv[1, 0], nsa_kn[1], cos, sin), kv[1, 1],
                          qk_prep(kv[2, 0], nsa_kn[2], cos, sin), kv[2, 1], gates)
    o = jnp.concatenate([o_moba, o_nsa], axis=1).transpose(0, 2, 1, 3).reshape(B, S, SPARSE_OUT)
    return o @ w_out

def diff_mixer(h, cos, sin, w_in, w_out, q_norm, k_norm, lam_params, out_norm, lam_init):
    B, S, _ = h.shape
    H, Qc = DIFF_HEADS, DIFF_Q_CHUNK
    qk_w = H * 2 * DIFF_QK_DIM
    q, k, v = jnp.split(h @ w_in, [qk_w, 2 * qk_w], axis=-1)
    cos5, sin5 = cos[:, :, None], sin[:, :, None]
    q = partial_rope(rms_norm(q.reshape(B, S, H, 2, DIFF_QK_DIM).transpose(0, 2, 3, 1, 4), q_norm), cos5, sin5)
    k = partial_rope(rms_norm(k.reshape(B, S, H, 2, DIFF_QK_DIM).transpose(0, 2, 3, 1, 4), k_norm), cos5, sin5)
    v = v.reshape(B, S, H, DIFF_V_DIM).transpose(0, 2, 1, 3)
    lp = lam_params.astype(jnp.float32)
    lam = jnp.exp(jnp.sum(lp[0] * lp[1])) - jnp.exp(jnp.sum(lp[2] * lp[3])) + lam_init
    scale = DIFF_QK_DIM ** -0.5
    key_idx = jnp.arange(S)

    def one_chunk(ci):
        t0 = ci * Qc
        pos = t0 + jnp.arange(Qc)
        qc = lax.dynamic_slice_in_dim(q, t0, Qc, axis=3)
        s = jnp.einsum('bhcqd,bhckd->bhcqk', qc, k) * scale
        p = masked_softmax(s, key_idx[None, :] <= pos[:, None])
        a = p[:, :, 0] - lam * p[:, :, 1]
        return jnp.einsum('bhqk,bhkd->bhqd', a.astype(v.dtype), v)

    o = lax.map(one_chunk, jnp.arange(S // Qc)).transpose(1, 2, 0, 3, 4).reshape(B, H, S, DIFF_V_DIM)
    o = rms_norm(o, out_norm) * (1.0 - lam_init)
    return o.transpose(0, 2, 1, 3).reshape(B, S, DIFF_OUT) @ w_out

def swiglu(h, w_gate, w_up, w_down):
    return (jax.nn.silu(h @ w_gate) * (h @ w_up)) @ w_down

def first_inputs(seed: int = 0) -> dict:
    key = jax.random.key(seed)
    keys = iter(jax.random.split(key, 40))
    n_even = (DEPTH + 1) // 2
    n_odd = DEPTH // 2

    def nrm(shape, scale):
        return jax.random.normal(next(keys), shape, jnp.float32) * scale

    def gain(shape):
        return 1.0 + nrm(shape, 0.05)

    offsets = jax.random.randint(next(keys), (BATCH, 1), 0, 1024, dtype=jnp.int32)
    positions = offsets + jnp.arange(SEQ, dtype=jnp.int32)[None, :]
    return {
        'x': nrm((BATCH, SEQ, D_MODEL), 1.0),
        'c': nrm((BATCH, D_MODEL), 1.0),
        'positions': positions,
        'ada_w': nrm((DEPTH, D_MODEL, 6 * D_MODEL), 0.5 * D_MODEL ** -0.5),
        'ada_b': nrm((DEPTH, 6 * D_MODEL), 0.02),
        'attn_norm': gain((DEPTH, D_MODEL)),
        'ffn_norm': gain((DEPTH, D_MODEL)),
        'ffn_w_gate': nrm((DEPTH, D_MODEL, FFN_HIDDEN), D_MODEL ** -0.5),
        'ffn_w_up': nrm((DEPTH, D_MODEL, FFN_HIDDEN), D_MODEL ** -0.5),
        'ffn_w_down': nrm((DEPTH, FFN_HIDDEN, D_MODEL), FFN_HIDDEN ** -0.5),
        'sp_w_in': nrm((n_even, D_MODEL, SPARSE_IN), D_MODEL ** -0.5),
        'sp_w_out': nrm((n_even, SPARSE_OUT, D_MODEL), SPARSE_OUT ** -0.5),
        'moba_q_norm': gain((n_even, HEAD_DIM)),
        'moba_k_norm': gain((n_even, HEAD_DIM)),
        'nsa_q_norm': gain((n_even, HEAD_DIM)),
        'nsa_k_norm': gain((n_even, 3, HEAD_DIM)),
        'nsa_cmp_pos': nrm((n_even, 2, NSA_CMP_LEN, HEAD_DIM), 0.1),
        'nsa_cmp_w1': nrm((n_even, 2, NSA_CMP_LEN, HEAD_DIM, NSA_CMP_HIDDEN), (NSA_CMP_LEN * HEAD_DIM) ** -0.5),
        'nsa_cmp_w2': nrm((n_even, 2, NSA_CMP_HIDDEN, HEAD_DIM), NSA_CMP_HIDDEN ** -0.5),
        'diff_w_in': nrm((n_odd, D_MODEL, DIFF_IN), D_MODEL ** -0.5),
        'diff_w_out': nrm((n_odd, DIFF_OUT, D_MODEL), DIFF_OUT ** -0.5),
        'diff_q_norm': gain((n_odd, DIFF_QK_DIM)),
        'diff_k_norm': gain((n_odd, DIFF_QK_DIM)),
        'diff_lambda': nrm((n_odd, 4, DIFF_QK_DIM), 0.1),
        'diff_out_norm': gain((n_odd, DIFF_V_DIM)),
    }

def first_block(x, c, positions, ada_w, ada_b, attn_norm, ffn_norm, ffn_w_gate, ffn_w_up, ffn_w_down,
              sp_w_in, sp_w_out, moba_q_norm, moba_k_norm, nsa_q_norm, nsa_k_norm, nsa_cmp_pos,
              nsa_cmp_w1, nsa_cmp_w2, diff_w_in, diff_w_out, diff_q_norm, diff_k_norm, diff_lambda,
              diff_out_norm):
    cos, sin = rope_tables(positions)
    for i in range(DEPTH):
        mod = jax.nn.silu(c) @ ada_w[i] + ada_b[i]
        sh_a, sc_a, g_a, sh_f, sc_f, g_f = jnp.split(mod[:, None, :], 6, axis=-1)
        h = rms_norm(x, attn_norm[i]) * (1.0 + sc_a) + sh_a
        j = i // 2
        if i % 2 == 0:
            y = sparse_mixer(h, cos, sin, sp_w_in[j], sp_w_out[j], moba_q_norm[j], moba_k_norm[j],
                             nsa_q_norm[j], nsa_k_norm[j], nsa_cmp_pos[j], nsa_cmp_w1[j], nsa_cmp_w2[j])
        else:
            lam_init = 0.8 - 0.6 * float(np.exp(-0.3 * i))
            y = diff_mixer(h, cos, sin, diff_w_in[j], diff_w_out[j], diff_q_norm[j], diff_k_norm[j],
                           diff_lambda[j], diff_out_norm[j], lam_init)
        x = x + g_a * y
        h = rms_norm(x, ffn_norm[i]) * (1.0 + sc_f) + sh_f
        x = x + g_f * swiglu(h, ffn_w_gate[i], ffn_w_up[i], ffn_w_down[i])
    return x


DEPTH_2 = 1

GRID_W = 64
CTX_LEN = 256

N_MIXERS = 2
MIXER_DELTA = 0
MIXER_HYENA = 1
N_DELTA_LAYERS = (DEPTH_2 - MIXER_DELTA + N_MIXERS - 1) // N_MIXERS
N_HYENA_LAYERS = (DEPTH_2 - MIXER_HYENA + N_MIXERS - 1) // N_MIXERS

EPS = 1e-6

DN_HEAD_DIM = 128
DN_HEADS = D_MODEL // DN_HEAD_DIM
DN_INNER = DN_HEADS * DN_HEAD_DIM
DN_CONV = 5
DN_CHUNK = 64
DN_CHUNK_LOG2 = 6
DN_PROJ = 4 * DN_INNER + 4 * DN_HEADS

HY_WIDTH = D_MODEL
HY_SHORT = 3
HY_BANDS = 16
HY_EMB = 1 + 2 * HY_BANDS
HY_FF = 64
HY_FAST = 0.3
HY_SLOW = 1.5
HY_TARGET = 1e-2

PEER_HEADS = 8
PEER_NKEYS = 128
PEER_EXPERTS = PEER_NKEYS * PEER_NKEYS
PEER_DK = 256
PEER_TOPK = 16
PEER_BLOCK = 128


def _rmsnorm(x, g):
    xf = x.astype(jnp.float32)
    y = xf * lax.rsqrt(jnp.mean(xf * xf, axis=-1, keepdims=True) + EPS)
    return (y * g.astype(jnp.float32)).astype(x.dtype)

def _modulate(xn, shift, scale):
    return xn * (1 + scale) + shift

def _l2norm(x):
    xf = x.astype(jnp.float32)
    return xf * lax.rsqrt(jnp.sum(xf * xf, axis=-1, keepdims=True) + EPS)

def _rev(t):
    return jnp.flip(t, axis=2)

def _short_conv(x, w, n_rows):
    B, L, C = x.shape
    K = w.shape[0]
    xr = x.reshape(B * n_rows, L // n_rows, C)
    y = lax.conv_general_dilated(
        xr, w.astype(x.dtype)[:, None, :], window_strides=(1,),
        padding=[((K - 1) // 2, (K - 1) // 2)],
        dimension_numbers=('NWC', 'WIO', 'NWC'), feature_group_count=C)
    return y.reshape(B, L, C)

def _dn_inputs(hn, n_rows, w_in, conv_w, a_log, dt_bias):
    B, L, _ = hn.shape
    z = hn @ w_in
    qkv = jax.nn.silu(_short_conv(z[..., :3 * DN_INNER], conv_w, n_rows))
    gate = z[..., 3 * DN_INNER:4 * DN_INNER]
    ba = z[..., 4 * DN_INNER:].astype(jnp.float32).reshape(B, L, 2, 2, DN_HEADS)
    qkv = qkv.reshape(B, L, 3, DN_HEADS, DN_HEAD_DIM).transpose(2, 0, 3, 1, 4)
    q = _l2norm(qkv[0]) * (DN_HEAD_DIM ** -0.5)
    k = _l2norm(qkv[1])
    v = qkv[2].astype(jnp.float32)
    beta = jax.nn.sigmoid(ba[:, :, 0]).transpose(0, 2, 3, 1)
    g = (-jnp.exp(a_log.astype(jnp.float32)) *
         jax.nn.softplus(ba[:, :, 1] + dt_bias.astype(jnp.float32))).transpose(0, 2, 3, 1)
    return q, k, v, beta, g, gate

def _unit_lower_inverse(a):
    eye = jnp.eye(a.shape[-1], dtype=a.dtype)
    t = eye - a
    p = a
    for _ in range(DN_CHUNK_LOG2 - 1):
        p = p @ p
        t = t @ (eye + p)
    return t

def _gated_delta_chunked(k, v, beta, g, s0, q=None):
    f32 = jnp.float32
    with_out = q is not None
    B, H, L, DK = k.shape
    DV = v.shape[-1]
    C = DN_CHUNK
    n = L // C
    k = k.astype(f32).reshape(B, H, n, C, DK)
    v = v.astype(f32).reshape(B, H, n, C, DV)
    beta = beta.astype(f32).reshape(B, H, n, C)
    G = jnp.cumsum(g.astype(f32).reshape(B, H, n, C), axis=-1)
    incl = jnp.tril(jnp.ones((C, C), bool))
    strict = jnp.tril(jnp.ones((C, C), bool), -1)
    dmat = jnp.exp(jnp.where(incl, G[..., :, None] - G[..., None, :], -jnp.inf))
    kb = k * beta[..., None]
    a = jnp.where(strict, jnp.einsum('bhnid,bhnjd->bhnij', kb, k) * dmat, 0.0)
    t = _unit_lower_inverse(a)
    u = t @ (v * beta[..., None])
    w = t @ (kb * jnp.exp(G)[..., None])
    kd = k * jnp.exp(G[..., -1:] - G)[..., None]
    gl = jnp.exp(G[..., -1])
    xs = (jnp.moveaxis(w, 2, 0), jnp.moveaxis(u, 2, 0), jnp.moveaxis(kd, 2, 0), jnp.moveaxis(gl, 2, 0))
    if with_out:
        q = q.astype(f32).reshape(B, H, n, C, DK)
        qa = jnp.einsum('bhnid,bhnjd->bhnij', q, k) * dmat
        qg = q * jnp.exp(G)[..., None]
        xs = xs + (jnp.moveaxis(qg, 2, 0), jnp.moveaxis(qa, 2, 0))

    def step(s, inp):
        w_c, u_c, kd_c, gl_c = inp[:4]
        v_new = u_c - jnp.einsum('bhck,bhkv->bhcv', w_c, s)
        s_next = s * gl_c[..., None, None] + jnp.einsum('bhck,bhcv->bhkv', kd_c, v_new)
        if not with_out:
            return s_next, None
        qg_c, qa_c = inp[4:]
        o_c = jnp.einsum('bhck,bhkv->bhcv', qg_c, s) + jnp.einsum('bhij,bhjv->bhiv', qa_c, v_new)
        return s_next, o_c

    s_fin, o = lax.scan(step, s0.astype(f32), xs)
    if not with_out:
        return None, s_fin
    return jnp.moveaxis(o, 0, 2).reshape(B, H, L, DV), s_fin

def _gated_out(o, gate, g_norm, w_out):
    B, H, L, DV = o.shape
    o = jnp.swapaxes(o, 1, 2)
    on = o * lax.rsqrt(jnp.mean(o * o, axis=-1, keepdims=True) + EPS) * g_norm.astype(jnp.float32)
    y = on * jax.nn.silu(gate.astype(jnp.float32)).reshape(B, L, H, DV)
    return y.reshape(B, L, H * DV).astype(gate.dtype) @ w_out

def _deltanet(hn, hcn, n_rows, w_in, conv_w, a_log, dt_bias, o_norm_g, w_out, ctx_out):
    q, k, v, beta, g, gate = _dn_inputs(hn, n_rows, w_in, conv_w, a_log, dt_bias)
    qc, kc, vc, betac, gc, gatec = _dn_inputs(hcn, 1, w_in, conv_w, a_log, dt_bias)
    B = hn.shape[0]
    s0 = jnp.zeros((B, DN_HEADS, DN_HEAD_DIM, DN_HEAD_DIM), jnp.float32)
    oc_f, sc_f = _gated_delta_chunked(kc, vc, betac[:, 0], gc[:, 0], s0, qc if ctx_out else None)
    oc_b, sc_b = _gated_delta_chunked(_rev(kc), _rev(vc), _rev(betac[:, 1]), _rev(gc[:, 1]), s0,
                                      _rev(qc) if ctx_out else None)
    o_f, _ = _gated_delta_chunked(k, v, beta[:, 0], g[:, 0], sc_f, q)
    o_b, _ = _gated_delta_chunked(_rev(k), _rev(v), _rev(beta[:, 1]), _rev(g[:, 1]), sc_b, _rev(q))
    y = _gated_out(o_f + _rev(o_b), gate, o_norm_g, w_out)
    yc = _gated_out(oc_f + _rev(oc_b), gatec, o_norm_g, w_out) if ctx_out else None
    return y, yc

def _hyena_filters(L, w1, b1, w2, b2, w3, b3, w4, freq):
    f32 = jnp.float32
    D = w4.shape[-1] // 4
    pos = jnp.arange(L, dtype=f32)
    t = pos / max(L - 1, 1)
    ang = (2 * math.pi * pos / L)[:, None] * jnp.linspace(1e-4, HY_BANDS - 1, HY_BANDS, dtype=f32)[None]
    z = jnp.concatenate([t[:, None], jnp.cos(ang), -jnp.sin(ang)], axis=-1)
    fr = freq.astype(f32)
    hid = jnp.sin(fr * (z @ w1.astype(f32) + b1.astype(f32)))
    hid = jnp.sin(fr * (hid @ w2.astype(f32) + b2.astype(f32)))
    hid = jnp.sin(fr * (hid @ w3.astype(f32) + b3.astype(f32)))
    h = hid @ w4.astype(f32)
    deltas = jnp.abs(jnp.linspace(math.log(HY_TARGET) / HY_FAST, math.log(HY_TARGET) / HY_SLOW, D, dtype=f32))
    decay = jnp.exp(-t[:, None] * deltas[None])
    return (h.reshape(L, 2, 2, D) * decay[:, None, None, :]).transpose(1, 2, 0, 3)

def _long_conv(u, hf, hb, d):
    B, L, D = u.shape
    filt2 = jnp.concatenate([hf, jnp.zeros((1, D), jnp.float32), jnp.flip(hb[1:], axis=0)], axis=0)
    uf = jnp.fft.rfft(u.astype(jnp.float32), n=2 * L, axis=1)
    y = jnp.fft.irfft(uf * jnp.fft.rfft(filt2, axis=0)[None], n=2 * L, axis=1)[:, :L]
    return (y + u.astype(jnp.float32) * d.astype(jnp.float32)).astype(u.dtype)

def _hyena(hn, n_rows, w_in, conv_w, conv_b, f_w1, f_b1, f_w2, f_b2, f_w3, f_b3, f_w4, freq, skip, w_out):
    B, L, _ = hn.shape
    z = _short_conv(hn @ w_in, conv_w, n_rows) + conv_b.astype(hn.dtype)
    v, x1, x2 = jnp.split(z, 3, axis=-1)
    filt = _hyena_filters(L, f_w1, f_b1, f_w2, f_b2, f_w3, f_b3, f_w4, freq)
    z1 = x1 * _long_conv(v, filt[0, 0], filt[0, 1], skip[0])
    z2 = x2 * _long_conv(z1, filt[1, 0], filt[1, 1], skip[1])
    return z2 @ w_out

def _peer(x, w_q, sub_keys, u_tab, v_tab):
    B, L, D = x.shape
    T = B * L
    xt = x.reshape(T, D)
    q = (xt @ w_q).astype(jnp.float32).reshape(T, PEER_HEADS, 2, PEER_DK // 2)
    s = jnp.einsum('thpd,hpkd->thpk', q, sub_keys.astype(jnp.float32))
    s1, i1 = lax.top_k(s[:, :, 0], PEER_TOPK)
    s2, i2 = lax.top_k(s[:, :, 1], PEER_TOPK)
    n_cand = PEER_TOPK * PEER_TOPK
    cand_s = (s1[..., :, None] + s2[..., None, :]).reshape(T, PEER_HEADS, n_cand)
    cand_i = (i1[..., :, None] * PEER_NKEYS + i2[..., None, :]).reshape(T, PEER_HEADS, n_cand)
    top_s, pos = lax.top_k(cand_s, PEER_TOPK)
    idx = jnp.take_along_axis(cand_i, pos, axis=-1)
    gate = jax.nn.softmax(top_s, axis=-1)
    nb = T // PEER_BLOCK

    def expert_block(args):
        xb, ib, gb = args
        hid = jnp.einsum('td,thkd->thk', xb, u_tab[ib]).astype(jnp.float32)
        coef = (jax.nn.gelu(hid, approximate=False) * gb).astype(xb.dtype)
        return jnp.einsum('thk,thkd->td', coef, v_tab[ib])

    y = lax.map(expert_block, (xt.reshape(nb, PEER_BLOCK, D),
                               idx.reshape(nb, PEER_BLOCK, PEER_HEADS, PEER_TOPK),
                               gate.reshape(nb, PEER_BLOCK, PEER_HEADS, PEER_TOPK)))
    return y.reshape(B, L, D)

def second_inputs(seed: int = 0) -> dict:
    key = jax.random.key(seed)
    ks = iter(jax.random.split(key, 32))
    f32 = jnp.float32
    D = D_MODEL

    def nrm(shape, scale):
        return jax.random.normal(next(ks), shape, f32) * scale

    x = nrm((BATCH, SEQ, D), 1.0)
    c = nrm((BATCH, D), 1.0)
    ctx = nrm((BATCH, CTX_LEN, D), 1.0)
    c_ctx = nrm((D,), 1.0)
    ada_w = nrm((DEPTH_2, D, 6 * D), 0.5 * D ** -0.5)
    ada_b = nrm((DEPTH_2, 6 * D), 0.02)
    norm_g = 1.0 + nrm((DEPTH_2, 2, D), 0.02)
    dn_w_in = nrm((N_DELTA_LAYERS, D, DN_PROJ), D ** -0.5)
    dn_conv_w = nrm((N_DELTA_LAYERS, DN_CONV, 3 * DN_INNER), DN_CONV ** -0.5)
    dn_a_log = jnp.log(jax.random.uniform(next(ks), (N_DELTA_LAYERS, 2, DN_HEADS), f32, 1.0, 16.0))
    dt = jnp.exp(jax.random.uniform(next(ks), (N_DELTA_LAYERS, 2, DN_HEADS), f32,
                                    math.log(1e-3), math.log(1e-1)))
    dn_dt_bias = dt + jnp.log(-jnp.expm1(-dt))
    dn_norm_g = 1.0 + nrm((N_DELTA_LAYERS, DN_HEAD_DIM), 0.02)
    dn_w_out = nrm((N_DELTA_LAYERS, DN_INNER, D), DN_INNER ** -0.5)
    hy_w_in = nrm((N_HYENA_LAYERS, D, 3 * HY_WIDTH), D ** -0.5)
    hy_conv_w = nrm((N_HYENA_LAYERS, HY_SHORT, 3 * HY_WIDTH), HY_SHORT ** -0.5)
    hy_conv_b = nrm((N_HYENA_LAYERS, 3 * HY_WIDTH), 0.02)
    hy_f_w1 = nrm((N_HYENA_LAYERS, HY_EMB, HY_FF), HY_EMB ** -0.5)
    hy_f_b1 = nrm((N_HYENA_LAYERS, HY_FF), 0.02)
    hy_f_w2 = nrm((N_HYENA_LAYERS, HY_FF, HY_FF), HY_FF ** -0.5)
    hy_f_b2 = nrm((N_HYENA_LAYERS, HY_FF), 0.02)
    hy_f_w3 = nrm((N_HYENA_LAYERS, HY_FF, HY_FF), HY_FF ** -0.5)
    hy_f_b3 = nrm((N_HYENA_LAYERS, HY_FF), 0.02)
    hy_f_w4 = nrm((N_HYENA_LAYERS, HY_FF, 4 * HY_WIDTH), 0.02 * HY_FF ** -0.5)
    hy_freq = 1.0 + nrm((N_HYENA_LAYERS, HY_FF), 0.02)
    hy_skip = nrm((N_HYENA_LAYERS, 2, HY_WIDTH), 1.0)
    hy_w_out = nrm((N_HYENA_LAYERS, HY_WIDTH, D), HY_WIDTH ** -0.5)
    peer_w_q = nrm((DEPTH_2, D, PEER_HEADS * PEER_DK), D ** -0.5)
    peer_keys = nrm((DEPTH_2, PEER_HEADS, 2, PEER_NKEYS, PEER_DK // 2), (PEER_DK // 2) ** -0.5)
    peer_u = nrm((DEPTH_2, PEER_EXPERTS, D), D ** -0.5)
    peer_v = nrm((DEPTH_2, PEER_EXPERTS, D), PEER_HEADS ** -0.5)
    final_g = 1.0 + nrm((D,), 0.02)
    return {"x": x, "c": c, "ctx": ctx, "c_ctx": c_ctx,
            "ada_w": ada_w, "ada_b": ada_b, "norm_g": norm_g,
            "dn_w_in": dn_w_in, "dn_conv_w": dn_conv_w, "dn_a_log": dn_a_log, "dn_dt_bias": dn_dt_bias,
            "dn_norm_g": dn_norm_g, "dn_w_out": dn_w_out,
            "hy_w_in": hy_w_in, "hy_conv_w": hy_conv_w, "hy_conv_b": hy_conv_b,
            "hy_f_w1": hy_f_w1, "hy_f_b1": hy_f_b1, "hy_f_w2": hy_f_w2, "hy_f_b2": hy_f_b2,
            "hy_f_w3": hy_f_w3, "hy_f_b3": hy_f_b3, "hy_f_w4": hy_f_w4, "hy_freq": hy_freq,
            "hy_skip": hy_skip, "hy_w_out": hy_w_out,
            "peer_w_q": peer_w_q, "peer_keys": peer_keys, "peer_u": peer_u, "peer_v": peer_v,
            "final_g": final_g}

def second_block(x, c, ctx, c_ctx, ada_w, ada_b, norm_g,
              dn_w_in, dn_conv_w, dn_a_log, dn_dt_bias, dn_norm_g, dn_w_out,
              hy_w_in, hy_conv_w, hy_conv_b, hy_f_w1, hy_f_b1, hy_f_w2, hy_f_b2,
              hy_f_w3, hy_f_b3, hy_f_w4, hy_freq, hy_skip, hy_w_out,
              peer_w_q, peer_keys, peer_u, peer_v, final_g):
    f32 = jnp.float32
    B, L, D = x.shape
    rows = L // GRID_W
    silu_c = jax.nn.silu(c.astype(f32))
    silu_cc = jax.nn.silu(c_ctx.astype(f32))
    h, hc = x, ctx
    for i in range(DEPTH_2):
        kind = i % N_MIXERS
        j = i // N_MIXERS
        ctx_out = any(l % N_MIXERS == MIXER_DELTA for l in range(i + 1, DEPTH_2))
        ctx_in = kind == MIXER_DELTA or ctx_out
        w_ada = ada_w[i].astype(f32)
        b_ada = ada_b[i].astype(f32)
        mod = (silu_c @ w_ada + b_ada).astype(h.dtype).reshape(B, 6, 1, D)
        sh1, sc1, gt1, sh2, sc2, gt2 = [mod[:, m] for m in range(6)]
        hn = _modulate(_rmsnorm(h, norm_g[i, 0]), sh1, sc1)
        hcn = None
        if ctx_in:
            modc = (silu_cc @ w_ada + b_ada).astype(hc.dtype).reshape(6, D)
            hcn = _modulate(_rmsnorm(hc, norm_g[i, 0]), modc[0], modc[1])
        if kind == MIXER_DELTA:
            y, yc = _deltanet(hn, hcn, rows, dn_w_in[j], dn_conv_w[j], dn_a_log[j], dn_dt_bias[j],
                              dn_norm_g[j], dn_w_out[j], ctx_out)
        else:
            hy_args = (hy_w_in[j], hy_conv_w[j], hy_conv_b[j], hy_f_w1[j], hy_f_b1[j], hy_f_w2[j],
                       hy_f_b2[j], hy_f_w3[j], hy_f_b3[j], hy_f_w4[j], hy_freq[j], hy_skip[j], hy_w_out[j])
            y = _hyena(hn, rows, *hy_args)
            yc = _hyena(hcn, 1, *hy_args) if ctx_out else None
        h = h + gt1 * y
        peer_args = (peer_w_q[i], peer_keys[i], peer_u[i], peer_v[i])
        h = h + gt2 * _peer(_modulate(_rmsnorm(h, norm_g[i, 1]), sh2, sc2), *peer_args)
        if ctx_out:
            hc = hc + modc[2] * yc
            hc = hc + modc[5] * _peer(_modulate(_rmsnorm(hc, norm_g[i, 1]), modc[3], modc[4]), *peer_args)
    return _rmsnorm(h, final_g)


def setup_inputs(seed=0):
    out = dict(first_inputs(seed))
    for name, value in second_inputs(seed + 1).items():
        if name != "x":
            out[name + "_2"] = value
    return out


def reference(
    x, c, positions, ada_w, ada_b, attn_norm, ffn_norm, ffn_w_gate, ffn_w_up, ffn_w_down,
    sp_w_in, sp_w_out, moba_q_norm, moba_k_norm, nsa_q_norm, nsa_k_norm, nsa_cmp_pos,
    nsa_cmp_w1, nsa_cmp_w2, diff_w_in, diff_w_out, diff_q_norm, diff_k_norm, diff_lambda,
    diff_out_norm, c_2, ctx_2, c_ctx_2, ada_w_2, ada_b_2, norm_g_2, dn_w_in_2, dn_conv_w_2,
    dn_a_log_2, dn_dt_bias_2, dn_norm_g_2, dn_w_out_2, hy_w_in_2, hy_conv_w_2, hy_conv_b_2,
    hy_f_w1_2, hy_f_b1_2, hy_f_w2_2, hy_f_b2_2, hy_f_w3_2, hy_f_b3_2, hy_f_w4_2, hy_freq_2,
    hy_skip_2, hy_w_out_2, peer_w_q_2, peer_keys_2, peer_u_2, peer_v_2, final_g_2,
):
    x = first_block(
        x, c, positions, ada_w, ada_b, attn_norm, ffn_norm, ffn_w_gate, ffn_w_up, ffn_w_down,
        sp_w_in, sp_w_out, moba_q_norm, moba_k_norm, nsa_q_norm, nsa_k_norm, nsa_cmp_pos,
        nsa_cmp_w1, nsa_cmp_w2, diff_w_in, diff_w_out, diff_q_norm, diff_k_norm, diff_lambda,
        diff_out_norm,
    )
    return second_block(
        x, c_2, ctx_2, c_ctx_2, ada_w_2, ada_b_2, norm_g_2, dn_w_in_2, dn_conv_w_2, dn_a_log_2,
        dn_dt_bias_2, dn_norm_g_2, dn_w_out_2, hy_w_in_2, hy_conv_w_2, hy_conv_b_2, hy_f_w1_2,
        hy_f_b1_2, hy_f_w2_2, hy_f_b2_2, hy_f_w3_2, hy_f_b3_2, hy_f_w4_2, hy_freq_2, hy_skip_2,
        hy_w_out_2, peer_w_q_2, peer_keys_2, peer_u_2, peer_v_2, final_g_2,
    )


_drawn_inputs = setup_inputs


def setup_inputs(seed=0):
    import zlib

    import numpy as np

    out = dict(_drawn_inputs(seed))
    spreads = {}
    factors = {'attn_norm': 3.66,
     'moba_q_norm': 8.0,
     'moba_k_norm': 8.0,
     'nsa_q_norm': 8.0,
     'nsa_k_norm': 8.0,
     'nsa_cmp_pos': 6.029,
     'diff_q_norm': 7.973,
     'diff_k_norm': 8.0,
     'diff_out_norm': 4.986,
     'ctx_2': 2.796,
     'c_ctx_2': 4.506,
     'ada_b_2': 3.192,
     'norm_g_2': 5.607,
     'dn_norm_g_2': 8.0,
     'final_g_2': 2.799}
    for name, (base, spread) in spreads.items():
        noise = np.random.default_rng([zlib.crc32(name.encode()), seed]).standard_normal(out[name].shape)
        drawn = base * np.exp(spread * noise) if base else spread * noise
        out[name] = jnp.asarray(drawn.astype(out[name].dtype))
    for name, factor in factors.items():
        out[name] = (out[name] * factor).astype(out[name].dtype)
    return out
```

```python
import math
from contextlib import ExitStack

import concourse.bass as bass
import numpy as np
from concourse import mybir

ALU = mybir.AluOpType
ACT = mybir.ActivationFunctionType
AX = mybir.AxisListType
F32 = mybir.dt.float32
I32 = mybir.dt.int32
U32 = mybir.dt.uint32

P = 128
D = 1024
KT = D // P
S = 256
TT = S // P
EPS = 1e-6
NEG = -1e30
CW = 512

HEAD = 64
ROT = HEAD // 4
HALF = ROT // 2
ROPE_THETA = 500000.0
HEADS = 8
FFN = 2816
FFN_CHUNKS = FFN // P

CMP_LEN, CMP_STRIDE, CMP_HIDDEN = 32, 16, 256
NCMP = (S - CMP_LEN) // CMP_STRIDE + 1
SP_IN = 2840
Z_MQ, Z_MK, Z_MV, Z_NQ, Z_KV, Z_GATE = 0, 512, 1024, 1536, 2048, 2816
KV_BRANCH, KV_VALUE = 256, 128

DIFF_LAM_INIT = 0.8 - 0.6 * float(np.exp(-0.3 * 1))

DN_HEADS = 8
DN_CONV = 5
ROW = 64
NKEYS = 128
TOPK = 16
PHEADS = 8

SC = 384


class Stage:

    def __init__(self, nc, name):
        self.nc, self.name, self.stack, self.sems = nc, name, ExitStack(), []

    def __enter__(self):
        self.stack.callback(self.clear)
        return self

    def clear(self):
        for sem in self.sems:
            self.nc.gpsimd.sem_clear(sem)
            self.nc.release_semaphore(sem)

    def __exit__(self, *error):
        return self.stack.__exit__(*error)

    def sb(self, name, shape, dtype=F32):
        return self.stack.enter_context(self.nc.sbuf_tensor(f"{self.name}_{name}", shape, dtype))

    def ps(self, name, shape):
        return self.stack.enter_context(self.nc.psum_tensor(f"{self.name}_{name}", shape, F32))

    def sem(self, name):
        self.sems.append(self.nc.alloc_semaphore(f"{self.name}_{name}"))
        return self.sems[-1]

    def block(self):
        return self.stack.enter_context(self.nc.Block())


class InOrder:

    def __init__(self, engine, done):
        self.engine, self.done, self.n = engine, done, 0

    def __call__(self, instruction):
        instruction.then_inc(self.done, 1)
        self.n += 1
        self.engine.wait_ge(self.done, self.n)


def constants(nc, pst, ins):
    k = {
        "ident": pst.sb("ident", [P, P]),
        "ones": pst.sb("ones", [P, P]),
        "iota": pst.sb("iota", [P, P]),
        "causal": pst.sb("causal", [P, SC]),
        "incl": pst.sb("incl", [P, 2, P]),
        "strict": pst.sb("strict", [P, 2, P]),
        "decay_mask": pst.sb("decay_mask", [P, 2, P]),
        "cmp_mask": pst.sb("cmp_mask", [P, TT, NCMP]),
        "cmp_valid": pst.sb("cmp_valid", [P, TT, NCMP]),
        "cos": pst.sb("cos", [P, TT, HALF]),
        "sin": pst.sb("sin", [P, TT, HALF]),
        "x": pst.sb("x", [P, TT, D]),
    }
    with Stage(nc, "const") as st:
        pos_i = st.sb("pos_i", [P, TT], I32)
        pos = st.sb("pos", [P, TT])
        freq = st.sb("freq", [P, HALF])
        ang = st.sb("ang", [P, TT, HALF])
        turns = st.sb("turns", [P, TT, HALF])
        rest = st.sb("rest", [P, 2, TT, HALF])
        loaded, filled, freq_set, reduced, tables, dve_done = (
            st.sem(n) for n in ("loaded", "filled", "freq_set", "reduced", "tables", "dve_done"))
        block = st.block()

        @block.sync
        def _(sp):
            sp.dma_start(k["x"][:], ins["x"].rearrange("(t p) d -> p t d", p=P)).then_inc(loaded, 16)
            sp.dma_start(pos_i[:], ins["positions"]).then_inc(loaded, 16)
            sp.wait_ge(loaded, 32)

        @block.gpsimd
        def _(pool):
            step = InOrder(pool, filled)
            for c in range(HALF):
                inv = np.float32(1.0) / np.float32(ROPE_THETA) ** np.float32(2 * c / ROT)
                pool.memset(freq[:, c:c + 1], float(inv)).then_inc(freq_set, 1)
            step(pool.memset(k["ident"][:], 0.0))
            step(pool.affine_select(out=k["ident"][:], in_=k["ident"][:], compare_op=ALU.not_equal, fill=1.0,
                                    base=0, pattern=[[-1, P]], channel_multiplier=1))
            step(pool.memset(k["ones"][:], 1.0))
            step(pool.iota(k["iota"][:], pattern=[[1, P]], base=0, channel_multiplier=0,
                           allow_small_or_imprecise_dtypes=True))
            step(pool.memset(k["causal"][:], 0.0))
            for lo, base in ((0, 0), (P, P)):
                width = P if lo == 0 else S
                step(pool.affine_select(out=k["causal"][:, lo:lo + width], in_=k["causal"][:, lo:lo + width],
                                        compare_op=ALU.is_ge, fill=NEG, base=base, pattern=[[-1, width]],
                                        channel_multiplier=1))
            for d, sign in ((0, 1), (1, -1)):
                for name, base, fill, start in (("incl", 0, 0.0, 1.0), ("strict", -1, 0.0, 1.0),
                                                ("decay_mask", 0, NEG, 0.0)):
                    v = k[name][:, d, :]
                    step(pool.memset(v, start))
                    step(pool.affine_select(out=v, in_=v, compare_op=ALU.is_ge, fill=fill, base=base,
                                            pattern=[[sign, P]], channel_multiplier=-sign))
            for name, fill, start in (("cmp_mask", NEG, 0.0), ("cmp_valid", 0.0, 1.0)):
                step(pool.memset(k[name][:], start))
                for t in range(TT):
                    step(pool.affine_select(out=k[name][:, t, :], in_=k[name][:, t, :], compare_op=ALU.is_ge,
                                            fill=fill, base=t * P - (CMP_LEN - 1), pattern=[[-CMP_STRIDE, NCMP]],
                                            channel_multiplier=1))

        @block.vector
        def _(dve):
            step = InOrder(dve, dve_done)
            two_pi = 2 * math.pi
            hi = float(np.float32(6.28125))
            mid = float(np.float32(two_pi - hi))
            lo = two_pi - hi - mid
            magic = 1.5 * 2.0 ** 23
            dve.wait_ge(loaded, 32)
            dve.wait_ge(freq_set, HALF)
            step(dve.tensor_copy(pos[:], pos_i[:]))
            step(dve.tensor_tensor(ang[:], pos[:].unsqueeze(2).broadcast_to([P, TT, HALF]),
                                   freq[:].unsqueeze(1).broadcast_to([P, TT, HALF]), ALU.mult))
            for n, shift in ((0, 0.0), (1, 0.25)):
                step(dve.tensor_scalar(turns[:], ang[:], 1 / two_pi, shift, ALU.mult, ALU.add))
                step(dve.tensor_scalar(turns[:], turns[:], magic, None, ALU.add))
                step(dve.tensor_scalar(turns[:], turns[:], -magic, None, ALU.add))
                r = rest[:, n]
                step(dve.scalar_tensor_tensor(r, turns[:], -hi, ang[:], ALU.mult, ALU.add))
                step(dve.scalar_tensor_tensor(r, turns[:], -mid, r, ALU.mult, ALU.add))
                step(dve.scalar_tensor_tensor(r, turns[:], -lo, r, ALU.mult, ALU.add))
                step(dve.tensor_scalar(r, r, shift * two_pi, None, ALU.add))
                step(dve.tensor_scalar(r, r, 3.1415925, -3.1415925, ALU.min, ALU.max))
            dve.tensor_copy(turns[:], rest[:, 0]).then_inc(reduced, 1)

        @block.scalar
        def _(act):
            act.wait_ge(reduced, 1)
            act.activation(k["sin"][:], rest[:, 0], ACT.Sin).then_inc(tables, 1)
            act.activation(k["cos"][:], rest[:, 1], ACT.Sin).then_inc(tables, 1)
            act.wait_ge(tables, 2)
    return k


def modulation(nc, k, name, weights, bias, vectors):
    with Stage(nc, name) as st:
        nv = len(vectors)
        ring = 3
        w = st.sb("w", [P, ring, KT, CW])
        c = st.sb("c", [P, nv, KT])
        cb = st.sb("cb", [P, nv, KT, P])
        psum = st.ps("psum", [P, 4, CW])
        slot_loaded = [st.sem(f"slot_loaded{i}") for i in range(ring)]
        c_loaded, bias_loaded, c_silu, c_ready, product, added = (
            st.sem(n) for n in ("c_loaded", "bias_loaded", "c_silu", "c_ready", "product", "added"))
        n_chunks = weights.shape[0]
        jobs = [(j, v) for j in range(n_chunks) for v in range(nv) if j < vectors[v][2]]
        last_job = {j: n for n, (j, _) in enumerate(jobs)}
        block = st.block()

        @block.sync
        def _(sp):
            for v, (source, row, chunks) in enumerate(vectors):
                sp.dma_start(c[:, v, :], source).then_inc(c_loaded, 16)
            for j in range(n_chunks):
                if j >= ring:
                    sp.wait_ge(product, last_job[j - ring] + 1)
                sp.dma_start(w[:, j % ring], weights[j]).then_inc(slot_loaded[j % ring], 16)

        @block.scalar
        def _(act):
            for v, (source, row, chunks) in enumerate(vectors):
                act.dma_start(row[:, 0:chunks * CW], bias[0:chunks * CW].partition_broadcast(P)).then_inc(bias_loaded, 16)
            act.wait_ge(c_loaded, 16 * nv)
            act.activation(c[:], c[:], ACT.Silu).then_inc(c_silu, 1)

        @block.vector
        def _(dve):
            dve.wait_ge(c_silu, 1)
            dve.tensor_copy(cb[:], c[:].unsqueeze(3).broadcast_to([P, nv, KT, P])).then_inc(c_ready, 1)
            dve.wait_ge(bias_loaded, 16 * nv)
            for n, (j, v) in enumerate(jobs):
                row = vectors[v][1][:, j * CW:(j + 1) * CW]
                dve.wait_ge(product, n + 1)
                dve.tensor_tensor(row, psum[:, n % 4, :], row, ALU.add).then_inc(added, 1)

        @block.tensor
        def _(pe):
            pe.wait_ge(c_ready, 1)
            for n, (j, v) in enumerate(jobs):
                pe.wait_ge(slot_loaded[j % ring], 16 * (j // ring + 1))
                if n >= 4:
                    pe.wait_ge(added, n - 3)
                for t in range(KT):
                    last = pe.matmul(psum[:, n % 4, :], cb[:, v, t, :], w[:, j % ring, t, :],
                                     start=(t == 0), stop=(t == KT - 1))
                last.then_inc(product, 1)


def normed(nc, k, name, x, gain, shift, scale, out_t):
    with Stage(nc, name) as st:
        g = st.sb("gain", [P, D])
        h = st.sb("h", [P, TT, D])
        junk = st.sb("junk", [P, D])
        ss = st.sb("ss", [P, TT])
        psum = st.ps("psum", [P, 4, CW])
        loaded, squared, mean_ready, root_ready, h_ready, turned, copied, dve_done, psum_copied = (
            st.sem(n) for n in ("loaded", "squared", "mean_ready", "root_ready", "h_ready", "turned",
                                "copied", "dve_done", "psum_copied"))
        block = st.block()
        groups = [(t, half) for t in range(TT) for half in range(2)]

        @block.sync
        def _(sp):
            sp.dma_start(g[:], gain.partition_broadcast(P)).then_inc(loaded, 16)

        @block.scalar
        def _(act):
            for t in range(TT):
                act.activation(junk[:], x[:, t, :], ACT.Square, accum_out=ss[:, t:t + 1]).then_inc(squared, 1)
                act.wait_ge(squared, t + 1)
            act.wait_ge(mean_ready, 1)
            act.activation(ss[:], ss[:], ACT.Sqrt).then_inc(root_ready, 1)
            for n in (1, 3):
                t, half = groups[n]
                act.wait_ge(turned, n + 1)
                act.copy(out_t[:, 4 * half:4 * half + 4, t * P:(t + 1) * P],
                         psum[:, n, :].rearrange("p (c q) -> p c q", c=4)).then_inc(psum_copied, 1)

        @block.vector
        def _(dve):
            step = InOrder(dve, dve_done)
            dve.wait_ge(loaded, 16)
            if scale is not None:
                step(dve.scalar_tensor_tensor(g[:], scale, 1.0, g[:], ALU.add, ALU.mult))
            dve.wait_ge(squared, TT)
            dve.tensor_scalar(ss[:], ss[:], 1.0 / D, EPS, ALU.mult, ALU.add).then_inc(mean_ready, 1)
            dve.wait_ge(root_ready, 1)
            step(dve.reciprocal(ss[:], ss[:]))
            for t in range(TT):
                step(dve.scalar_tensor_tensor(h[:, t, :], x[:, t, :], ss[:, t:t + 1], g[:], ALU.mult, ALU.mult))
                dve.tensor_tensor(h[:, t, :], h[:, t, :], shift, ALU.add).then_inc(h_ready, 1)
            for n in (0, 2):
                t, half = groups[n]
                dve.wait_ge(turned, n + 1)
                dve.tensor_copy(out_t[:, 4 * half:4 * half + 4, t * P:(t + 1) * P],
                                psum[:, n, :].rearrange("p (c q) -> p c q", c=4)).then_inc(copied, 1)

        @block.tensor
        def _(pe):
            for n, (t, half) in enumerate(groups):
                pe.wait_ge(h_ready, t + 1)
                for c in range(4):
                    last = pe.transpose(psum[:, n, c * P:(c + 1) * P],
                                        h[:, t, (4 * half + c) * P:(4 * half + c + 1) * P], k["ident"][:])
                last.then_inc(turned, 1)


def turn(nc, k, name, z, blocks, out_t):
    with Stage(nc, name) as st:
        banks = 6
        psum = st.ps("psum", [P, banks, CW])
        turned, copied = st.sem("turned"), st.sem("copied")
        moved = st.sem("moved")
        pairs = [blocks[i:i + 2] for i in range(0, len(blocks), 2)]
        block = st.block()

        def bank_free(pe, n):
            if n >= banks:
                prior = n - banks
                pe.wait_ge(copied if prior % 2 == 0 else moved, prior // 2 + 1)

        def source(n):
            w = len(pairs[n])
            return (out_t[:, 2 * n:2 * n + w, :],
                    psum[:, n % banks, 0:w * S].rearrange("p (b q) -> p b q", b=w))

        @block.tensor
        def _(pe):
            for n, pair in enumerate(pairs):
                bank_free(pe, n)
                for b, col in enumerate(pair):
                    for t in range(TT):
                        last = pe.transpose(psum[:, n % banks, b * S + t * P:b * S + (t + 1) * P],
                                            z[:, t, col:col + P], k["ident"][:])
                last.then_inc(turned, 1)

        @block.vector
        def _(dve):
            for n in range(0, len(pairs), 2):
                dve.wait_ge(turned, n + 1)
                dve.tensor_copy(*source(n)).then_inc(copied, 1)

        @block.scalar
        def _(act):
            for n in range(1, len(pairs), 2):
                act.wait_ge(turned, n + 1)
                act.copy(*source(n)).then_inc(moved, 1)


def project(nc, k, name, h_t, chunks, residual=None, out=None):
    with Stage(nc, name) as st:
        ring = 3
        w = st.sb("w", [P, ring, KT * CW])
        tmp = st.sb("tmp", [P, 2, CW])
        psum = st.ps("psum", [P, 4, CW])
        slot_loaded = [st.sem(f"slot_loaded{i}") for i in range(ring)]
        product, taken, scaled, moved = (st.sem(n) for n in ("product", "taken", "scaled", "moved"))
        jobs = [(j, t) for j in range(len(chunks)) for t in range(TT)]
        block = st.block()

        @block.sync
        def _(sp):
            for j, (source, col, width) in enumerate(chunks):
                if j >= ring:
                    sp.wait_ge(product, TT * (j - ring + 1))
                sp.dma_start(w[:, j % ring, 0:KT * width], source).then_inc(slot_loaded[j % ring], 16)

        @block.tensor
        def _(pe):
            for n, (j, t) in enumerate(jobs):
                width = chunks[j][2]
                pe.wait_ge(slot_loaded[j % ring], 16 * (j // ring + 1))
                if n >= 4 and residual is not None:
                    pe.wait_ge(scaled, n - 3)
                if n >= 4 and residual is None:
                    pe.wait_ge(taken if n % 2 == 0 else moved, n // 2 - 1)
                for c in range(KT):
                    last = pe.matmul(psum[:, n % 4, 0:width], h_t[:, c, t * P:(t + 1) * P],
                                     w[:, j % ring, c * width:(c + 1) * width],
                                     start=(c == 0), stop=(c == KT - 1))
                last.then_inc(product, 1)

        @block.vector
        def _(dve):
            for n, (j, t) in enumerate(jobs):
                col, width = chunks[j][1:]
                if residual is None:
                    if n % 2 == 0:
                        dve.wait_ge(product, n + 1)
                        dve.tensor_copy(out[:, t, col:col + width], psum[:, n % 4, 0:width]).then_inc(taken, 1)
                    continue
                x, gate = residual
                dve.wait_ge(product, n + 1)
                if n >= 2:
                    dve.wait_ge(taken, n - 1)
                dve.tensor_tensor(tmp[:, n % 2, 0:width], psum[:, n % 4, 0:width], gate[:, col:col + width],
                                  ALU.mult).then_inc(scaled, 1)
                dve.wait_ge(scaled, n + 1)
                dve.tensor_tensor(x[:, t, col:col + width], x[:, t, col:col + width], tmp[:, n % 2, 0:width],
                                  ALU.add).then_inc(taken, 1)

        @block.scalar
        def _(act):
            for n, (j, t) in enumerate(jobs):
                col, width = chunks[j][1:]
                if residual is None and n % 2 == 1:
                    act.wait_ge(product, n + 1)
                    act.copy(out[:, t, col:col + width], psum[:, n % 4, 0:width]).then_inc(moved, 1)


def head_norm_rope(nc, k, name, z, segments):
    with Stage(nc, name) as st:
        total = sum(n for _, n, _ in segments)
        most = max(n for _, n, _ in segments)
        sq = st.sb("sq", [P, TT, most, HEAD])
        ss = st.sb("ss", [P, TT, total])
        gains = st.sb("gains", [P, len(segments), HEAD])
        rot = [st.sb(f"rot{i}", [P, TT, most, HALF]) for i in range(4)]
        loaded, mean_ready, root_ready, dve_done = (
            st.sem(n) for n in ("loaded", "mean_ready", "root_ready", "dve_done"))
        block = st.block()

        @block.sync
        def _(sp):
            for s, (_, _, gain) in enumerate(segments):
                sp.dma_start(gains[:, s, :], gain.partition_broadcast(P)).then_inc(loaded, 16)

        @block.scalar
        def _(act):
            act.wait_ge(mean_ready, 1)
            act.activation(ss[:], ss[:], ACT.Sqrt).then_inc(root_ready, 1)

        @block.vector
        def _(dve):
            step = InOrder(dve, dve_done)

            def heads(s):
                col, n, _ = segments[s]
                return z[:, :, col:col + n * HEAD].rearrange("p t (n d) -> p t n d", d=HEAD)

            at = 0
            for s, (_, n, _) in enumerate(segments):
                step(dve.tensor_tensor(sq[:, :, 0:n, :], heads(s), heads(s), ALU.mult))
                step(dve.tensor_reduce(ss[:, :, at:at + n], sq[:, :, 0:n, :], AX.X, ALU.add))
                at += n
            dve.tensor_scalar(ss[:], ss[:], 1.0 / HEAD, EPS, ALU.mult, ALU.add).then_inc(mean_ready, 1)
            dve.wait_ge(loaded, 16 * len(segments))
            dve.wait_ge(root_ready, 1)
            step(dve.reciprocal(ss[:], ss[:]))
            at = 0
            for s, (_, n, _) in enumerate(segments):
                v = heads(s)
                rs = ss[:, :, at:at + n].unsqueeze(3).broadcast_to([P, TT, n, HEAD])
                at += n
                step(dve.tensor_tensor(v, v, rs, ALU.mult))
                for t in range(TT):
                    g = gains[:, s, :].unsqueeze(1).broadcast_to([P, n, HEAD])
                    step(dve.tensor_tensor(v[:, t], v[:, t], g, ALU.mult))
                t1, t2 = v[:, :, :, 0:HALF], v[:, :, :, HALF:ROT]
                cos = k["cos"][:].unsqueeze(2).broadcast_to([P, TT, n, HALF])
                sin = k["sin"][:].unsqueeze(2).broadcast_to([P, TT, n, HALF])
                for r, (a, b) in enumerate(((t1, cos), (t2, sin), (t2, cos), (t1, sin))):
                    step(dve.tensor_tensor(rot[r][:, :, 0:n, :], a, b, ALU.mult))
                step(dve.tensor_tensor(t1, rot[0][:, :, 0:n, :], rot[1][:, :, 0:n, :], ALU.subtract))
                step(dve.tensor_tensor(t2, rot[2][:, :, 0:n, :], rot[3][:, :, 0:n, :], ALU.add))


def compress(nc, k, ins, z, q_t, pc_t, vc, gates):
    G = 2
    N = G * NCMP
    with Stage(nc, "cmp") as st:
        w1 = st.sb("w1", [HEAD, CMP_LEN, CMP_HIDDEN])
        w2 = st.sb("w2", [P, 2, 2, HEAD])
        pos_t = st.sb("pos_t", [HEAD, 2, CMP_LEN])
        tok_t = st.sb("tok_t", [HEAD, 2, G, S])
        blk = st.sb("blk", [HEAD, 2, CMP_LEN, N])
        hid = st.sb("hid", [P, 2, 2, N])
        kc_t = st.sb("kc_t", [P, G, NCMP])
        sc = st.sb("sc", [P, TT, HEADS, NCMP])
        mx = st.sb("mx", [P, TT, HEADS])
        sm = st.sb("sm", [P, TT, HEADS])
        pt = [st.ps(f"pt{i}", [P, CW]) for i in range(2)]
        ph = st.ps("ph", [P, 2, CW])
        pk = st.ps("pk", [P, CW])
        pv = st.ps("pv", [P, CW])
        psc = st.ps("psc", [P, CW])
        loaded, w1_loaded, turned, tok_ready, blk_ready, hid_sum, hid_ready, small, kv_ready, scored, \
            shifted, exped, gate_e, p_ready, p_turned, p_half, dve_done = (st.sem(n) for n in (
                "loaded", "w1_loaded", "turned", "tok_ready", "blk_ready", "hid_sum", "hid_ready", "small",
                "kv_ready", "scored", "shifted", "exped", "gate_e", "p_ready", "p_turned", "p_half", "dve_done"))
        block = st.block()

        @block.sync
        def _(sp):
            sp.dma_start(pos_t[:], ins["cmp_pos"]).then_inc(loaded, 16)
            sp.dma_start(w2[:], ins["cmp_w2"]).then_inc(loaded, 16)
            for kv in range(2):
                if kv:
                    sp.wait_ge(hid_sum, 1)
                sp.dma_start(w1[:], ins["cmp_w1"][kv]).then_inc(w1_loaded, 16)

        @block.tensor
        def _(pe):
            for kv in range(2):
                for g in range(G):
                    for t in range(TT):
                        col = Z_KV + kv * KV_VALUE + g * HEAD
                        last = pe.transpose(pt[kv][0:HEAD, g * S + t * P:g * S + (t + 1) * P],
                                            z[:, t, col:col + HEAD], k["ident"][:])
                last.then_inc(turned, 1)
            pe.wait_ge(blk_ready, 2 * G)
            for kv in range(2):
                pe.wait_ge(w1_loaded, 16 * (kv + 1))
                for e in range(2):
                    for l in range(CMP_LEN):
                        last = pe.matmul(ph[:, kv, e * N:(e + 1) * N], w1[:, l, e * P:(e + 1) * P],
                                         blk[:, kv, l, :], start=(l == 0), stop=(l == CMP_LEN - 1))
                last.then_inc(hid_sum, 1)
            pe.wait_ge(hid_ready, 2)
            pe.wait_ge(loaded, 32)
            for g in range(G):
                for e in range(2):
                    pe.matmul(pk[g * HEAD:(g + 1) * HEAD, 0:NCMP], w2[:, 0, e, :],
                              hid[:, 0, e, g * NCMP:(g + 1) * NCMP], start=(e == 0), stop=(e == 1))
            for g in range(G):
                for e in range(2):
                    last = pe.matmul(pv[0:NCMP, g * HEAD:(g + 1) * HEAD], hid[:, 1, e, g * NCMP:(g + 1) * NCMP],
                                     w2[:, 1, e, :], start=(e == 0), stop=(e == 1))
            last.then_inc(small, 1)
            pe.wait_ge(kv_ready, G + 1)
            for t in range(TT):
                for b in range(HEADS // G):
                    at = (t * HEADS + b * G) * NCMP
                    last = pe.matmul(psc[:, at:at + N], q_t[:, b, t * P:(t + 1) * P],
                                     kc_t[:].rearrange("p g n -> p (g n)"), start=True, stop=True)
            last.then_inc(scored, 1)
            pe.wait_ge(p_ready, 1)
            for quarter in range(4):
                if quarter >= 2:
                    pe.wait_ge(p_half, quarter - 1)
                for h in (2 * quarter, 2 * quarter + 1):
                    for t in range(TT):
                        last = pe.transpose(pt[quarter % 2][0:NCMP, (h % 2) * S + t * P:(h % 2) * S + (t + 1) * P],
                                            sc[:, t, h, :], k["ident"][:])
                last.then_inc(p_turned, 1)

        @block.scalar
        def _(act):
            act.activation(gates[:], z[:, :, Z_GATE:Z_GATE + 3 * HEADS], ACT.Exp, scale=-1.0).then_inc(gate_e, 1)
            act.wait_ge(hid_sum, 2)
            for kv in range(2):
                act.activation(hid[:, kv].rearrange("p e n -> p (e n)"), ph[:, kv, 0:2 * N],
                               ACT.Silu).then_inc(hid_ready, 1)
            act.wait_ge(shifted, 1)
            act.activation(sc[:], sc[:], ACT.Exp).then_inc(exped, 1)

        @block.vector
        def _(dve):
            step = InOrder(dve, dve_done)
            dve.wait_ge(gate_e, 1)
            step(dve.tensor_scalar(gates[:], gates[:], 1.0, None, ALU.add))
            step(dve.memset(kc_t[:], 0.0))
            step(dve.reciprocal(gates[:], gates[:]))
            dve.wait_ge(loaded, 32)
            for kv in range(2):
                dve.wait_ge(turned, kv + 1)
                step(dve.tensor_copy(tok_t[:, kv].rearrange("d g s -> d (g s)"), pt[kv][0:HEAD, :]))
                for g in range(G):
                    for n in range(NCMP):
                        last = dve.tensor_tensor(blk[:, kv, :, g * NCMP + n],
                                                 tok_t[:, kv, g, n * CMP_STRIDE:n * CMP_STRIDE + CMP_LEN],
                                                 pos_t[:, kv, :], ALU.add)
                    last.then_inc(blk_ready, 1)
            dve.wait_ge(small, 1)
            for g in range(G):
                rows = slice(g * HEAD, (g + 1) * HEAD)
                dve.tensor_copy(kc_t[rows, g, :], pk[rows, 0:NCMP]).then_inc(kv_ready, 1)
            dve.tensor_copy(vc[:].rearrange("n g d -> n (g d)"), pv[0:NCMP, 0:G * HEAD]).then_inc(kv_ready, 1)
            dve.wait_ge(scored, 1)
            for t in range(TT):
                step(dve.scalar_tensor_tensor(
                    sc[:, t], psc[:, t * HEADS * NCMP:(t + 1) * HEADS * NCMP].rearrange("p (h n) -> p h n", h=HEADS),
                    HEAD ** -0.5, k["cmp_mask"][:, t, :].unsqueeze(1).broadcast_to([P, HEADS, NCMP]),
                    ALU.mult, ALU.add))
            wide = [P, TT, HEADS, NCMP]
            step(dve.tensor_reduce(mx[:], sc[:], AX.X, ALU.max))
            dve.tensor_tensor(sc[:], sc[:], mx[:].unsqueeze(3).broadcast_to(wide), ALU.subtract).then_inc(shifted, 1)
            dve.wait_ge(exped, 1)
            step(dve.tensor_reduce(sm[:], sc[:], AX.X, ALU.add))
            step(dve.reciprocal(sm[:], sm[:]))
            step(dve.tensor_tensor(sm[:], sm[:], gates[:, :, 0:HEADS], ALU.mult))
            step(dve.tensor_tensor(sc[:], sc[:], k["cmp_valid"][:].unsqueeze(2).broadcast_to(wide), ALU.mult))
            dve.tensor_tensor(sc[:], sc[:], sm[:].unsqueeze(3).broadcast_to(wide), ALU.mult).then_inc(p_ready, 1)
            for quarter in range(4):
                dve.wait_ge(p_turned, quarter + 1)
                dve.tensor_copy(pc_t[:, 2 * quarter:2 * quarter + 2, :].rearrange("n h s -> n (h s)"),
                                pt[quarter % 2][0:NCMP, :]).then_inc(p_half, 1)


def sparse_attention(nc, k, z, zt, pc_t, vc, gates, o_t):
    maps = []
    for h in range(HEADS):
        maps.append((h // 2, 4 + h // 2, h % 2, Z_MV + h * HEAD, None, h // 2, "only"))
    for h in range(HEADS):
        for br, part in ((1, "first"), (2, "last")):
            maps.append((8 + h // 2, 12 + br, h % 2, Z_KV + br * KV_BRANCH + KV_VALUE + (h % 2) * HEAD,
                         (br, h), 4 + h // 2, part))
    n_maps = len(maps)
    with Stage(nc, "attn") as st:
        sc = st.sb("sc", [P, 2, SC])
        pt = st.sb("pt", [P, 2, SC])
        nm = st.sb("nm", [P, 2, TT])
        sm = st.sb("sm", [P, 2, TT])
        ps = st.ps("ps", [P, 2, CW])
        pp = st.ps("pp", [P, 2, CW])
        po = st.ps("po", [P, 2, CW])
        scored, masked, neg_max, exped, probs, turned, pt_ready, attended, stored, dve_done = (
            st.sem(n) for n in ("scored", "masked", "neg_max", "exped", "probs", "turned", "pt_ready",
                                "attended", "stored", "dve_done"))
        block = st.block()
        parts = ((0, P), (P, SC))

        @block.tensor
        def _(pe):
            def scores(i):
                q, key, half, *_ = maps[i]
                rows = slice(half * HEAD, (half + 1) * HEAD)
                if i >= 2:
                    pe.wait_ge(masked, i - 1)
                for t, (lo, hi) in enumerate(parts):
                    last = pe.matmul(ps[:, i % 2, lo:hi], zt[rows, q, t * P:(t + 1) * P],
                                     zt[rows, key, 0:hi - lo], start=True, stop=True)
                last.then_inc(scored, 1)

            def turn_probs(i):
                pe.wait_ge(probs, i + 1)
                if i >= 2:
                    pe.wait_ge(pt_ready, i - 1)
                for c in range(3):
                    last = pe.transpose(pp[:, i % 2, c * P:(c + 1) * P], sc[:, i % 2, c * P:(c + 1) * P],
                                        k["ident"][:])
                last.then_inc(turned, 1)

            def values(i):
                _, _, half, vcol, gate, dest, part = maps[i]
                rows = slice(half * HEAD, (half + 1) * HEAD)
                pe.wait_ge(pt_ready, i + 1)
                if dest >= 2 and half == 0 and part != "last":
                    pe.wait_ge(stored, dest - 1)
                o = po[rows, dest % 2, :]
                first = part != "last"
                pe.matmul(o[:, 0:S], z[:, 0, vcol:vcol + HEAD], pt[:, i % 2, 0:S], start=first, stop=False)
                last = pe.matmul(o[:, P:S], z[:, 1, vcol:vcol + HEAD], pt[:, i % 2, S:SC], start=False,
                                 stop=(part == "only"))
                if part == "last":
                    last = pe.matmul(o[:, 0:S], vc[:, half, :], pc_t[:, gate[1], :], start=False, stop=True)
                last.then_inc(attended, 1)

            for i in range(n_maps + 2):
                if i < n_maps:
                    scores(i)
                if 1 <= i <= n_maps:
                    turn_probs(i - 1)
                if i >= 2:
                    values(i - 2)

        ends = [i for i, m in enumerate(maps) if m[2] == 1 and m[6] != "first"]

        @block.vector
        def _(dve):
            step = InOrder(dve, dve_done)

            def mask(i):
                dve.wait_ge(scored, i + 1)
                if i >= 2:
                    dve.wait_ge(turned, i - 1)
                s = sc[:, i % 2, :]
                dve.scalar_tensor_tensor(s, ps[:, i % 2, 0:SC], HEAD ** -0.5, k["causal"][:], ALU.mult,
                                         ALU.add).then_inc(masked, 1)
                dve.wait_ge(masked, i + 1)
                for t, (lo, hi) in enumerate(parts):
                    dve.tensor_reduce(nm[:, i % 2, t:t + 1], s[:, lo:hi], AX.X, ALU.max,
                                      negate=True).then_inc(neg_max, 1)

            def scale(i):
                dve.wait_ge(exped, 2 * i + 2)
                r = sm[:, i % 2, :]
                step(dve.reciprocal(r, r))
                if maps[i][4]:
                    br, h = maps[i][4]
                    step(dve.tensor_tensor(r, r, gates[:, :, br * HEADS + h], ALU.mult))
                for t, (lo, hi) in enumerate(parts):
                    last = dve.tensor_scalar(sc[:, i % 2, lo:hi], sc[:, i % 2, lo:hi], sm[:, i % 2, t:t + 1], None,
                                             ALU.mult)
                last.then_inc(probs, 1)

            for i in range(n_maps + 1):
                if i < n_maps:
                    mask(i)
                if i >= 1:
                    scale(i - 1)

        @block.scalar
        def _(act):
            def exp(i):
                for t, (lo, hi) in enumerate(parts):
                    act.wait_ge(neg_max, 2 * i + t + 1)
                    act.activation(sc[:, i % 2, lo:hi], sc[:, i % 2, lo:hi], ACT.Exp, bias=nm[:, i % 2, t:t + 1],
                                   accum_out=sm[:, i % 2, t:t + 1]).then_inc(exped, 1)

            def move_probs(i):
                act.wait_ge(turned, i + 1)
                if i >= 2:
                    act.wait_ge(attended, i - 1)
                act.copy(pt[:, i % 2, :], pp[:, i % 2, 0:SC]).then_inc(pt_ready, 1)

            def store(i):
                if i in ends:
                    n = ends.index(i)
                    act.wait_ge(attended, i + 1)
                    act.copy(o_t[:, n, :], po[:, n % 2, 0:S]).then_inc(stored, 1)

            for i in range(n_maps + 2):
                if i < n_maps:
                    exp(i)
                if 1 <= i <= n_maps:
                    move_probs(i - 1)
                if i >= 2:
                    store(i - 2)


def streamed_mlp(nc, k, name, h_t, packed, kind, residual, table=None):
    x, gate = residual
    n_tiles, _, width = packed.shape
    first = width - D
    halves = first // D
    assert n_tiles % 2 == 0
    with Stage(nc, name) as st:
        w = st.sb("w", [P, 4, width])
        act_out = st.sb("act_out", [P, 2, S])
        coef = st.sb("coef", [P, 2, S])
        tmp = st.sb("tmp", [P, 2, CW])
        pa = st.ps("pa", [P, 2, CW])
        py = st.ps("py", [P, TT * 2, CW])
        slot_loaded = [st.sem(f"slot_loaded{i}") for i in range(4)]
        rows_ready, acted, coef_ready, down_done, scaled, summed = (
            st.sem(n) for n in ("rows_ready", "acted", "coef_ready", "down_done", "scaled", "summed"))
        block = st.block()
        ring = 4
        rounds = n_tiles // ring
        left = n_tiles % ring

        @block.sync
        def _(sp):
            for s in range(ring):
                sp.dma_start(w[:, s, :], packed[s]).then_inc(slot_loaded[s], 16)
            with sp.Fori(1, rounds) as r:
                for s in range(ring):
                    sp.wait_ge(down_done, r * ring + (s - ring + 1))
                    sp.dma_start(w[:, s, :], packed[bass.ds(r * ring + s, 1)].rearrange("a p n -> p (a n)")
                                 ).then_inc(slot_loaded[s], 16)
            for s in range(left):
                i = rounds * ring + s
                sp.wait_ge(down_done, i - ring + 1)
                sp.dma_start(w[:, s, :], packed[i]).then_inc(slot_loaded[s], 16)

        @block.tensor
        def _(pe):
            def up(i, s, rnd, early=False):
                b = s % 2
                pe.wait_ge(slot_loaded[s], 16 * rnd + 16)
                if not early:
                    pe.wait_ge(coef_ready, i - 1)
                for half in range(halves):
                    for c in range(KT):
                        last = pe.matmul(pa[:, b, half * S:(half + 1) * S],
                                         w[:, s, half * D + c * P:half * D + (c + 1) * P], h_t[:, c, :],
                                         start=(c == 0), stop=(c == KT - 1))
                last.then_inc(rows_ready, 1)

            def down(i, s, start=False, stop=False):
                b = s % 2
                pe.wait_ge(coef_ready, i + 1)
                for t in range(TT):
                    for n in range(2):
                        last = pe.matmul(py[:, 2 * t + n, :], coef[:, b, t * P:(t + 1) * P],
                                         w[:, s, first + n * CW:first + (n + 1) * CW], start=start, stop=stop)
                last.then_inc(down_done, 1)

            up(0, 0, 0, early=True)
            up(1, 1, 0, early=True)
            down(0, 0, start=True)
            for s in range(2, ring):
                up(s, s, 0)
                down(s - 1, s - 1)
            with pe.Fori(1, rounds) as r:
                for s in range(ring):
                    up(r * ring + s, s, r)
                    down(r * ring + (s - 1), (s - 1) % ring)
            for s in range(left):
                up(rounds * ring + s, s, rounds)
                down(rounds * ring + s - 1, (s - 1) % ring)
            down(n_tiles - 1, (n_tiles - 1) % ring, stop=True)

        @block.scalar
        def _(act):
            func = ACT.Silu if kind == "swiglu" else ACT.Gelu

            def gate_tile(i, b, early=False):
                act.wait_ge(rows_ready, i + 1)
                if not early:
                    act.wait_ge(coef_ready, i - 1)
                act.activation(act_out[:, b, :], pa[:, b, 0:S], func).then_inc(acted, 1)

            for b in range(2):
                gate_tile(b, b, early=True)
            with act.Fori(1, n_tiles // 2) as r:
                for b in range(2):
                    gate_tile(2 * r + b, b)

        @block.vector
        def _(dve):
            def weigh(i, b, early=False):
                dve.wait_ge(acted, i + 1)
                if not early:
                    dve.wait_ge(down_done, i - 1)
                if kind == "swiglu":
                    other = pa[:, b, S:2 * S]
                elif early:
                    other = table[:, i, :]
                else:
                    other = table[:, bass.ds(i, 1), :].rearrange("p a s -> p (a s)")
                dve.tensor_tensor(coef[:, b, :], act_out[:, b, :], other, ALU.mult).then_inc(coef_ready, 1)

            for b in range(2):
                weigh(b, b, early=True)
            with dve.Fori(1, n_tiles // 2) as r:
                for b in range(2):
                    weigh(2 * r + b, b)
            dve.wait_ge(down_done, n_tiles)
            for n in range(2 * TT):
                t, c = n // 2, (n % 2) * CW
                if n >= 2:
                    dve.wait_ge(summed, n - 1)
                dve.tensor_tensor(tmp[:, n % 2, :], py[:, n, :], gate[:, c:c + CW], ALU.mult).then_inc(scaled, 1)
                dve.wait_ge(scaled, n + 1)
                dve.tensor_tensor(x[:, t, c:c + CW], x[:, t, c:c + CW], tmp[:, n % 2, :], ALU.add).then_inc(summed, 1)


def chunked(source, width, first=0):
    return [(source[j], first + j * CW, CW) for j in range(width // CW)]


def sparse_layer(nc, k, ins):
    x = k["x"]
    with Stage(nc, "l0") as st:
        mod = st.sb("mod", [P, 6 * D])
        modulation(nc, k, "ada0", ins["ada_w0"], ins["ada_b0"], [(ins["c"], mod, 12)])
        m = [mod[:, i * D:(i + 1) * D] for i in range(6)]
        with Stage(nc, "l0a") as sa:
            o_t = sa.sb("o_t", [P, KT, S])
            with Stage(nc, "l0b") as sb:
                z = sb.sb("z", [P, TT, SP_IN])
                h_t = sb.sb("h_t", [P, KT, S])
                normed(nc, k, "norm0", x, ins["attn_norm0"], m[0], m[1], h_t)
                tail = SP_IN - 5 * CW
                project(nc, k, "proj0", h_t, chunked(ins["sp_w_in"], 5 * CW) + [(ins["sp_w_in_tail"], 5 * CW, tail)],
                        out=z)
                segs = [(Z_MQ, 8, ins["moba_q_norm"]), (Z_MK, 8, ins["moba_k_norm"]), (Z_NQ, 8, ins["nsa_q_norm"])]
                segs += [(Z_KV + br * KV_BRANCH, 2, ins["nsa_k_norm"][br]) for br in range(3)]
                head_norm_rope(nc, k, "rope0", z, segs)
                zt = sb.sb("zt", [P, 15, S])
                blocks = [Z_MQ + i * P for i in range(4)] + [Z_MK + i * P for i in range(4)]
                blocks += [Z_NQ + i * P for i in range(4)] + [Z_KV + br * KV_BRANCH for br in range(3)]
                turn(nc, k, "turn0", z, blocks, zt)
                pc_t = sb.sb("pc_t", [NCMP, HEADS, S])
                vc = sb.sb("vc", [NCMP, 2, HEAD])
                gates = sb.sb("gates", [P, TT, 3 * HEADS])
                compress(nc, k, ins, z, zt[:, 8:12, :], pc_t, vc, gates)
                sparse_attention(nc, k, z, zt, pc_t, vc, gates, o_t)
            project(nc, k, "out0", o_t, chunked(ins["sp_w_out"], D), residual=(x, m[2]))
        h_t = st.sb("h_t", [P, KT, S])
        normed(nc, k, "fnorm0", x, ins["ffn_norm0"], m[3], m[4], h_t)
        streamed_mlp(nc, k, "ffn0", h_t, ins["ffn0"], "swiglu", (x, m[5]))


def head_norm(nc, k, name, o, gain, factor, gate=None):
    with Stage(nc, name) as st:
        sq = st.sb("sq", [P, TT, D])
        ss = st.sb("ss", [P, TT, HEADS])
        g = st.sb("g", [P, P])
        loaded, gated, mean_ready, root_ready, dve_done = (
            st.sem(n) for n in ("loaded", "gated", "mean_ready", "root_ready", "dve_done"))
        block = st.block()

        def by_head(v):
            return v.rearrange("p t (h d) -> p t h d", h=HEADS)

        @block.sync
        def _(sp):
            sp.dma_start(g[:], gain.partition_broadcast(P)).then_inc(loaded, 16)

        @block.scalar
        def _(act):
            if gate is not None:
                act.activation(gate, gate, ACT.Silu).then_inc(gated, 1)
            act.wait_ge(mean_ready, 1)
            act.activation(ss[:], ss[:], ACT.Sqrt).then_inc(root_ready, 1)

        @block.vector
        def _(dve):
            step = InOrder(dve, dve_done)
            step(dve.tensor_tensor(sq[:], o, o, ALU.mult))
            step(dve.tensor_reduce(ss[:], by_head(sq[:]), AX.X, ALU.add))
            dve.tensor_scalar(ss[:], ss[:], 1.0 / P, EPS, ALU.mult, ALU.add).then_inc(mean_ready, 1)
            dve.wait_ge(loaded, 16)
            step(dve.tensor_scalar(g[:], g[:], factor, None, ALU.mult))
            for t in range(TT):
                v = o[:, t, :].rearrange("p (h d) -> p h d", h=HEADS)
                step(dve.tensor_tensor(v, v, g[:].unsqueeze(1).broadcast_to([P, HEADS, P]), ALU.mult))
            if gate is not None:
                dve.wait_ge(gated, 1)
                step(dve.tensor_tensor(o, o, gate, ALU.mult))
            dve.wait_ge(root_ready, 1)
            step(dve.reciprocal(ss[:], ss[:]))
            step(dve.tensor_tensor(by_head(o), by_head(o), ss[:].unsqueeze(3).broadcast_to([P, TT, HEADS, P]),
                                   ALU.mult))


def diff_attention(nc, k, ins, z, zt, o):
    parts = ((0, P), (P, SC))
    with Stage(nc, "diff") as st:
        lp = st.sb("lp", [P, 4, HEAD])
        lam = st.sb("lam", [P, 2])
        neg_lam = st.sb("neg_lam", [P, 1])
        sc = st.sb("sc", [P, 2, 2, SC])
        pt = st.sb("pt", [P, 2, SC])
        nm = st.sb("nm", [P, 2, TT, 2])
        sm = st.sb("sm", [P, 2, TT, 2])
        ps = st.ps("ps", [P, 2, 2, CW])
        pp = st.ps("pp", [P, 2, CW])
        po = st.ps("po", [P, 2, CW])
        loaded, lam_sum, lam_exp, scored, masked, neg_max, exped, probs, turned, pt_ready, attended, stored, \
            dve_done = (st.sem(n) for n in (
                "loaded", "lam_sum", "lam_exp", "scored", "masked", "neg_max", "exped", "probs", "turned",
                "pt_ready", "attended", "stored", "dve_done"))
        block = st.block()

        @block.sync
        def _(sp):
            sp.dma_start(lp[:].rearrange("p a d -> p (a d)"), ins["diff_lambda"].partition_broadcast(P)
                         ).then_inc(loaded, 16)

        @block.tensor
        def _(pe):
            def scores(h):
                if h >= 2:
                    pe.wait_ge(masked, h - 1)
                for c in range(2):
                    rows = slice(c * HEAD, (c + 1) * HEAD)
                    for t, (lo, hi) in enumerate(parts):
                        last = pe.matmul(ps[:, h % 2, c, lo:hi], zt[rows, h, t * P:(t + 1) * P],
                                         zt[rows, 8 + h, 0:hi - lo], start=True, stop=True)
                last.then_inc(scored, 1)

            def turn_probs(h):
                pe.wait_ge(probs, h + 1)
                if h >= 2:
                    pe.wait_ge(pt_ready, h - 1)
                for c in range(3):
                    last = pe.transpose(pp[:, h % 2, c * P:(c + 1) * P], sc[:, h % 2, 0, c * P:(c + 1) * P],
                                        k["ident"][:])
                last.then_inc(turned, 1)

            def values(h):
                pe.wait_ge(pt_ready, h + 1)
                if h >= 2:
                    pe.wait_ge(stored, h - 1)
                v = [z[:, t, 2 * D + h * P:2 * D + (h + 1) * P] for t in range(TT)]
                pe.matmul(po[:, h % 2, 0:P], pt[:, h % 2, 0:P], v[0], start=True, stop=True)
                pe.matmul(po[:, h % 2, P:2 * P], pt[:, h % 2, P:2 * P], v[0], start=True, stop=False)
                pe.matmul(po[:, h % 2, P:2 * P], pt[:, h % 2, 2 * P:SC], v[1], start=False,
                          stop=True).then_inc(attended, 1)

            for h in range(HEADS + 2):
                if h < HEADS:
                    scores(h)
                if 1 <= h <= HEADS:
                    turn_probs(h - 1)
                if h >= 2:
                    values(h - 2)

        @block.vector
        def _(dve):
            step = InOrder(dve, dve_done)
            dve.wait_ge(loaded, 16)
            step(dve.tensor_tensor(lp[:, 0, :], lp[:, 0, :], lp[:, 1, :], ALU.mult))
            step(dve.tensor_tensor(lp[:, 2, :], lp[:, 2, :], lp[:, 3, :], ALU.mult))
            dve.tensor_reduce(lam[:, 0:1], lp[:, 0, :], AX.X, ALU.add).then_inc(lam_sum, 1)
            dve.tensor_reduce(lam[:, 1:2], lp[:, 2, :], AX.X, ALU.add).then_inc(lam_sum, 1)
            dve.wait_ge(lam_exp, 1)
            step(dve.tensor_tensor(neg_lam[:], lam[:, 1:2], lam[:, 0:1], ALU.subtract))
            step(dve.tensor_scalar(neg_lam[:], neg_lam[:], -DIFF_LAM_INIT, None, ALU.add))

            def mask(h):
                dve.wait_ge(scored, h + 1)
                if h >= 2:
                    dve.wait_ge(turned, h - 1)
                s = sc[:, h % 2]
                dve.scalar_tensor_tensor(s, ps[:, h % 2, :, 0:SC], HEAD ** -0.5,
                                         k["causal"][:].unsqueeze(1).broadcast_to([P, 2, SC]), ALU.mult,
                                         ALU.add).then_inc(masked, 1)
                dve.wait_ge(masked, h + 1)
                for t, (lo, hi) in enumerate(parts):
                    dve.tensor_reduce(nm[:, h % 2, t, :], s[:, :, lo:hi], AX.X, ALU.max,
                                      negate=True).then_inc(neg_max, 1)

            def combine(h):
                dve.wait_ge(exped, 4 * h + 4)
                r = sm[:, h % 2]
                step(dve.reciprocal(r, r))
                step(dve.tensor_scalar(r[:, :, 1], r[:, :, 1], neg_lam[:], None, ALU.mult))
                for t, (lo, hi) in enumerate(parts):
                    last = dve.tensor_scalar(sc[:, h % 2, 1, lo:hi], sc[:, h % 2, 1, lo:hi], sm[:, h % 2, t, 1:2],
                                             None, ALU.mult)
                step(last)
                for t, (lo, hi) in enumerate(parts):
                    last = dve.scalar_tensor_tensor(sc[:, h % 2, 0, lo:hi], sc[:, h % 2, 0, lo:hi],
                                                    sm[:, h % 2, t, 0:1], sc[:, h % 2, 1, lo:hi], ALU.mult, ALU.add)
                last.then_inc(probs, 1)

            for h in range(HEADS + 1):
                if h < HEADS:
                    mask(h)
                if h >= 1:
                    combine(h - 1)

        @block.scalar
        def _(act):
            act.wait_ge(lam_sum, 2)
            act.activation(lam[:], lam[:], ACT.Exp).then_inc(lam_exp, 1)

            def exp(h):
                for t, (lo, hi) in enumerate(parts):
                    act.wait_ge(neg_max, 2 * h + t + 1)
                    for c in range(2):
                        act.activation(sc[:, h % 2, c, lo:hi], sc[:, h % 2, c, lo:hi], ACT.Exp,
                                       bias=nm[:, h % 2, t, c:c + 1],
                                       accum_out=sm[:, h % 2, t, c:c + 1]).then_inc(exped, 1)

            def move_probs(h):
                act.wait_ge(turned, h + 1)
                if h >= 2:
                    act.wait_ge(attended, h - 1)
                act.copy(pt[:, h % 2, :], pp[:, h % 2, 0:SC]).then_inc(pt_ready, 1)

            def store(h):
                act.wait_ge(attended, h + 1)
                act.copy(o[:, :, h * P:(h + 1) * P],
                         po[:, h % 2, 0:2 * P].rearrange("p (t d) -> p t d", t=TT)).then_inc(stored, 1)

            for h in range(HEADS + 2):
                if h < HEADS:
                    exp(h)
                if 1 <= h <= HEADS:
                    move_probs(h - 1)
                if h >= 2:
                    store(h - 2)


def diff_layer(nc, k, ins):
    x = k["x"]
    with Stage(nc, "l1") as st:
        mod = st.sb("mod", [P, 6 * D])
        modulation(nc, k, "ada1", ins["ada_w1"], ins["ada_b1"], [(ins["c"], mod, 12)])
        m = [mod[:, i * D:(i + 1) * D] for i in range(6)]
        h_t = st.sb("h_t", [P, KT, S])
        with Stage(nc, "l1b") as sb:
            z = sb.sb("z", [P, TT, 3 * D])
            zt = sb.sb("zt", [P, 16, S])
            o = sb.sb("o", [P, TT, D])
            normed(nc, k, "norm1", x, ins["attn_norm1"], m[0], m[1], h_t)
            project(nc, k, "proj1", h_t, chunked(ins["diff_w_in"], 3 * D), out=z)
            head_norm_rope(nc, k, "rope1", z, [(0, 16, ins["diff_q_norm"]), (D, 16, ins["diff_k_norm"])])
            turn(nc, k, "turn1", z, [i * P for i in range(16)], zt)
            diff_attention(nc, k, ins, z, zt, o)
            head_norm(nc, k, "onorm1", o[:], ins["diff_out_norm"], 1.0 - DIFF_LAM_INIT)
            turn(nc, k, "oturn1", o, [i * P for i in range(KT)], h_t)
        project(nc, k, "out1", h_t, chunked(ins["diff_w_out"], D), residual=(x, m[2]))
        normed(nc, k, "fnorm1", x, ins["ffn_norm1"], m[3], m[4], h_t)
        streamed_mlp(nc, k, "ffn1", h_t, ins["ffn1"], "swiglu", (x, m[5]))


XC = 2 * S
DH = 2 * DN_HEADS
TILES = 2 * TT


def delta_qkv(nc, k, ins, h_t, q_t, k_t, v_t):
    with Stage(nc, "dnqkv") as st:
        ring = 3
        w = st.sb("w", [P, ring, KT * CW])
        taps = st.sb("taps", [P, 3 * KT, DN_CONV])
        y = st.sb("y", [P, 2, XC])
        psum = st.ps("psum", [P, 4, CW])
        slot_loaded = [st.sem(f"slot_loaded{i}") for i in range(ring)]
        taps_loaded, product, conved, silued, dve_done = (
            st.sem(n) for n in ("taps_loaded", "product", "conved", "silued", "dve_done"))
        blocks = 3 * KT
        block = st.block()

        @block.sync
        def _(sp):
            sp.dma_start(taps[:], ins["dn_conv"]).then_inc(taps_loaded, 16)
            for j in range(blocks // 4):
                if j >= ring:
                    sp.wait_ge(product, 4 * (j - ring + 1))
                sp.dma_start(w[:, j % ring, :], ins["dn_w_qkv"][j]).then_inc(slot_loaded[j % ring], 16)

        @block.tensor
        def _(pe):
            for b in range(blocks):
                j, col = b // 4, (b % 4) * P
                n = S if b < KT else XC
                pe.wait_ge(slot_loaded[j % ring], 16 * (j // ring + 1))
                if b >= 4:
                    pe.wait_ge(conved, b - 3)
                for c in range(KT):
                    last = pe.matmul(psum[:, b % 4, 0:n], w[:, j % ring, c * CW + col:c * CW + col + P],
                                     h_t[:, c, 0:n], start=(c == 0), stop=(c == KT - 1))
                last.then_inc(product, 1)

        @block.vector
        def _(dve):
            step = InOrder(dve, dve_done)
            dve.wait_ge(taps_loaded, 16)
            mid = DN_CONV // 2
            for b in range(blocks):
                dve.wait_ge(product, b + 1)
                if b >= 2:
                    dve.wait_ge(silued, b - 1)
                n = S if b < KT else XC
                step(dve.tensor_scalar(y[:, b % 2, 0:n], psum[:, b % 4, 0:n], taps[:, b, mid:mid + 1], None, ALU.mult))
                for tap in (0, 1, 3, 4):
                    s = tap - mid
                    for lo, hi, row in ((0, S, ROW), (S, XC, S)):
                        if hi > n:
                            continue
                        to = y[:, b % 2, lo:hi].rearrange("p (r w) -> p r w", w=row)[:, :, max(0, -s):row - max(0, s)]
                        of = psum[:, b % 4, lo:hi].rearrange("p (r w) -> p r w", w=row)[
                            :, :, max(0, s):row - max(0, -s)]
                        last = dve.scalar_tensor_tensor(to, of, taps[:, b, tap:tap + 1], to, ALU.mult, ALU.add)
                    if tap < 4:
                        step(last)
                last.then_inc(conved, 1)

        @block.scalar
        def _(act):
            for b in range(blocks):
                kind, h = b // KT, b % KT
                n = S if b < KT else XC
                act.wait_ge(conved, b + 1)
                act.activation((q_t, k_t, v_t)[kind][:, h, 0:n], y[:, b % 2, 0:n], ACT.Silu).then_inc(silued, 1)


def delta_unit(nc, k, q_t, k_t):
    jobs = [(q_t, h, S, P ** -0.5) for h in range(DN_HEADS)] + [(k_t, h, XC, 1.0) for h in range(DN_HEADS)]
    with Stage(nc, "dnunit") as st:
        sq = st.sb("sq", [P, 2, XC])
        root = st.sb("root", [P, 2, XC])
        psum = st.ps("psum", [P, 2, CW])
        squared, summed, plus_eps, rooted, dve_done = (
            st.sem(n) for n in ("squared", "summed", "plus_eps", "rooted", "dve_done"))
        block = st.block()

        @block.scalar
        def _(act):
            def square(i):
                v, h, n, _ = jobs[i]
                if i >= 2:
                    act.wait_ge(summed, i - 1)
                act.activation(sq[:, i % 2, 0:n], v[:, h, 0:n], ACT.Square).then_inc(squared, 1)

            for i in range(len(jobs) + 1):
                if i < len(jobs):
                    square(i)
                if i >= 1:
                    n = jobs[i - 1][2]
                    r = root[:, (i - 1) % 2, 0:n]
                    act.wait_ge(plus_eps, i)
                    act.activation(r, r, ACT.Sqrt).then_inc(rooted, 1)

        @block.tensor
        def _(pe):
            for i, (_, _, n, _) in enumerate(jobs):
                pe.wait_ge(squared, i + 1)
                if i >= 2:
                    pe.wait_ge(plus_eps, i - 1)
                pe.matmul(psum[:, i % 2, 0:n], k["ones"][:], sq[:, i % 2, 0:n], start=True,
                          stop=True).then_inc(summed, 1)

        @block.vector
        def _(dve):
            step = InOrder(dve, dve_done)
            for i in range(len(jobs) + 1):
                if i < len(jobs):
                    n = jobs[i][2]
                    dve.wait_ge(summed, i + 1)
                    dve.tensor_scalar(root[:, i % 2, 0:n], psum[:, i % 2, 0:n], EPS, None, ALU.add).then_inc(plus_eps, 1)
                if i >= 1:
                    v, h, n, factor = jobs[i - 1]
                    r = root[:, (i - 1) % 2, 0:n]
                    dve.wait_ge(rooted, i)
                    step(dve.reciprocal(r, r))
                    step(dve.scalar_tensor_tensor(v[:, h, 0:n], v[:, h, 0:n], factor, r, ALU.mult, ALU.mult))


def delta_gates(nc, k, ins, h_t, dg):
    beta, g_sum, exp_g, exp_rest, exp_last, rows = (dg[n] for n in (
        "beta", "g_sum", "exp_g", "exp_rest", "exp_last", "rows"))
    wide = [P, TILES, DH]
    with Stage(nc, "dngate") as st:
        w = st.sb("w", [P, KT, 2 * DH])
        dt = st.sb("dt", [P, DH])
        la = st.sb("la", [P, DH])
        a = st.sb("a", wide)
        e = st.sb("e", wide)
        pba = st.ps("pba", [P, CW])
        pg = st.ps("pg", [P, CW])
        pl = st.ps("pl", [P, CW])
        pr = st.ps("pr", [P, 2, CW])
        loaded, product, neg_abs, exp_abs, one_plus, logged, g_ready, sums, turned, rest_ready, exps, dve_done = (
            st.sem(n) for n in ("loaded", "product", "neg_abs", "exp_abs", "one_plus", "logged", "g_ready",
                                "sums", "turned", "rest_ready", "exps", "dve_done"))
        block = st.block()

        @block.sync
        def _(sp):
            sp.dma_start(w[:].rearrange("p c n -> p (c n)"), ins["dn_w_ba"]).then_inc(loaded, 16)
            sp.dma_start(dt[:], ins["dn_dt_bias"].partition_broadcast(P)).then_inc(loaded, 16)
            sp.dma_start(la[:], ins["dn_a_log"].partition_broadcast(P)).then_inc(loaded, 16)

        @block.tensor
        def _(pe):
            pe.wait_ge(loaded, 48)
            for t in range(TILES):
                for c in range(KT):
                    last = pe.matmul(pba[:, t * 2 * DH:(t + 1) * 2 * DH], h_t[:, c, t * P:(t + 1) * P], w[:, c, :],
                                     start=(c == 0), stop=(c == KT - 1))
            last.then_inc(product, 1)
            pe.wait_ge(g_ready, 1)
            for t in range(TILES):
                for d in range(2):
                    at = t * DH + d * DN_HEADS
                    pe.matmul(pg[:, at:at + DN_HEADS], k["incl"][:, d, :], a[:, t, d * DN_HEADS:(d + 1) * DN_HEADS],
                              start=True, stop=True)
            pe.matmul(pl[:, 0:TILES * DH], k["ones"][:], a[:].rearrange("p t n -> p (t n)"), start=True,
                      stop=True).then_inc(sums, 1)
            pe.wait_ge(rest_ready, 1)
            for t in range(TILES):
                pe.transpose(pr[0:DH, t // 2, (t % 2) * S:(t % 2) * S + P], g_sum[:, t, :], k["ident"][:])
                last = pe.transpose(pr[0:DH, t // 2, (t % 2) * S + P:(t % 2 + 1) * S], beta[:, t, :], k["ident"][:])
            last.then_inc(turned, 1)

        @block.scalar
        def _(act):
            act.wait_ge(loaded, 48)
            act.activation(la[:], la[:], ACT.Exp).then_inc(exp_abs, 1)
            act.wait_ge(neg_abs, 2)
            act.activation(beta[:], beta[:], ACT.Exp, scale=-1.0).then_inc(exp_abs, 1)
            act.activation(e[:], e[:], ACT.Exp).then_inc(exp_abs, 1)
            act.wait_ge(one_plus, 1)
            act.activation(e[:], e[:], ACT.Ln).then_inc(logged, 1)
            act.wait_ge(rest_ready, 1)
            for v in (exp_g, exp_rest, exp_last):
                act.activation(v[:], v[:], ACT.Exp).then_inc(exps, 1)

        @block.vector
        def _(dve):
            step = InOrder(dve, dve_done)
            dve.wait_ge(product, 1)
            ba = pba[:, 0:TILES * 2 * DH].rearrange("p (t n) -> p t n", t=TILES)
            dve.tensor_copy(beta[:], ba[:, :, 0:DH]).then_inc(neg_abs, 1)
            step(dve.tensor_tensor(a[:], ba[:, :, DH:2 * DH], dt[:].unsqueeze(1).broadcast_to(wide), ALU.add))
            step(dve.tensor_scalar(e[:], a[:], -1.0, None, ALU.mult))
            dve.tensor_tensor(e[:], e[:], a[:], ALU.min).then_inc(neg_abs, 1)
            dve.wait_ge(exp_abs, 3)
            dve.tensor_scalar(e[:], e[:], 1.0, None, ALU.add).then_inc(one_plus, 1)
            step(dve.tensor_scalar(beta[:], beta[:], 1.0, None, ALU.add))
            step(dve.reciprocal(beta[:], beta[:]))
            step(dve.tensor_scalar(a[:], a[:], 0.0, None, ALU.max))
            dve.wait_ge(logged, 1)
            step(dve.tensor_tensor(a[:], a[:], e[:], ALU.add))
            dve.scalar_tensor_tensor(a[:], a[:], -1.0, la[:].unsqueeze(1).broadcast_to(wide), ALU.mult,
                                     ALU.mult).then_inc(g_ready, 1)
            dve.wait_ge(sums, 1)
            total = pl[:, 0:TILES * DH].rearrange("p (t n) -> p t n", t=TILES)
            so_far = pg[:, 0:TILES * DH].rearrange("p (t n) -> p t n", t=TILES)
            step(dve.tensor_copy(g_sum[:], so_far))
            step(dve.tensor_copy(exp_g[:], so_far))
            step(dve.tensor_copy(exp_last[:], total))
            dve.tensor_tensor(exp_rest[:], exp_last[:], g_sum[:], ALU.subtract).then_inc(rest_ready, 1)
            dve.wait_ge(turned, 1)
            dve.wait_ge(exps, 3)
            step(dve.tensor_copy(rows[:].rearrange("n (a b) s -> n a (b s)", a=2), pr[0:DH]))


def delta_matrices(nc, k, dg, q_t, k_t, at_m, qd):
    quads = [(t, g, d) for t in range(TILES) for g in range(2) for d in range(2)]
    n_jobs = len(quads)
    with Stage(nc, "dnmat") as st:
        dt = st.sb("dt", [P, 2, 4, P])
        pgram = st.ps("pgram", [P, CW])
        pkq = st.ps("pkq", [P, CW])
        prow = st.ps("prow", [P, 2, 4, S])
        sel = st.sb("sel", [DH, DH, P])
        sel_ready, grams, row_sums, diffs, decays, used, dve_done = (
            st.sem(n) for n in ("sel_ready", "grams", "row_sums", "diffs", "decays", "used", "dve_done"))
        block = st.block()

        @block.gpsimd
        def _(pool):
            pool.memset(sel[:], 1.0).then_inc(sel_ready, 1)
            pool.wait_ge(sel_ready, 1)
            pool.affine_select(out=sel[:], in_=sel[:], compare_op=ALU.is_equal, fill=0.0, base=0,
                               pattern=[[-1, DH], [0, P]], channel_multiplier=1).then_inc(sel_ready, 1)

        @block.tensor
        def _(pe):
            pe.wait_ge(sel_ready, 2)
            for i, (t, g, d) in enumerate(quads):
                if i >= 2:
                    pe.wait_ge(used, i - 1)
                for h in range(4):
                    last = pe.matmul(prow[:, i % 2, h, :], sel[:, d * DN_HEADS + g * 4 + h, :], dg["rows"][:, t, :],
                                     start=True, stop=True)
                last.then_inc(row_sums, 1)
                if d == 0:
                    if i >= 2:
                        pe.wait_ge(used, i)
                    for h in range(4):
                        key = k_t[:, g * 4 + h, t * P:(t + 1) * P]
                        last = pe.matmul(pgram[:, h * P:(h + 1) * P], key, key, start=True, stop=True)
                    if t < TT:
                        for h in range(4):
                            last = pe.matmul(pkq[:, h * P:(h + 1) * P], k_t[:, g * 4 + h, t * P:(t + 1) * P],
                                             q_t[:, g * 4 + h, t * P:(t + 1) * P], start=True, stop=True)
                    last.then_inc(grams, 1)

        @block.vector
        def _(dve):
            step = InOrder(dve, dve_done)
            four = [P, 4, P]

            def diff(i):
                t, g, d = quads[i]
                gs = dg["g_sum"][:, t, d * DN_HEADS + g * 4:d * DN_HEADS + g * 4 + 4]
                dve.wait_ge(row_sums, i + 1)
                step(dve.tensor_tensor(dt[:, i % 2], prow[:, i % 2, :, 0:P], gs.unsqueeze(2).broadcast_to(four),
                                       ALU.subtract))
                dve.tensor_tensor(dt[:, i % 2], dt[:, i % 2],
                                  k["decay_mask"][:, d, :].unsqueeze(1).broadcast_to(four), ALU.add).then_inc(diffs, 1)

            def matrices(i):
                t, g, d = quads[i]
                m = at_m[:, t, d, g * 4:g * 4 + 4, :]
                dve.wait_ge(decays, i + 1)
                dve.wait_ge(grams, i // 2 + 1)
                gram = pgram[:].rearrange("p (h s) -> p h s", h=4)
                step(dve.tensor_tensor(m, gram, dt[:, i % 2], ALU.mult))
                step(dve.tensor_tensor(m, m, k["strict"][:, d, :].unsqueeze(1).broadcast_to(four), ALU.mult))
                if t < TT:
                    step(dve.tensor_tensor(qd[:, t, d, g * 4:g * 4 + 4, :], pkq[:].rearrange("p (h s) -> p h s", h=4),
                                           dt[:, i % 2], ALU.mult))
                dve.tensor_tensor(m, m, prow[:, i % 2, :, P:S], ALU.mult).then_inc(used, 1)
                dve.wait_ge(used, i + 1)

            for i in range(n_jobs + 1):
                if i < n_jobs:
                    diff(i)
                if i >= 1:
                    matrices(i - 1)

        @block.scalar
        def _(act):
            for i in range(n_jobs):
                act.wait_ge(diffs, i + 1)
                act.activation(dt[:, i % 2], dt[:, i % 2], ACT.Exp).then_inc(decays, 1)


def delta_inverse(nc, k, at_m):
    groups = [(t, d, g) for t in range(TILES) for d in range(2) for g in range(2)]
    levels = 6
    steps = [(pair, level, which) for pair in range(len(groups) // 2) for level in range(levels + 1)
             for which in range(2)]
    with Stage(nc, "dninv") as st:
        pw = st.sb("pw", [P, 2, 4, P])
        pwt = st.sb("pwt", [P, 2, 4, P])
        pp = st.ps("pp", [P, 2, CW])
        pt = st.ps("pt", [P, 2, CW])
        pi = st.ps("pi", [P, 2, CW])
        powers, power_ready, t_power_ready, product, inverse_ready = (
            st.sem(n) for n in ("powers", "power_ready", "t_power_ready", "product", "inverse_ready"))
        block = st.block()

        def inverse(pair, which):
            t, d, g = groups[2 * pair + which]
            return at_m[:, t, d, g * 4:g * 4 + 4, :]

        @block.tensor
        def _(pe):
            def power(n):
                pair, level, b = steps[n]
                m = inverse(pair, b)
                if n >= 2:
                    pe.wait_ge(power_ready, n - 1)
                    pe.wait_ge(t_power_ready, n - 1)
                for h in range(4):
                    cols = slice(h * P, (h + 1) * P)
                    if level == 0:
                        last = pe.transpose(pp[:, b, cols], m[:, h, :], k["ident"][:])
                    else:
                        pe.matmul(pp[:, b, cols], pwt[:, b, h, :], pw[:, b, h, :], start=True, stop=True)
                        last = pe.matmul(pt[:, b, cols], pw[:, b, h, :], pwt[:, b, h, :], start=True, stop=True)
                last.then_inc(powers, 1)

            def apply(n):
                pair, level, b = steps[n]
                if level == 0:
                    return
                m = inverse(pair, b)
                pe.wait_ge(power_ready, n + 1)
                pe.wait_ge(inverse_ready, n - 1)
                for h in range(4):
                    last = pe.matmul(pi[:, b, h * P:(h + 1) * P], pw[:, b, h, :], m[:, h, :], start=True, stop=True)
                last.then_inc(product, 1)

            for n in range(len(steps) + 1):
                if n < len(steps):
                    power(n)
                if n >= 1:
                    apply(n - 1)

        def products_before(n):
            return sum(1 for _, level, _ in steps[:n] if level)

        @block.scalar
        def _(act):
            for n, (pair, level, b) in enumerate(steps):
                act.wait_ge(powers, n + 1)
                if n >= 2:
                    act.wait_ge(product, products_before(n - 1)) if products_before(n - 1) else None
                act.copy(pw[:, b], pp[:, b, :].rearrange("p (h s) -> p h s", h=4)).then_inc(power_ready, 1)

        @block.vector
        def _(dve):
            def t_power(n):
                pair, level, b = steps[n]
                m = inverse(pair, b)
                dve.wait_ge(powers, n + 1)
                if level == 0:
                    dve.tensor_copy(pwt[:, b], m).then_inc(t_power_ready, 1)
                else:
                    dve.tensor_copy(pwt[:, b], pt[:, b, :].rearrange("p (h s) -> p h s", h=4)
                                    ).then_inc(t_power_ready, 1)

            def factor(n):
                pair, level, b = steps[n]
                m = inverse(pair, b)
                if level == 0:
                    dve.wait_ge(t_power_ready, n + 1)
                    dve.scalar_tensor_tensor(m, m, -1.0, k["ident"][:].unsqueeze(1).broadcast_to([P, 4, P]), ALU.mult,
                                             ALU.add).then_inc(inverse_ready, 1)
                else:
                    dve.wait_ge(product, products_before(n + 1))
                    dve.wait_ge(inverse_ready, n - 1)
                    dve.tensor_tensor(m, m, pi[:, b, :].rearrange("p (h s) -> p h s", h=4), ALU.add
                                      ).then_inc(inverse_ready, 1)

            for n in range(len(steps) + 1):
                if n < len(steps):
                    t_power(n)
                if n >= 1:
                    factor(n - 1)


def delta_recurrence(nc, k, dg, q_t, k_t, k_tok, v_tok, inv_t, qd, o):
    order = {0: [2, 3, 0, 1], 1: [3, 2, 1, 0]}
    jobs = [(order[d][s], d, g) for s in range(TILES) for d in range(2) for g in range(2)]
    n_jobs = len(jobs)
    with Stage(nc, "dnrec") as st:
        state = st.sb("state", [P, 2, 2, 4, P])
        rhs = st.sb("rhs", [P, 2, 4, P])
        kd = st.sb("kd", [P, 2, 4, P])
        vn = st.sb("vn", [P, 2, 4, P])
        tmp = st.sb("tmp", [P, 4, P])
        pks = st.ps("pks", [P, 2, CW])
        pqs = st.ps("pqs", [P, CW])
        pvn = st.ps("pvn", [P, 2, CW])
        psu = st.ps("psu", [P, 2, CW])
        poi = st.ps("poi", [P, CW])
        zeroed, recalled, rhs_ready, kd_ready, v_new, vn_ready, updated, state_ready, out_done, dve_done = (
            st.sem(n) for n in ("zeroed", "recalled", "rhs_ready", "kd_ready", "v_new", "vn_ready", "updated",
                                "state_ready", "out_done", "dve_done"))
        block = st.block()

        def four(ap):
            return ap.rearrange("p (h s) -> p h s", h=4)

        def factor(what, i):
            t, d, g = jobs[i]
            v = dg[what][:, t, d * DN_HEADS + g * 4:d * DN_HEADS + g * 4 + 4]
            return v.unsqueeze(2).broadcast_to([P, 4, P])

        def outs(i):
            return sum(1 for t, _, _ in jobs[:i] if t < TT)

        @block.tensor
        def _(pe):
            def recall(i):
                t, d, g = jobs[i]
                pe.wait_ge(zeroed, 2)
                if i >= 4:
                    pe.wait_ge(state_ready, i - 3)
                if i >= 2:
                    pe.wait_ge(rhs_ready, i - 1)
                for h in range(4):
                    last = pe.matmul(pks[:, i % 2, h * P:(h + 1) * P], k_t[:, g * 4 + h, t * P:(t + 1) * P],
                                     state[:, d, g, h, :], start=True, stop=True)
                if t < TT:
                    if outs(i) >= 1:
                        pe.wait_ge(out_done, outs(i))
                    for h in range(4):
                        last = pe.matmul(pqs[:, h * P:(h + 1) * P], q_t[:, g * 4 + h, t * P:(t + 1) * P],
                                         state[:, d, g, h, :], start=True, stop=True)
                last.then_inc(recalled, 1)

            def solve(i):
                t, d, g = jobs[i]
                pe.wait_ge(rhs_ready, i + 1)
                if i >= 2:
                    pe.wait_ge(vn_ready, i - 1)
                for h in range(4):
                    last = pe.matmul(pvn[:, i % 2, h * P:(h + 1) * P], inv_t[:, t, d, g * 4 + h, :],
                                     rhs[:, i % 2, h, :], start=True, stop=True)
                last.then_inc(v_new, 1)

            def update(i):
                t, d, g = jobs[i]
                pe.wait_ge(vn_ready, i + 1)
                pe.wait_ge(kd_ready, i + 1)
                if i >= 2:
                    pe.wait_ge(state_ready, i - 1)
                for h in range(4):
                    last = pe.matmul(psu[:, i % 2, h * P:(h + 1) * P], kd[:, i % 2, h, :], vn[:, i % 2, h, :],
                                     start=True, stop=True)
                if t < TT:
                    if outs(i) >= 1:
                        pe.wait_ge(out_done, outs(i))
                    for h in range(4):
                        last = pe.matmul(poi[:, h * P:(h + 1) * P], qd[:, t, d, g * 4 + h, :], vn[:, i % 2, h, :],
                                         start=True, stop=True)
                last.then_inc(updated, 1)

            for i in range(n_jobs):
                recall(i)
                solve(i)
                update(i)

        @block.gpsimd
        def _(pool):
            pool.memset(state[:], 0.0).then_inc(zeroed, 1)
            pool.memset(o[:], 0.0).then_inc(zeroed, 1)
            for i, (t, d, g) in enumerate(jobs):
                if i >= 2:
                    pool.wait_ge(updated, i - 1)
                pool.tensor_tensor(kd[:, i % 2], k_tok[:, t, g * 4 * P:(g + 1) * 4 * P].rearrange(
                    "p (h s) -> p h s", h=4), factor("exp_rest", i), ALU.mult).then_inc(kd_ready, 1)

        @block.scalar
        def _(act):
            for i in range(n_jobs):
                act.wait_ge(v_new, i + 1)
                if i >= 2:
                    act.wait_ge(updated, i - 1)
                act.copy(vn[:, i % 2], four(pvn[:, i % 2, :])).then_inc(vn_ready, 1)

        @block.vector
        def _(dve):
            step = InOrder(dve, dve_done)
            dve.wait_ge(zeroed, 2)
            for i, (t, d, g) in enumerate(jobs):
                cols = slice(g * 4 * P, (g + 1) * 4 * P)
                dve.wait_ge(recalled, i + 1)
                if i >= 2:
                    dve.wait_ge(v_new, i - 1)
                r = rhs[:, i % 2]
                step(dve.tensor_tensor(r, four(pks[:, i % 2, :]), factor("exp_g", i), ALU.mult))
                step(dve.tensor_tensor(r, four(v_tok[:, t, cols]), r, ALU.subtract))
                dve.tensor_tensor(r, r, factor("beta", i), ALU.mult).then_inc(rhs_ready, 1)
                s = state[:, d, g]
                step(dve.tensor_tensor(s, s, factor("exp_last", i), ALU.mult))
                if t < TT:
                    step(dve.tensor_tensor(tmp[:], four(pqs[:]), factor("exp_g", i), ALU.mult))
                    step(dve.tensor_tensor(four(o[:, t, cols]), four(o[:, t, cols]), tmp[:], ALU.add))
                dve.wait_ge(updated, i + 1)
                dve.tensor_tensor(s, s, four(psu[:, i % 2, :]), ALU.add).then_inc(state_ready, 1)
                if t < TT:
                    dve.tensor_tensor(four(o[:, t, cols]), four(o[:, t, cols]), four(poi[:]), ALU.add
                                      ).then_inc(out_done, 1)
                    dve.wait_ge(out_done, outs(i + 1))


def turn_back(nc, k, name, v_t, out):
    with Stage(nc, name) as st:
        banks = 6
        psum = st.ps("psum", [P, banks, CW])
        turned, copied, moved = st.sem("turned"), st.sem("copied"), st.sem("moved")
        jobs = [(t, g) for t in range(TILES) for g in range(2)]
        block = st.block()

        @block.tensor
        def _(pe):
            for n, (t, g) in enumerate(jobs):
                if n >= banks:
                    prior = n - banks
                    pe.wait_ge(copied if prior % 2 == 0 else moved, prior // 2 + 1)
                for h in range(4):
                    last = pe.transpose(psum[:, n % banks, h * P:(h + 1) * P],
                                        v_t[:, g * 4 + h, t * P:(t + 1) * P], k["ident"][:])
                last.then_inc(turned, 1)

        @block.vector
        def _(dve):
            for n in range(0, len(jobs), 2):
                t, g = jobs[n]
                dve.wait_ge(turned, n + 1)
                dve.tensor_copy(out[:, t, g * CW:(g + 1) * CW], psum[:, n % banks, :]).then_inc(copied, 1)

        @block.scalar
        def _(act):
            for n in range(1, len(jobs), 2):
                t, g = jobs[n]
                act.wait_ge(turned, n + 1)
                act.copy(out[:, t, g * CW:(g + 1) * CW], psum[:, n % banks, :]).then_inc(moved, 1)


def delta_layer(nc, k, ins, mod, modc):
    x = k["x"]
    m = [mod[:, i * D:(i + 1) * D] for i in range(6)]
    with Stage(nc, "dn") as st:
        o = st.sb("o", [P, TT, D])
        gate = st.sb("gate", [P, TT, D])
        with Stage(nc, "dna") as sa:
            q_t = sa.sb("q_t", [P, DN_HEADS, S])
            k_t = sa.sb("k_t", [P, DN_HEADS, XC])
            v_tok = sa.sb("v_tok", [P, TILES, D])
            dg = {n: sa.sb(n, [P, TILES, DH]) for n in ("beta", "g_sum", "exp_g", "exp_rest", "exp_last")}
            dg["rows"] = sa.sb("rows", [DH, TILES, S])
            with Stage(nc, "dnb") as sb:
                h_t = sb.sb("h_t", [P, KT, XC])
                with Stage(nc, "dnc") as sc:
                    ctx = sc.sb("ctx", [P, TT, D])
                    loaded = sc.sem("loaded")
                    block = nc.Block()
                    with block as block:
                        @block.sync
                        def _(sp):
                            sp.dma_start(ctx[:], ins["ctx"].rearrange("(t p) d -> p t d", p=P)).then_inc(loaded, 16)
                            sp.wait_ge(loaded, 16)
                    normed(nc, k, "dnorm", x, ins["norm_g2"][0], m[0], m[1], h_t[:, :, 0:S])
                    normed(nc, k, "dcnorm", ctx, ins["norm_g2"][0], modc[:, 0:D], modc[:, D:2 * D], h_t[:, :, S:XC])
                with Stage(nc, "dnd") as sd:
                    v_t = sd.sb("v_t", [P, DN_HEADS, XC])
                    delta_qkv(nc, k, ins, h_t, q_t, k_t, v_t)
                    turn_back(nc, k, "dnv", v_t, v_tok)
                delta_unit(nc, k, q_t, k_t)
                project(nc, k, "dngp", h_t, chunked(ins["dn_w_gate"], D), out=gate)
                delta_gates(nc, k, ins, h_t, dg)
            k_tok = sa.sb("k_tok", [P, TILES, D])
            turn_back(nc, k, "dnk", k_t, k_tok)
            at_m = sa.sb("at_m", [P, TILES, 2, DN_HEADS, P])
            qd = sa.sb("qd", [P, TT, 2, DN_HEADS, P])
            delta_matrices(nc, k, dg, q_t, k_t, at_m, qd)
            delta_inverse(nc, k, at_m)
            delta_recurrence(nc, k, dg, q_t, k_t, k_tok, v_tok, at_m, qd, o)
        h_t = st.sb("o_t", [P, KT, S])
        head_norm(nc, k, "dnon", o[:], ins["dn_norm_g"], 1.0, gate=gate[:])
        turn(nc, k, "dnot", o, [i * P for i in range(KT)], h_t)
        project(nc, k, "dnout", h_t, chunked(ins["dn_w_out"], D), residual=(x, m[2]))


def peer_scores(nc, k, ins, h_t, scores):
    with Stage(nc, "pq") as st:
        ring = 3
        w = st.sb("w", [P, ring, KT * CW])
        q_t = st.sb("q_t", [P, 16, S])
        keys = st.sb("keys", [P, 16, NKEYS])
        psum = st.ps("psum", [P, 4, CW])
        pscore = st.ps("pscore", [P, 2, CW])
        slot_loaded = [st.sem(f"slot_loaded{i}") for i in range(ring)]
        keys_loaded, product, q_ready, scored, stored = (
            st.sem(n) for n in ("keys_loaded", "product", "q_ready", "scored", "stored"))
        block = st.block()

        @block.sync
        def _(sp):
            for j in range(4):
                if j >= ring:
                    sp.wait_ge(product, 4 * (j - ring + 1))
                sp.dma_start(w[:, j % ring, :], ins["peer_w_q"][j]).then_inc(slot_loaded[j % ring], 16)
            sp.dma_start(keys[:], ins["peer_keys"]).then_inc(keys_loaded, 16)

        @block.tensor
        def _(pe):
            for b in range(16):
                j, col = b // 4, (b % 4) * P
                pe.wait_ge(slot_loaded[j % ring], 16 * (j // ring + 1))
                if b >= 4:
                    pe.wait_ge(q_ready, b - 3)
                for c in range(KT):
                    last = pe.matmul(psum[:, b % 4, 0:S], w[:, j % ring, c * CW + col:c * CW + col + P],
                                     h_t[:, c, :], start=(c == 0), stop=(c == KT - 1))
                last.then_inc(product, 1)
            pe.wait_ge(keys_loaded, 16)
            pe.wait_ge(q_ready, 16)
            for n in range(8):
                t, quad = n // 4, n % 4
                if n >= 2:
                    pe.wait_ge(stored, n - 1)
                for b in range(4):
                    hp = quad * 4 + b
                    last = pe.matmul(pscore[:, n % 2, b * P:(b + 1) * P], q_t[:, hp, t * P:(t + 1) * P],
                                     keys[:, hp, :], start=True, stop=True)
                last.then_inc(scored, 1)

        @block.scalar
        def _(act):
            for b in range(16):
                act.wait_ge(product, b + 1)
                act.copy(q_t[:, b, :], psum[:, b % 4, 0:S]).then_inc(q_ready, 1)
            for n in range(8):
                t, quad = n // 4, n % 4
                act.wait_ge(scored, n + 1)
                act.copy(scores[:, t, quad * 4:quad * 4 + 4, :],
                         pscore[:, n % 2, :].rearrange("p (b s) -> p b s", b=4)).then_inc(stored, 1)


def peer_route(nc, k, scores, chosen):
    with Stage(nc, "route") as st:
        val = st.sb("val", [P, TT, 16, TOPK])
        idx = st.sb("idx", [P, TT, 16, TOPK], U32)
        idx_f = st.sb("idx_f", [P, TT, 16, TOPK])
        cand = st.sb("cand", [P, PHEADS, TOPK, TOPK])
        left = st.sb("left", [P, 2, TOPK * TOPK])
        top = st.sb("top", [P, TT, PHEADS, TOPK])
        pos = st.sb("pos", [P, TT, PHEADS, TOPK], U32)
        ab = st.sb("ab", [P, 2, PHEADS * TOPK], U32)
        ab_f = st.sb("ab_f", [P, 2, PHEADS * TOPK])
        hot = st.sb("hot", [P, PHEADS, TOPK, TOPK])
        pick = st.sb("pick", [P, TT, 3, P])
        total = st.sb("total", [P, PHEADS])
        psum = st.ps("psum", [P, 2, CW])
        shifted, exped, picked, turned, dve_done = (
            st.sem(n) for n in ("shifted", "exped", "picked", "turned", "dve_done"))
        block = st.block()

        @block.vector
        def _(dve):
            step = InOrder(dve, dve_done)

            def top16(values, spare, out_v, out_i):
                step(dve.max(out_v[:, 0:8], values))
                step(dve.match_replace(spare, out_v[:, 0:8], values, NEG))
                step(dve.max(out_v[:, 8:16], spare))
                step(dve.max_index(out_i[:, 0:8], out_v[:, 0:8], values))
                step(dve.max_index(out_i[:, 8:16], out_v[:, 8:16], spare))

            for t in range(TT):
                for hp in range(16):
                    top16(scores[:, t, hp, :], left[:, hp % 2, 0:P], val[:, t, hp, :], idx[:, t, hp, :])
            step(dve.tensor_copy(idx_f[:], idx[:]))
            for t in range(TT):
                v = val[:, t].rearrange("p (h two) n -> p h two n", two=2)
                four_d = [P, PHEADS, TOPK, TOPK]
                step(dve.tensor_tensor(cand[:], v[:, :, 0, :].unsqueeze(3).broadcast_to(four_d),
                                       v[:, :, 1, :].unsqueeze(2).broadcast_to(four_d), ALU.add))
                for h in range(PHEADS):
                    top16(cand[:, h].rearrange("p a b -> p (a b)"), left[:, h % 2, :], top[:, t, h, :], pos[:, t, h, :])
                flat = pos[:, t].rearrange("p h n -> p (h n)")
                step(dve.tensor_scalar(ab[:, 0, :], flat, 4, None, ALU.logical_shift_right))
                step(dve.tensor_scalar(ab[:, 1, :], flat, TOPK - 1, None, ALU.bitwise_and))
                step(dve.tensor_copy(ab_f[:], ab[:]))
                of = idx_f[:, t].rearrange("p (h two) n -> p h two n", two=2)
                for part in range(2):
                    step(dve.tensor_tensor(hot[:].rearrange("p h n a -> p (h n) a"),
                                           ab_f[:, part, :].unsqueeze(2).broadcast_to([P, P, TOPK]),
                                           k["iota"][:, 0:TOPK].unsqueeze(1).broadcast_to([P, P, TOPK]), ALU.is_equal))
                    step(dve.tensor_tensor(hot[:], hot[:], of[:, :, part, :].unsqueeze(2).broadcast_to(four_d), ALU.mult))
                    step(dve.tensor_reduce(pick[:, t, part, :], hot[:].rearrange("p h n a -> p (h n) a"), AX.X, ALU.add))
                gate = pick[:, t, 2, :].rearrange("p (h n) -> p h n", h=PHEADS)
                three = [P, PHEADS, TOPK]
                dve.tensor_tensor(gate, top[:, t], top[:, t, :, 0:1].broadcast_to(three), ALU.subtract).then_inc(shifted, 1)
                dve.wait_ge(exped, t + 1)
                step(dve.tensor_reduce(total[:], gate, AX.X, ALU.add))
                step(dve.reciprocal(total[:], total[:]))
                dve.tensor_tensor(gate, gate, total[:].unsqueeze(2).broadcast_to(three), ALU.mult).then_inc(picked, 1)
            for t in range(TT):
                dve.wait_ge(turned, t + 1)
                step(dve.tensor_copy(chosen[:, :, t * P:(t + 1) * P],
                                     psum[:, t, 0:3 * P].rearrange("p (c s) -> p c s", c=3)))

        @block.scalar
        def _(act):
            for t in range(TT):
                act.wait_ge(shifted, t + 1)
                act.activation(pick[:, t, 2, :], pick[:, t, 2, :], ACT.Exp).then_inc(exped, 1)

        @block.tensor
        def _(pe):
            for t in range(TT):
                pe.wait_ge(picked, t + 1)
                for c in range(3):
                    last = pe.transpose(psum[:, t, c * P:(c + 1) * P], pick[:, t, c, :], k["ident"][:])
                last.then_inc(turned, 1)


def peer_table(nc, k, chosen, table):
    per = 4
    quads = S // per
    with Stage(nc, "table") as st:
        first = st.sb("first", [P, 2, per, NKEYS])
        second = st.sb("second", [P, 2, per, NKEYS])
        psum = st.ps("psum", [P, 4, CW])
        hot, product, stored = (st.sem(n) for n in ("hot", "product", "stored"))
        block = st.block()

        @block.vector
        def _(dve):
            def one_hot(i, b, early=False):
                if not early:
                    dve.wait_ge(product, i - 1)
                for j in range(per):
                    at = [chosen[:, c, bass.ds(i * per + j, 1)] for c in range(3)]
                    dve.tensor_scalar(first[:, b, j, :], k["iota"][:], at[0], None, ALU.is_equal)
                    last = dve.tensor_scalar(second[:, b, j, :], k["iota"][:], at[1], at[2], ALU.is_equal, ALU.mult)
                last.then_inc(hot, 1)

            one_hot(0, 0, early=True)
            one_hot(1, 1, early=True)
            with dve.Fori(1, quads // 2) as r:
                for b in range(2):
                    one_hot(r * 2 + b, b)

        @block.tensor
        def _(pe):
            def products(i, b, bank, early=False):
                pe.wait_ge(hot, i + 1)
                if not early:
                    pe.wait_ge(stored, i - 3)
                for j in range(per):
                    last = pe.matmul(psum[:, bank, j * P:(j + 1) * P], first[:, b, j, :], second[:, b, j, :],
                                     start=True, stop=True)
                last.then_inc(product, 1)

            for i in range(4):
                products(i, i % 2, i, early=True)
            with pe.Fori(1, quads // 4) as r:
                for b in range(4):
                    products(r * 4 + b, b % 2, b)

        @block.scalar
        def _(act):
            with act.Fori(0, quads // 4) as r:
                for b in range(4):
                    act.wait_ge(product, r * 4 + (b + 1))
                    act.copy(table[:, :, bass.ds((r * 4 + b) * per, per)].rearrange("p n t -> p t n"),
                             psum[:, b, :].rearrange("p (t n) -> p t n", t=per)).then_inc(stored, 1)


def final_norm(nc, k, ins, out):
    x = k["x"]
    with Stage(nc, "final") as st:
        g = st.sb("g", [P, D])
        junk = st.sb("junk", [P, D])
        ss = st.sb("ss", [P, TT])
        loaded, squared, mean_ready, root_ready, ready, stored, dve_done = (
            st.sem(n) for n in ("loaded", "squared", "mean_ready", "root_ready", "ready", "stored", "dve_done"))
        block = st.block()

        @block.sync
        def _(sp):
            sp.dma_start(g[:], ins["final_g"].partition_broadcast(P)).then_inc(loaded, 16)
            for t in range(TT):
                sp.wait_ge(ready, t + 1)
                sp.dma_start(out[t * P:(t + 1) * P, :], x[:, t, :]).then_inc(stored, 16)
            sp.wait_ge(stored, 16 * TT)

        @block.scalar
        def _(act):
            for t in range(TT):
                act.activation(junk[:], x[:, t, :], ACT.Square, accum_out=ss[:, t:t + 1]).then_inc(squared, 1)
                act.wait_ge(squared, t + 1)
            act.wait_ge(mean_ready, 1)
            act.activation(ss[:], ss[:], ACT.Sqrt).then_inc(root_ready, 1)

        @block.vector
        def _(dve):
            step = InOrder(dve, dve_done)
            dve.wait_ge(squared, TT)
            dve.tensor_scalar(ss[:], ss[:], 1.0 / D, EPS, ALU.mult, ALU.add).then_inc(mean_ready, 1)
            dve.wait_ge(root_ready, 1)
            step(dve.reciprocal(ss[:], ss[:]))
            dve.wait_ge(loaded, 16)
            for t in range(TT):
                dve.scalar_tensor_tensor(x[:, t, :], x[:, t, :], ss[:, t:t + 1], g[:], ALU.mult,
                                         ALU.mult).then_inc(ready, 1)




def program(nc, ins, out):
    with Stage(nc, "all") as pst:
        k = constants(nc, pst, ins)
        sparse_layer(nc, k, ins)
        diff_layer(nc, k, ins)
        gate2 = pst.sb("gate2", [P, D])
        chosen = pst.sb("chosen", [P, 3, S])
        modc = pst.sb("modc", [P, 2 * D])
        h_t = modc[:].rearrange("p (c s) -> p c s", c=KT)
        with Stage(nc, "l2") as st:
            mod = st.sb("mod", [P, 6 * D])
            modulation(nc, k, "ada2", ins["ada_w2"], ins["ada_b2"], [(ins["c2"], mod, 12), (ins["c_ctx2"], modc, 4)])
            delta_layer(nc, k, ins, mod, modc)
            m = [mod[:, i * D:(i + 1) * D] for i in range(6)]
            normed(nc, k, "pnorm", k["x"], ins["norm_g2"][1], m[3], m[4], h_t)
            kept = st.sem("kept")
            with nc.Block() as block:
                @block.vector
                def _(dve):
                    dve.tensor_copy(gate2[:], m[5]).then_inc(kept, 1)
                    dve.wait_ge(kept, 1)
            scores = st.sb("scores", [P, TT, 16, NKEYS])
            peer_scores(nc, k, ins, h_t, scores)
            peer_route(nc, k, scores, chosen)
        with Stage(nc, "peer") as st:
            table = st.sb("table", [P, NKEYS, S])
            peer_table(nc, k, chosen, table)
            streamed_mlp(nc, k, "experts", h_t, ins["peer_uv"], "peer", (k["x"], gate2[:]), table=table)
        final_norm(nc, k, ins, out)




def _column_tiles(w, width=CW):
    n = w.shape[1] // width
    return w.reshape(KT, P, n, width).transpose(2, 1, 0, 3).reshape(n, P, KT * width)


def _mlp_tiles(columns, rows):
    n = rows.shape[0] // P
    parts = [c.reshape(KT, P, n, P).transpose(2, 1, 0, 3).reshape(n, P, KT * P) for c in columns]
    return np.concatenate(parts + [rows.reshape(n, P, D)], axis=2)


def _layout(a):
    a = {name: np.asarray(v) for name, v in a.items()}
    slots = np.array([b + 4 * g for b in range(4) for g in range(2)])
    w = a["sp_w_in"][0]
    nq = w[:, Z_NQ:Z_KV].reshape(D, HEADS, HEAD)[:, slots].reshape(D, -1)
    ng = w[:, Z_GATE:].reshape(D, 3, HEADS)[:, :, slots].reshape(D, -1)
    w = np.concatenate([w[:, :Z_NQ], nq, w[:, Z_KV:Z_GATE], ng], axis=1)
    out = {"x": a["x"][0], "positions": a["positions"].reshape(TT, P).T, "sp_w_in": _column_tiles(w[:, :5 * CW]),
           "sp_w_in_tail": _column_tiles(w[:, 5 * CW:], SP_IN - 5 * CW)[0]}
    wo = a["sp_w_out"][0].reshape(2, HEADS, HEAD, D)
    wo = np.concatenate([wo[0], wo[1][slots]]).reshape(D, D)
    out["sp_w_out"] = _column_tiles(wo)
    for i in range(2):
        out[f"ada_w{i}"] = _column_tiles(a["ada_w"][i]).reshape(12, P, KT, CW)
        out[f"ada_b{i}"] = a["ada_b"][i]
        out[f"attn_norm{i}"] = a["attn_norm"][i]
        out[f"ffn_norm{i}"] = a["ffn_norm"][i]
        out[f"ffn{i}"] = _mlp_tiles([a["ffn_w_gate"][i], a["ffn_w_up"][i]], a["ffn_w_down"][i])
    out["c"] = a["c"].reshape(KT, P).T
    out["moba_q_norm"], out["moba_k_norm"] = a["moba_q_norm"][0], a["moba_k_norm"][0]
    out["nsa_q_norm"], out["nsa_k_norm"] = a["nsa_q_norm"][0], a["nsa_k_norm"][0]
    out["cmp_pos"] = a["nsa_cmp_pos"][0].transpose(2, 0, 1)
    out["cmp_w1"] = a["nsa_cmp_w1"][0].transpose(0, 2, 1, 3)
    out["cmp_w2"] = a["nsa_cmp_w2"][0].reshape(2, 2, P, HEAD).transpose(2, 0, 1, 3)
    out["diff_w_in"], out["diff_w_out"] = _column_tiles(a["diff_w_in"][0]), _column_tiles(a["diff_w_out"][0])
    out["diff_q_norm"], out["diff_k_norm"] = a["diff_q_norm"][0], a["diff_k_norm"][0]
    out["diff_lambda"], out["diff_out_norm"] = a["diff_lambda"][0].reshape(-1), a["diff_out_norm"][0]
    out["ada_w2"], out["ada_b2"] = _column_tiles(a["ada_w_2"][0]).reshape(12, P, KT, CW), a["ada_b_2"][0]
    out["c2"], out["c_ctx2"] = a["c_2"].reshape(KT, P).T, a["c_ctx_2"].reshape(KT, P).T
    out["ctx"], out["norm_g2"] = a["ctx_2"][0], a["norm_g_2"][0]
    dn = a["dn_w_in_2"][0]
    out["dn_w_qkv"] = _column_tiles(dn[:, :3 * D])
    out["dn_w_gate"] = _column_tiles(dn[:, 3 * D:4 * D])
    out["dn_w_ba"] = _column_tiles(dn[:, 4 * D:], 4 * DN_HEADS)[0]
    out["dn_conv"] = a["dn_conv_w_2"][0].reshape(DN_CONV, 3 * KT, P).transpose(2, 1, 0)
    out["dn_a_log"], out["dn_dt_bias"] = a["dn_a_log_2"][0].reshape(-1), a["dn_dt_bias_2"][0].reshape(-1)
    out["dn_norm_g"], out["dn_w_out"] = a["dn_norm_g_2"][0], _column_tiles(a["dn_w_out_2"][0])
    out["peer_w_q"] = _column_tiles(a["peer_w_q_2"][0])
    out["peer_keys"] = a["peer_keys_2"][0].reshape(16, NKEYS, P).transpose(2, 0, 1)
    u = a["peer_u_2"][0].reshape(NKEYS, NKEYS, KT, P).transpose(1, 3, 2, 0).reshape(NKEYS, P, KT * P)
    v = a["peer_v_2"][0].reshape(NKEYS, NKEYS, D).transpose(1, 0, 2)
    out["peer_uv"] = np.concatenate([u, v], axis=2)
    out["final_g"] = a["final_g_2"]
    return {name: np.ascontiguousarray(v) for name, v in out.items()}


def kernel(**inputs):
    import concourse.bacc as _bacc
    from concourse.bass_utils import run_bass_kernel_spmd as _run

    nc = _bacc.Bacc("TRN2", target_bir_lowering=False, num_devices=1)
    arrays, aps = {}, {}
    for name, a in _layout(inputs).items():
        arrays[f"in_{name}"] = a
        aps[name] = nc.dram_tensor(f"in_{name}", a.shape, mybir.dt.from_np(a.dtype), kind="ExternalInput").ap()
    out = nc.dram_tensor("out_x", (S, D), F32, kind="ExternalOutput").ap()
    program(nc, aps, out)
    r = _run(nc, [arrays], core_ids=[0])
    return r.results[0]["out_x"].reshape(1, S, D)
```

```python
import math
from contextlib import ExitStack

import concourse.bass as bass
import numpy as np
from concourse import mybir

ALU = mybir.AluOpType
ACT = mybir.ActivationFunctionType
AX = mybir.AxisListType
F32 = mybir.dt.float32
F32R = mybir.dt.float32r
I32 = mybir.dt.int32
U32 = mybir.dt.uint32

P = 128
D = 1024
KT = D // P
S = 256
TT = S // P
EPS = 1e-6
NEG = -1e30
CW = 512

HEAD = 64
ROT = HEAD // 4
HALF = ROT // 2
ROPE_THETA = 500000.0
HEADS = 8
FFN = 2816
FFN_CHUNKS = FFN // P

CMP_LEN, CMP_STRIDE, CMP_HIDDEN = 32, 16, 256
NCMP = (S - CMP_LEN) // CMP_STRIDE + 1
SP_IN = 2840
Z_MQ, Z_MK, Z_MV, Z_NQ, Z_KV, Z_GATE = 0, 512, 1024, 1536, 2048, 2816
KV_BRANCH, KV_VALUE = 256, 128

DIFF_LAM_INIT = 0.8 - 0.6 * float(np.exp(-0.3 * 1))

DN_HEADS = 8
DN_CONV = 5
ROW = 64
NKEYS = 128
TOPK = 16
PHEADS = 8

SC = 384


class Stage:

    def __init__(self, nc, name):
        self.nc, self.name, self.stack, self.sems = nc, name, ExitStack(), []

    def __enter__(self):
        self.stack.callback(self.clear)
        return self

    def clear(self):
        for sem in self.sems:
            self.nc.gpsimd.sem_clear(sem)
            self.nc.release_semaphore(sem)

    def __exit__(self, *error):
        return self.stack.__exit__(*error)

    def sb(self, name, shape, dtype=F32):
        return self.stack.enter_context(self.nc.sbuf_tensor(f"{self.name}_{name}", shape, dtype))

    def ps(self, name, shape):
        return self.stack.enter_context(self.nc.psum_tensor(f"{self.name}_{name}", shape, F32))

    def sem(self, name):
        self.sems.append(self.nc.alloc_semaphore(f"{self.name}_{name}"))
        return self.sems[-1]

    def block(self):
        self.engines = self.stack.enter_context(ExitStack())
        return self.engines.enter_context(self.nc.Block())

    def end_block(self):
        self.engines.close()


class InOrder:

    def __init__(self, engine, done):
        self.engine, self.done, self.n = engine, done, 0

    def __call__(self, instruction):
        instruction.then_inc(self.done, 1)
        self.n += 1
        self.engine.wait_ge(self.done, self.n)


def constants(nc, pst, ins, k):
    k.update({
        "causal": pst.sb("causal", [P, SC]),
        "incl": pst.sb("incl", [P, 2, P]),
        "strict": pst.sb("strict", [P, 2, P]),
        "decay_mask": pst.sb("decay_mask", [P, 2, P]),
        "cmp_mask": pst.sb("cmp_mask", [P, TT, NCMP]),
        "cmp_valid": pst.sb("cmp_valid", [P, TT, NCMP]),
        "cos": pst.sb("cos", [P, TT, HALF]),
        "sin": pst.sb("sin", [P, TT, HALF]),
        "silu_c": pst.sb("silu_c", [P, 3, KT]),
        "x": pst.sb("x", [P, TT, D]),
    })
    with Stage(nc, "const") as st:
        pos_i = st.sb("pos_i", [P, TT], I32)
        pos = st.sb("pos", [P, TT])
        freq = st.sb("freq", [P, HALF])
        ang = st.sb("ang", [P, TT, HALF])
        turns = st.sb("turns", [P, TT, HALF])
        rest = st.sb("rest", [P, 2, TT, HALF])
        loaded, c_loaded, filled, freq_set, reduced, tables, dve_done = (
            st.sem(n) for n in ("loaded", "c_loaded", "filled", "freq_set", "reduced", "tables", "dve_done"))
        block = st.block()

        @block.sync
        def _(sp):
            sp.dma_start(k["x"][:], ins["x"].rearrange("(t p) d -> p t d", p=P)).then_inc(loaded, 16)
            sp.dma_start(pos_i[:], ins["positions"]).then_inc(loaded, 16)
            for v, name in enumerate(("c", "c2", "c_ctx2")):
                sp.dma_start(k["silu_c"][:, v, :], ins[name]).then_inc(c_loaded, 16)
            sp.wait_ge(loaded, 32)

        @block.gpsimd
        def _(pool):
            step = InOrder(pool, filled)
            for c in range(HALF):
                inv = np.float32(1.0) / np.float32(ROPE_THETA) ** np.float32(2 * c / ROT)
                pool.memset(freq[:, c:c + 1], float(inv)).then_inc(freq_set, 1)
            step(pool.memset(k["ident"][:], 0.0))
            step(pool.affine_select(out=k["ident"][:], in_=k["ident"][:], compare_op=ALU.not_equal, fill=1.0,
                                    base=0, pattern=[[-1, P]], channel_multiplier=1))
            step(pool.memset(k["ones"][:], 1.0))
            step(pool.iota(k["iota"][:], pattern=[[1, P]], base=0, channel_multiplier=0,
                           allow_small_or_imprecise_dtypes=True))
            step(pool.memset(k["causal"][:], 0.0))
            for lo, base in ((0, 0), (P, P)):
                width = P if lo == 0 else S
                step(pool.affine_select(out=k["causal"][:, lo:lo + width], in_=k["causal"][:, lo:lo + width],
                                        compare_op=ALU.is_ge, fill=NEG, base=base, pattern=[[-1, width]],
                                        channel_multiplier=1))
            for d, sign in ((0, 1), (1, -1)):
                for name, base, fill, start in (("incl", 0, 0.0, 1.0), ("strict", -1, 0.0, 1.0),
                                                ("decay_mask", 0, NEG, 0.0)):
                    v = k[name][:, d, :]
                    step(pool.memset(v, start))
                    step(pool.affine_select(out=v, in_=v, compare_op=ALU.is_ge, fill=fill, base=base,
                                            pattern=[[sign, P]], channel_multiplier=-sign))
            for name, fill, start in (("cmp_mask", NEG, 0.0), ("cmp_valid", 0.0, 1.0)):
                step(pool.memset(k[name][:], start))
                for t in range(TT):
                    step(pool.affine_select(out=k[name][:, t, :], in_=k[name][:, t, :], compare_op=ALU.is_ge,
                                            fill=fill, base=t * P - (CMP_LEN - 1), pattern=[[-CMP_STRIDE, NCMP]],
                                            channel_multiplier=1))

        @block.vector
        def _(dve):
            step = InOrder(dve, dve_done)
            two_pi = 2 * math.pi
            hi = float(np.float32(6.28125))
            mid = float(np.float32(two_pi - hi))
            lo = two_pi - hi - mid
            magic = 1.5 * 2.0 ** 23
            dve.wait_ge(loaded, 32)
            dve.wait_ge(freq_set, HALF)
            step(dve.tensor_copy(pos[:], pos_i[:]))
            step(dve.tensor_tensor(ang[:], pos[:].unsqueeze(2).broadcast_to([P, TT, HALF]),
                                   freq[:].unsqueeze(1).broadcast_to([P, TT, HALF]), ALU.mult))
            for n, shift in ((0, 0.0), (1, 0.25)):
                step(dve.tensor_scalar(turns[:], ang[:], 1 / two_pi, shift, ALU.mult, ALU.add))
                step(dve.tensor_scalar(turns[:], turns[:], magic, None, ALU.add))
                step(dve.tensor_scalar(turns[:], turns[:], -magic, None, ALU.add))
                r = rest[:, n]
                step(dve.scalar_tensor_tensor(r, turns[:], -hi, ang[:], ALU.mult, ALU.add))
                step(dve.scalar_tensor_tensor(r, turns[:], -mid, r, ALU.mult, ALU.add))
                step(dve.scalar_tensor_tensor(r, turns[:], -lo, r, ALU.mult, ALU.add))
                step(dve.tensor_scalar(r, r, shift * two_pi, None, ALU.add))
                step(dve.tensor_scalar(r, r, 3.1415925, -3.1415925, ALU.min, ALU.max))
            dve.tensor_copy(turns[:], rest[:, 0]).then_inc(reduced, 1)

        @block.scalar
        def _(act):
            act.wait_ge(c_loaded, 48)
            act.activation(k["silu_c"][:], k["silu_c"][:], ACT.Silu).then_inc(tables, 1)
            act.wait_ge(reduced, 1)
            act.activation(k["sin"][:], rest[:, 0], ACT.Sin).then_inc(tables, 1)
            act.activation(k["cos"][:], rest[:, 1], ACT.Sin).then_inc(tables, 1)
            act.wait_ge(tables, 3)


class Modulation:

    def __init__(self, nc, k, st, weights, bias, vectors, first=0):
        self.nc, self.k, self.weights, self.bias, self.vectors, self.first = nc, k, weights, bias, vectors, first
        self.w = st.sb("ada_w", [P, 2, KT, CW // 2])
        self.w_loaded = [st.sem(f"ada_w_loaded{i}") for i in range(2)]
        self.folded = st.sem("ada_folded")
        self.step_done = st.sem("ada_step_done")

    def load(self, sp, half, slot, early=False):
        if not early:
            sp.wait_ge(self.folded, half - (self.first + 1))
        source = self.weights[half] if isinstance(half, int) else \
            self.weights[bass.ds(half, 1)].rearrange("a p c n -> p (a c) n")
        sp.dma_start(self.w[:, slot], source).then_inc(self.w_loaded[slot], 16)

    def fold(self, dve, half, slot, steps_before, rounds_before):
        dve.wait_ge(self.w_loaded[slot], 16 * rounds_before + 16)
        n = 0
        for silu_c, row, _ in [v for v in self.vectors if not isinstance(half, int) or half < 2 * v[2]]:
            if not isinstance(half, int) and row is not self.vectors[0][1]:
                continue
            width = CW // 2
            acc = row[:, half * width:(half + 1) * width] if isinstance(half, int) else \
                row[:, bass.ds(half * width, width)]
            for c in range(KT):
                if c == 0:
                    last = dve.tensor_scalar(acc, self.w[:, slot, c, :], silu_c[:, c:c + 1], None, ALU.mult)
                else:
                    dve.wait_ge(self.step_done, steps_before + n)
                    last = dve.scalar_tensor_tensor(acc, self.w[:, slot, c, :], silu_c[:, c:c + 1], acc, ALU.mult,
                                                    ALU.add)
                last.then_inc(self.step_done, 1)
                n += 1
        dve.wait_ge(self.step_done, steps_before + n)
        dve.sem_inc(self.folded, 1)
        return n


def finish_modulation(nc, k, name, bias, rows):
    jobs = [(row, j) for row, lo, hi in rows for j in range(lo, hi)]
    with Stage(nc, name) as st:
        b = st.sb("b", [P, 6 * D])
        psum = st.ps("psum", [P, 4, CW])
        loaded = [st.sem(f"loaded{i}") for i in range(len(jobs))]
        summed, added = st.sem("summed"), st.sem("added")
        block = st.block()

        @block.sync
        def _(sp):
            for n, (row, j) in enumerate(jobs):
                cols = slice(j * CW, (j + 1) * CW)
                if (row, j) == jobs[n] and j not in [x for _, x in jobs[:n]]:
                    sp.dma_start(b[:, cols], bias[cols].partition_broadcast(P)).then_inc(loaded[n], 16)

        @block.tensor
        def _(pe):
            for n, (row, j) in enumerate(jobs):
                if n >= 4:
                    pe.wait_ge(added, n - 3)
                pe.matmul(psum[:, n % 4, :], k["ones"][:], row[:, j * CW:(j + 1) * CW], start=True,
                          stop=True).then_inc(summed, 1)

        @block.vector
        def _(dve):
            first_use = {}
            for n, (row, j) in enumerate(jobs):
                first_use.setdefault(j, n)
                cols = slice(j * CW, (j + 1) * CW)
                dve.wait_ge(loaded[first_use[j]], 16)
                dve.wait_ge(summed, n + 1)
                dve.tensor_tensor(row[:, cols], psum[:, n % 4, :], b[:, cols], ALU.add).then_inc(added, 1)


def first_modulation(nc, k, name, weights, silu_c, row, halves):
    with Stage(nc, name) as st:
        ring = 4
        width = CW // 2
        w = st.sb("w", [P, ring, KT, width])
        cb = st.sb("cb", [P, KT, P])
        b = st.sb("b", [P, halves * width])
        psum = st.ps("psum", [P, 4, CW])
        slot_loaded = [st.sem(f"slot_loaded{i}") for i in range(ring)]
        c_ready, product, added, b_loaded = (st.sem(n) for n in ("c_ready", "product", "added", "b_loaded"))
        source, bias = weights
        block = st.block()

        @block.sync
        def _(sp):
            for j in range(halves):
                if j >= ring:
                    sp.wait_ge(product, j - ring + 1)
                sp.dma_start(w[:, j % ring], source[j]).then_inc(slot_loaded[j % ring], 16)

        @block.scalar
        def _(act):
            act.dma_start(b[:], bias[0:halves * width].partition_broadcast(P)).then_inc(b_loaded, 16)

        @block.vector
        def _(dve):
            dve.tensor_copy(cb[:], silu_c.unsqueeze(2).broadcast_to([P, KT, P])).then_inc(c_ready, 1)
            dve.wait_ge(b_loaded, 16)
            for n in range(halves):
                cols = slice(n * width, (n + 1) * width)
                dve.wait_ge(product, n + 1)
                dve.tensor_tensor(row[:, cols], psum[:, n % 4, 0:width], b[:, cols], ALU.add).then_inc(added, 1)

        @block.tensor
        def _(pe):
            pe.wait_ge(c_ready, 1)
            for n in range(halves):
                pe.wait_ge(slot_loaded[n % ring], 16 * (n // ring + 1))
                if n >= 4:
                    pe.wait_ge(added, n - 3)
                for t in range(KT):
                    last = pe.matmul(psum[:, n % 4, 0:width], cb[:, t, :], w[:, n % ring, t, :],
                                     start=(t == 0), stop=(t == KT - 1))
                last.then_inc(product, 1)


def normed(nc, k, name, x, gain, shift, scale, out_t):
    with Stage(nc, name) as st:
        g = st.sb("gain", [P, D])
        h = st.sb("h", [P, TT, D])
        junk = st.sb("junk", [P, D])
        ss = st.sb("ss", [P, TT])
        psum = st.ps("psum", [P, 4, CW])
        loaded, squared, mean_ready, root_ready, h_ready, turned, copied, dve_done, psum_copied = (
            st.sem(n) for n in ("loaded", "squared", "mean_ready", "root_ready", "h_ready", "turned",
                                "copied", "dve_done", "psum_copied"))
        block = st.block()
        groups = [(t, half) for t in range(TT) for half in range(2)]

        @block.sync
        def _(sp):
            sp.dma_start(g[:], gain.partition_broadcast(P)).then_inc(loaded, 16)

        @block.scalar
        def _(act):
            for t in range(TT):
                act.activation(junk[:], x[:, t, :], ACT.Square, accum_out=ss[:, t:t + 1]).then_inc(squared, 1)
                act.wait_ge(squared, t + 1)
            act.wait_ge(mean_ready, 1)
            act.activation(ss[:], ss[:], ACT.Sqrt).then_inc(root_ready, 1)
            for n in (1, 3):
                t, half = groups[n]
                act.wait_ge(turned, n + 1)
                act.copy(out_t[:, 4 * half:4 * half + 4, t * P:(t + 1) * P],
                         psum[:, n, :].rearrange("p (c q) -> p c q", c=4)).then_inc(psum_copied, 1)

        @block.vector
        def _(dve):
            step = InOrder(dve, dve_done)
            dve.wait_ge(loaded, 16)
            if scale is not None:
                step(dve.scalar_tensor_tensor(g[:], scale, 1.0, g[:], ALU.add, ALU.mult))
            dve.wait_ge(squared, TT)
            dve.tensor_scalar(ss[:], ss[:], 1.0 / D, EPS, ALU.mult, ALU.add).then_inc(mean_ready, 1)
            dve.wait_ge(root_ready, 1)
            step(dve.reciprocal(ss[:], ss[:]))
            for t in range(TT):
                step(dve.scalar_tensor_tensor(h[:, t, :], x[:, t, :], ss[:, t:t + 1], g[:], ALU.mult, ALU.mult))
                dve.tensor_tensor(h[:, t, :], h[:, t, :], shift, ALU.add).then_inc(h_ready, 1)
            for n in (0, 2):
                t, half = groups[n]
                dve.wait_ge(turned, n + 1)
                dve.tensor_copy(out_t[:, 4 * half:4 * half + 4, t * P:(t + 1) * P],
                                psum[:, n, :].rearrange("p (c q) -> p c q", c=4)).then_inc(copied, 1)

        @block.tensor
        def _(pe):
            for n, (t, half) in enumerate(groups):
                pe.wait_ge(h_ready, t + 1)
                for c in range(4):
                    last = pe.transpose(psum[:, n, c * P:(c + 1) * P],
                                        h[:, t, (4 * half + c) * P:(4 * half + c + 1) * P], k["ident"][:])
                last.then_inc(turned, 1)


def turn(nc, k, name, z, blocks, out_t):
    with Stage(nc, name) as st:
        banks = 6
        psum = st.ps("psum", [P, banks, CW])
        turned, copied = st.sem("turned"), st.sem("copied")
        moved = st.sem("moved")
        pairs = [blocks[i:i + 2] for i in range(0, len(blocks), 2)]
        block = st.block()

        def bank_free(pe, n):
            if n >= banks:
                prior = n - banks
                pe.wait_ge(copied if prior % 2 == 0 else moved, prior // 2 + 1)

        def source(n):
            w = len(pairs[n])
            return (out_t[:, 2 * n:2 * n + w, :],
                    psum[:, n % banks, 0:w * S].rearrange("p (b q) -> p b q", b=w))

        @block.tensor
        def _(pe):
            for n, pair in enumerate(pairs):
                bank_free(pe, n)
                for b, col in enumerate(pair):
                    for t in range(TT):
                        last = pe.transpose(psum[:, n % banks, b * S + t * P:b * S + (t + 1) * P],
                                            z[:, t, col:col + P], k["ident"][:])
                last.then_inc(turned, 1)

        @block.vector
        def _(dve):
            for n in range(0, len(pairs), 2):
                dve.wait_ge(turned, n + 1)
                dve.tensor_copy(*source(n)).then_inc(copied, 1)

        @block.scalar
        def _(act):
            for n in range(1, len(pairs), 2):
                act.wait_ge(turned, n + 1)
                act.copy(*source(n)).then_inc(moved, 1)


def project(nc, k, name, h_t, chunks, residual=None, out=None, ada=None):
    with Stage(nc, name) as st:
        beside = Modulation(nc, k, st, ada[0], None, ada[1], first=ada[2]) if ada else None
        halves = list(range(ada[2], ada[3])) if ada else []
        ring = 3
        w = st.sb("w", [P, ring, KT * CW])
        tmp = st.sb("tmp", [P, 2, CW])
        psum = st.ps("psum", [P, 4, CW])
        slot_loaded = [st.sem(f"slot_loaded{i}") for i in range(ring)]
        product, taken, scaled, moved = (st.sem(n) for n in ("product", "taken", "scaled", "moved"))
        jobs = [(j, t) for j in range(len(chunks)) for t in range(TT)]
        block = st.block()

        def halves_at(j, of):
            return range(j * len(halves) // of, (j + 1) * len(halves) // of)

        @block.sync
        def _(sp):
            for j, (source, col, width) in enumerate(chunks):
                if j >= ring:
                    sp.wait_ge(product, TT * (j - ring + 1))
                sp.dma_start(w[:, j % ring, 0:KT * width], source).then_inc(slot_loaded[j % ring], 16)
                for n in halves_at(j, len(chunks)):
                    beside.load(sp, halves[n], n % 2, early=(n < 2))

        @block.tensor
        def _(pe):
            for n, (j, t) in enumerate(jobs):
                width = chunks[j][2]
                pe.wait_ge(slot_loaded[j % ring], 16 * (j // ring + 1))
                if n >= 4 and residual is not None:
                    pe.wait_ge(scaled, n - 3)
                if n >= 4 and residual is None:
                    pe.wait_ge(taken if n % 2 == 0 else moved, n // 2 - 1)
                for c in range(KT):
                    last = pe.matmul(psum[:, n % 4, 0:width], h_t[:, c, t * P:(t + 1) * P],
                                     w[:, j % ring, c * width:(c + 1) * width],
                                     start=(c == 0), stop=(c == KT - 1))
                last.then_inc(product, 1)

        @block.vector
        def _(dve):
            steps = 0
            for n, (j, t) in enumerate(jobs):
                for m in halves_at(n, len(jobs)):
                    steps += beside.fold(dve, halves[m], m % 2, steps, m // 2)
                col, width = chunks[j][1:]
                if residual is None:
                    if n % 2 == 0:
                        dve.wait_ge(product, n + 1)
                        dve.tensor_copy(out[:, t, col:col + width], psum[:, n % 4, 0:width]).then_inc(taken, 1)
                    continue
                x, gate = residual
                dve.wait_ge(product, n + 1)
                if n >= 2:
                    dve.wait_ge(taken, n - 1)
                dve.tensor_tensor(tmp[:, n % 2, 0:width], psum[:, n % 4, 0:width], gate[:, col:col + width],
                                  ALU.mult).then_inc(scaled, 1)
                dve.wait_ge(scaled, n + 1)
                dve.tensor_tensor(x[:, t, col:col + width], x[:, t, col:col + width], tmp[:, n % 2, 0:width],
                                  ALU.add).then_inc(taken, 1)

        @block.scalar
        def _(act):
            for n, (j, t) in enumerate(jobs):
                col, width = chunks[j][1:]
                if residual is None and n % 2 == 1:
                    act.wait_ge(product, n + 1)
                    act.copy(out[:, t, col:col + width], psum[:, n % 4, 0:width]).then_inc(moved, 1)


def head_norm_rope(nc, k, name, z, segments):
    with Stage(nc, name) as st:
        total = sum(n for _, n, _ in segments)
        most = max(n for _, n, _ in segments)
        sq = st.sb("sq", [P, TT, most, HEAD])
        ss = st.sb("ss", [P, TT, total])
        gains = st.sb("gains", [P, len(segments), HEAD])
        rot = [st.sb(f"rot{i}", [P, TT, most, HALF]) for i in range(4)]
        loaded, mean_ready, root_ready, dve_done = (
            st.sem(n) for n in ("loaded", "mean_ready", "root_ready", "dve_done"))
        block = st.block()

        @block.sync
        def _(sp):
            for s, (_, _, gain) in enumerate(segments):
                sp.dma_start(gains[:, s, :], gain.partition_broadcast(P)).then_inc(loaded, 16)

        @block.scalar
        def _(act):
            act.wait_ge(mean_ready, 1)
            act.activation(ss[:], ss[:], ACT.Sqrt).then_inc(root_ready, 1)

        @block.vector
        def _(dve):
            step = InOrder(dve, dve_done)

            def heads(s):
                col, n, _ = segments[s]
                return z[:, :, col:col + n * HEAD].rearrange("p t (n d) -> p t n d", d=HEAD)

            at = 0
            for s, (_, n, _) in enumerate(segments):
                step(dve.tensor_tensor(sq[:, :, 0:n, :], heads(s), heads(s), ALU.mult))
                step(dve.tensor_reduce(ss[:, :, at:at + n], sq[:, :, 0:n, :], AX.X, ALU.add))
                at += n
            dve.tensor_scalar(ss[:], ss[:], 1.0 / HEAD, EPS, ALU.mult, ALU.add).then_inc(mean_ready, 1)
            dve.wait_ge(loaded, 16 * len(segments))
            dve.wait_ge(root_ready, 1)
            step(dve.reciprocal(ss[:], ss[:]))
            at = 0
            for s, (_, n, _) in enumerate(segments):
                v = heads(s)
                rs = ss[:, :, at:at + n].unsqueeze(3).broadcast_to([P, TT, n, HEAD])
                at += n
                step(dve.tensor_tensor(v, v, rs, ALU.mult))
                for t in range(TT):
                    g = gains[:, s, :].unsqueeze(1).broadcast_to([P, n, HEAD])
                    step(dve.tensor_tensor(v[:, t], v[:, t], g, ALU.mult))
                t1, t2 = v[:, :, :, 0:HALF], v[:, :, :, HALF:ROT]
                cos = k["cos"][:].unsqueeze(2).broadcast_to([P, TT, n, HALF])
                sin = k["sin"][:].unsqueeze(2).broadcast_to([P, TT, n, HALF])
                for r, (a, b) in enumerate(((t1, cos), (t2, sin), (t2, cos), (t1, sin))):
                    step(dve.tensor_tensor(rot[r][:, :, 0:n, :], a, b, ALU.mult))
                step(dve.tensor_tensor(t1, rot[0][:, :, 0:n, :], rot[1][:, :, 0:n, :], ALU.subtract))
                step(dve.tensor_tensor(t2, rot[2][:, :, 0:n, :], rot[3][:, :, 0:n, :], ALU.add))


def compress(nc, k, ins, z, q_t, pc_t, vc, gates):
    G = 2
    N = G * NCMP
    with Stage(nc, "cmp") as st:
        w1 = st.sb("w1", [HEAD, CMP_LEN, CMP_HIDDEN])
        w2 = st.sb("w2", [P, 2, 2, HEAD])
        pos_t = st.sb("pos_t", [HEAD, 2, CMP_LEN])
        tok_t = st.sb("tok_t", [HEAD, 2, G, S])
        blk = st.sb("blk", [HEAD, 2, CMP_LEN, N])
        hid = st.sb("hid", [P, 2, 2, N])
        kc_t = st.sb("kc_t", [P, G, NCMP])
        sc = st.sb("sc", [P, TT, HEADS, NCMP])
        mx = st.sb("mx", [P, TT, HEADS])
        sm = st.sb("sm", [P, TT, HEADS])
        pt = [st.ps(f"pt{i}", [P, CW]) for i in range(2)]
        ph = st.ps("ph", [P, 2, CW])
        pk = st.ps("pk", [P, CW])
        pv = st.ps("pv", [P, CW])
        psc = st.ps("psc", [P, CW])
        loaded, w1_loaded, turned, tok_ready, blk_ready, hid_sum, hid_ready, small, kv_ready, scored, \
            shifted, exped, gate_e, p_ready, p_turned, p_half, dve_done = (st.sem(n) for n in (
                "loaded", "w1_loaded", "turned", "tok_ready", "blk_ready", "hid_sum", "hid_ready", "small",
                "kv_ready", "scored", "shifted", "exped", "gate_e", "p_ready", "p_turned", "p_half", "dve_done"))
        block = st.block()

        @block.sync
        def _(sp):
            sp.dma_start(pos_t[:], ins["cmp_pos"]).then_inc(loaded, 16)
            sp.dma_start(w2[:], ins["cmp_w2"]).then_inc(loaded, 16)
            for kv in range(2):
                if kv:
                    sp.wait_ge(hid_sum, 1)
                sp.dma_start(w1[:], ins["cmp_w1"][kv]).then_inc(w1_loaded, 16)

        @block.tensor
        def _(pe):
            for kv in range(2):
                for g in range(G):
                    for t in range(TT):
                        col = Z_KV + kv * KV_VALUE + g * HEAD
                        last = pe.transpose(pt[kv][0:HEAD, g * S + t * P:g * S + (t + 1) * P],
                                            z[:, t, col:col + HEAD], k["ident"][:])
                last.then_inc(turned, 1)
            pe.wait_ge(blk_ready, 2 * G)
            for kv in range(2):
                pe.wait_ge(w1_loaded, 16 * (kv + 1))
                for e in range(2):
                    for l in range(CMP_LEN):
                        last = pe.matmul(ph[:, kv, e * N:(e + 1) * N], w1[:, l, e * P:(e + 1) * P],
                                         blk[:, kv, l, :], start=(l == 0), stop=(l == CMP_LEN - 1))
                last.then_inc(hid_sum, 1)
            pe.wait_ge(hid_ready, 2)
            pe.wait_ge(loaded, 32)
            for g in range(G):
                for e in range(2):
                    pe.matmul(pk[g * HEAD:(g + 1) * HEAD, 0:NCMP], w2[:, 0, e, :],
                              hid[:, 0, e, g * NCMP:(g + 1) * NCMP], start=(e == 0), stop=(e == 1))
            for g in range(G):
                for e in range(2):
                    last = pe.matmul(pv[0:NCMP, g * HEAD:(g + 1) * HEAD], hid[:, 1, e, g * NCMP:(g + 1) * NCMP],
                                     w2[:, 1, e, :], start=(e == 0), stop=(e == 1))
            last.then_inc(small, 1)
            pe.wait_ge(kv_ready, G + 1)
            for t in range(TT):
                for b in range(HEADS // G):
                    at = (t * HEADS + b * G) * NCMP
                    last = pe.matmul(psc[:, at:at + N], q_t[:, b, t * P:(t + 1) * P],
                                     kc_t[:].rearrange("p g n -> p (g n)"), start=True, stop=True)
            last.then_inc(scored, 1)
            pe.wait_ge(p_ready, 1)
            for quarter in range(4):
                if quarter >= 2:
                    pe.wait_ge(p_half, quarter - 1)
                for h in (2 * quarter, 2 * quarter + 1):
                    for t in range(TT):
                        last = pe.transpose(pt[quarter % 2][0:NCMP, (h % 2) * S + t * P:(h % 2) * S + (t + 1) * P],
                                            sc[:, t, h, :], k["ident"][:])
                last.then_inc(p_turned, 1)

        @block.scalar
        def _(act):
            act.activation(gates[:], z[:, :, Z_GATE:Z_GATE + 3 * HEADS], ACT.Exp, scale=-1.0).then_inc(gate_e, 1)
            act.wait_ge(hid_sum, 2)
            for kv in range(2):
                act.activation(hid[:, kv].rearrange("p e n -> p (e n)"), ph[:, kv, 0:2 * N],
                               ACT.Silu).then_inc(hid_ready, 1)
            act.wait_ge(shifted, 1)
            act.activation(sc[:], sc[:], ACT.Exp).then_inc(exped, 1)

        @block.vector
        def _(dve):
            step = InOrder(dve, dve_done)
            dve.wait_ge(gate_e, 1)
            step(dve.tensor_scalar(gates[:], gates[:], 1.0, None, ALU.add))
            step(dve.memset(kc_t[:], 0.0))
            step(dve.reciprocal(gates[:], gates[:]))
            dve.wait_ge(loaded, 32)
            for kv in range(2):
                dve.wait_ge(turned, kv + 1)
                step(dve.tensor_copy(tok_t[:, kv].rearrange("d g s -> d (g s)"), pt[kv][0:HEAD, :]))
                for g in range(G):
                    for n in range(NCMP):
                        last = dve.tensor_tensor(blk[:, kv, :, g * NCMP + n],
                                                 tok_t[:, kv, g, n * CMP_STRIDE:n * CMP_STRIDE + CMP_LEN],
                                                 pos_t[:, kv, :], ALU.add)
                    last.then_inc(blk_ready, 1)
            dve.wait_ge(small, 1)
            for g in range(G):
                rows = slice(g * HEAD, (g + 1) * HEAD)
                dve.tensor_copy(kc_t[rows, g, :], pk[rows, 0:NCMP]).then_inc(kv_ready, 1)
            dve.tensor_copy(vc[:].rearrange("n g d -> n (g d)"), pv[0:NCMP, 0:G * HEAD]).then_inc(kv_ready, 1)
            dve.wait_ge(scored, 1)
            for t in range(TT):
                step(dve.scalar_tensor_tensor(
                    sc[:, t], psc[:, t * HEADS * NCMP:(t + 1) * HEADS * NCMP].rearrange("p (h n) -> p h n", h=HEADS),
                    HEAD ** -0.5, k["cmp_mask"][:, t, :].unsqueeze(1).broadcast_to([P, HEADS, NCMP]),
                    ALU.mult, ALU.add))
            wide = [P, TT, HEADS, NCMP]
            step(dve.tensor_reduce(mx[:], sc[:], AX.X, ALU.max))
            dve.tensor_tensor(sc[:], sc[:], mx[:].unsqueeze(3).broadcast_to(wide), ALU.subtract).then_inc(shifted, 1)
            dve.wait_ge(exped, 1)
            step(dve.tensor_reduce(sm[:], sc[:], AX.X, ALU.add))
            step(dve.reciprocal(sm[:], sm[:]))
            step(dve.tensor_tensor(sm[:], sm[:], gates[:, :, 0:HEADS], ALU.mult))
            step(dve.tensor_tensor(sc[:], sc[:], k["cmp_valid"][:].unsqueeze(2).broadcast_to(wide), ALU.mult))
            dve.tensor_tensor(sc[:], sc[:], sm[:].unsqueeze(3).broadcast_to(wide), ALU.mult).then_inc(p_ready, 1)
            for quarter in range(4):
                dve.wait_ge(p_turned, quarter + 1)
                dve.tensor_copy(pc_t[:, 2 * quarter:2 * quarter + 2, :].rearrange("n h s -> n (h s)"),
                                pt[quarter % 2][0:NCMP, :]).then_inc(p_half, 1)


def sparse_attention(nc, k, z, zt, pc_t, vc, gates, o_t):
    maps = []
    for h in range(HEADS):
        maps.append((h // 2, 4 + h // 2, h % 2, Z_MV + h * HEAD, None, h // 2, "only"))
    for h in range(HEADS):
        for br, part in ((1, "first"), (2, "last")):
            maps.append((8 + h // 2, 12 + br, h % 2, Z_KV + br * KV_BRANCH + KV_VALUE + (h % 2) * HEAD,
                         (br, h), 4 + h // 2, part))
    n_maps = len(maps)
    with Stage(nc, "attn") as st:
        sc = st.sb("sc", [P, 2, SC])
        pt = st.sb("pt", [P, 2, SC])
        nm = st.sb("nm", [P, 2, TT])
        sm = st.sb("sm", [P, 2, TT])
        ps = st.ps("ps", [P, 2, CW])
        pp = st.ps("pp", [P, 2, CW])
        po = st.ps("po", [P, 2, CW])
        scored, masked, neg_max, exped, probs, turned, pt_ready, attended, stored, dve_done = (
            st.sem(n) for n in ("scored", "masked", "neg_max", "exped", "probs", "turned", "pt_ready",
                                "attended", "stored", "dve_done"))
        block = st.block()
        parts = ((0, P), (P, SC))

        @block.tensor
        def _(pe):
            def scores(i):
                q, key, half, *_ = maps[i]
                rows = slice(half * HEAD, (half + 1) * HEAD)
                if i >= 2:
                    pe.wait_ge(masked, i - 1)
                for t, (lo, hi) in enumerate(parts):
                    last = pe.matmul(ps[:, i % 2, lo:hi], zt[rows, q, t * P:(t + 1) * P],
                                     zt[rows, key, 0:hi - lo], start=True, stop=True)
                last.then_inc(scored, 1)

            def turn_probs(i):
                pe.wait_ge(probs, i + 1)
                if i >= 2:
                    pe.wait_ge(pt_ready, i - 1)
                for c in range(3):
                    last = pe.transpose(pp[:, i % 2, c * P:(c + 1) * P], sc[:, i % 2, c * P:(c + 1) * P],
                                        k["ident"][:])
                last.then_inc(turned, 1)

            def values(i):
                _, _, half, vcol, gate, dest, part = maps[i]
                rows = slice(half * HEAD, (half + 1) * HEAD)
                pe.wait_ge(pt_ready, i + 1)
                if dest >= 2 and half == 0 and part != "last":
                    pe.wait_ge(stored, dest - 1)
                o = po[rows, dest % 2, :]
                first = part != "last"
                pe.matmul(o[:, 0:S], z[:, 0, vcol:vcol + HEAD], pt[:, i % 2, 0:S], start=first, stop=False)
                last = pe.matmul(o[:, P:S], z[:, 1, vcol:vcol + HEAD], pt[:, i % 2, S:SC], start=False,
                                 stop=(part == "only"))
                if part == "last":
                    last = pe.matmul(o[:, 0:S], vc[:, half, :], pc_t[:, gate[1], :], start=False, stop=True)
                last.then_inc(attended, 1)

            for i in range(n_maps + 2):
                if i < n_maps:
                    scores(i)
                if 1 <= i <= n_maps:
                    turn_probs(i - 1)
                if i >= 2:
                    values(i - 2)

        ends = [i for i, m in enumerate(maps) if m[2] == 1 and m[6] != "first"]

        @block.vector
        def _(dve):
            step = InOrder(dve, dve_done)

            def mask(i):
                dve.wait_ge(scored, i + 1)
                if i >= 2:
                    dve.wait_ge(turned, i - 1)
                s = sc[:, i % 2, :]
                dve.scalar_tensor_tensor(s, ps[:, i % 2, 0:SC], HEAD ** -0.5, k["causal"][:], ALU.mult,
                                         ALU.add).then_inc(masked, 1)
                dve.wait_ge(masked, i + 1)
                for t, (lo, hi) in enumerate(parts):
                    dve.tensor_reduce(nm[:, i % 2, t:t + 1], s[:, lo:hi], AX.X, ALU.max,
                                      negate=True).then_inc(neg_max, 1)

            def scale(i):
                dve.wait_ge(exped, 2 * i + 2)
                r = sm[:, i % 2, :]
                step(dve.reciprocal(r, r))
                if maps[i][4]:
                    br, h = maps[i][4]
                    step(dve.tensor_tensor(r, r, gates[:, :, br * HEADS + h], ALU.mult))
                for t, (lo, hi) in enumerate(parts):
                    last = dve.tensor_scalar(sc[:, i % 2, lo:hi], sc[:, i % 2, lo:hi], sm[:, i % 2, t:t + 1], None,
                                             ALU.mult)
                last.then_inc(probs, 1)

            for i in range(n_maps + 1):
                if i < n_maps:
                    mask(i)
                if i >= 1:
                    scale(i - 1)

        @block.scalar
        def _(act):
            def exp(i):
                for t, (lo, hi) in enumerate(parts):
                    act.wait_ge(neg_max, 2 * i + t + 1)
                    act.activation(sc[:, i % 2, lo:hi], sc[:, i % 2, lo:hi], ACT.Exp, bias=nm[:, i % 2, t:t + 1],
                                   accum_out=sm[:, i % 2, t:t + 1]).then_inc(exped, 1)

            def move_probs(i):
                act.wait_ge(turned, i + 1)
                if i >= 2:
                    act.wait_ge(attended, i - 1)
                act.copy(pt[:, i % 2, :], pp[:, i % 2, 0:SC]).then_inc(pt_ready, 1)

            def store(i):
                if i in ends:
                    n = ends.index(i)
                    act.wait_ge(attended, i + 1)
                    act.copy(o_t[:, n, :], po[:, n % 2, 0:S]).then_inc(stored, 1)

            for i in range(n_maps + 2):
                if i < n_maps:
                    exp(i)
                if 1 <= i <= n_maps:
                    move_probs(i - 1)
                if i >= 2:
                    store(i - 2)


def streamed_mlp(nc, k, name, columns, rows, kind, h_split, residual=None, kept=None, table=None, ada=None,
                 then=None):
    n_tiles, _, first = columns.shape
    halves = first // D
    lead = 3
    pairs = n_tiles // 2
    h_hi, h_lo = h_split
    with Stage(nc, name) as st:
        u = st.sb("u", [P, 2, first])
        u_hi, u_lo = (st.sb(n, [P, 2, first], F32R) for n in ("u_hi", "u_lo"))
        v = st.sb("v", [P, 2, D])
        v_hi, v_lo = (st.sb(n, [P, 2, D], F32R) for n in ("v_hi", "v_lo"))
        act_out = st.sb("act_out", [P, 2, S])
        coef = st.sb("coef", [P, S])
        c_hi, c_lo = (st.sb(n, [P, 2, S], F32R) for n in ("c_hi", "c_lo"))
        pa = st.ps("pa", [P, 2, CW])
        py = st.ps("py", [P, TT * 2, CW])
        u_loaded = [st.sem(f"u_loaded{i}") for i in range(2)]
        v_loaded = [st.sem(f"v_loaded{i}") for i in range(2)]
        u_hi_ready, u_split, v_hi_ready, v_split, rows_ready, acted, weighed, rounded, coef_ready, down_done, \
            kept_loaded, scaled, summed = (st.sem(n) for n in (
                "u_hi_ready", "u_split", "v_hi_ready", "v_split", "rows_ready", "acted", "weighed", "rounded",
                "coef_ready", "down_done", "kept_loaded", "scaled", "summed"))
        beside = Modulation(nc, k, st, ada[0], None, ada[1]) if ada else None
        x, gate = residual or (u[:], v[:, 0, :])
        tmp = v[:, 1, :].rearrange("p (a n) -> p a n", a=2)

        def halves_at(i):
            return range(i * 8 // 6, (i + 1) * 8 // 6)

        block = st.block()

        @block.sync
        def _(sp):
            def load(i, b, early=False):
                at = (lambda m: m[i]) if isinstance(i, int) else \
                    (lambda m: m[bass.ds(i, 1)].rearrange("a p n -> p (a n)"))
                if not early:
                    sp.wait_ge(u_split, i - 1)
                sp.dma_start(u[:, b, :], at(columns)).then_inc(u_loaded[b], 16)
                if not early:
                    sp.wait_ge(v_split, i - 1)
                sp.dma_start(v[:, b, :], at(rows)).then_inc(v_loaded[b], 16)

            for i in range(2 * lead):
                load(i, i % 2, early=(i < 2))
                if ada:
                    for half in halves_at(i):
                        beside.load(sp, half, half % 2, early=(half < 2))
            with sp.Fori(lead, pairs) as r:
                for b in range(2):
                    load(2 * r + b, b)
                    if ada:
                        beside.load(sp, 2 * r + (b + 2), b)
            if kept:
                sp.wait_ge(u_split, n_tiles)
                sp.dma_start(x, kept[0]).then_inc(kept_loaded, 16)
                sp.wait_ge(v_split, n_tiles)
                sp.dma_start(gate, kept[1]).then_inc(kept_loaded, 16)

        @block.tensor
        def _(pe):
            def up(i, b, early=False):
                pe.wait_ge(u_split, i + 1)
                if not early:
                    pe.wait_ge(coef_ready, i - 1)
                for half in range(halves):
                    for c in range(KT):
                        cols = slice(half * D + c * P, half * D + (c + 1) * P)
                        out = pa[:, b, half * S:(half + 1) * S]
                        pe.matmul(out, u_hi[:, b, cols], h_hi[:, c, :], start=(c == 0), stop=False)
                        pe.matmul(out, u_hi[:, b, cols], h_lo[:, c, :], start=False, stop=False)
                        last = pe.matmul(out, u_lo[:, b, cols], h_hi[:, c, :], start=False, stop=(c == KT - 1))
                last.then_inc(rows_ready, 1)

            def down(i, b, start=False, stop=False):
                pe.wait_ge(coef_ready, i + 1)
                pe.wait_ge(v_split, i + 1)
                for t in range(TT):
                    part = slice(t * P, (t + 1) * P)
                    for n in range(2):
                        cols = slice(n * CW, (n + 1) * CW)
                        pe.matmul(py[:, 2 * t + n, :], c_hi[:, b, part], v_hi[:, b, cols], start=start, stop=False)
                        pe.matmul(py[:, 2 * t + n, :], c_hi[:, b, part], v_lo[:, b, cols], start=False, stop=False)
                    for n in range(2):
                        cols = slice(n * CW, (n + 1) * CW)
                        last = pe.matmul(py[:, 2 * t + n, :], c_lo[:, b, part], v_hi[:, b, cols], start=False,
                                         stop=stop)
                last.then_inc(down_done, 1)

            up(0, 0, early=True)
            up(1, 1, early=True)
            down(0, 0, start=True)
            for i in range(2, 2 * lead):
                up(i, i % 2)
                down(i - 1, (i - 1) % 2)
            with pe.Fori(lead, pairs) as r:
                for b in range(2):
                    up(2 * r + b, b)
                    down(2 * r + (b - 1), 1 - b)
            down(n_tiles - 1, 1, stop=True)

        @block.scalar
        def _(act):
            func = ACT.Silu if kind == "swiglu" else ACT.Gelu

            def high_u(i, b, rnd, early=False):
                act.wait_ge(u_loaded[b], 16 * rnd + 16)
                if not early:
                    act.wait_ge(rows_ready, i - 1)
                act.copy(u_hi[:, b, :], u[:, b, :]).then_inc(u_hi_ready, 1)

            def high_v(i, b, rnd, early=False):
                act.wait_ge(v_loaded[b], 16 * rnd + 16)
                if not early:
                    act.wait_ge(down_done, i - 1)
                act.copy(v_hi[:, b, :], v[:, b, :]).then_inc(v_hi_ready, 1)

            def gate_tile(i, b, early=False):
                act.wait_ge(rows_ready, i + 1)
                if not early:
                    act.wait_ge(coef_ready, i - 1)
                act.activation(act_out[:, b, :], pa[:, b, 0:S], func).then_inc(acted, 1)

            high_u(0, 0, 0, early=True)
            high_v(0, 0, 0, early=True)
            for i in range(2 * lead):
                high_u(i + 1, (i + 1) % 2, (i + 1) // 2, early=(i < 1))
                gate_tile(i, i % 2, early=(i < 2))
                high_v(i + 1, (i + 1) % 2, (i + 1) // 2, early=(i < 1))
            with act.Fori(lead, pairs - 1) as r:
                for b in range(2):
                    high_u(2 * r + (b + 1), 1 - b, r + b)
                    gate_tile(2 * r + b, b)
                    high_v(2 * r + (b + 1), 1 - b, r + b)
            high_u(n_tiles - 1, 1, pairs - 1)
            gate_tile(n_tiles - 2, 0)
            high_v(n_tiles - 1, 1, pairs - 1)
            gate_tile(n_tiles - 1, 1)

        @block.vector
        def _(dve):
            def low_u(i, b):
                dve.wait_ge(u_hi_ready, i + 1)
                dve.tensor_tensor(u_lo[:, b, :], u[:, b, :], u_hi[:, b, :].bitcast(F32), ALU.subtract
                                  ).then_inc(u_split, 1)

            def low_v(i, b):
                dve.wait_ge(v_hi_ready, i + 1)
                dve.tensor_tensor(v_lo[:, b, :], v[:, b, :], v_hi[:, b, :].bitcast(F32), ALU.subtract
                                  ).then_inc(v_split, 1)

            def weigh(i, b, early=False):
                dve.wait_ge(acted, i + 1)
                if kind == "swiglu":
                    other = pa[:, b, S:2 * S]
                elif isinstance(i, int):
                    other = table[:, i, :]
                else:
                    other = table[:, bass.ds(i, 1), :].rearrange("p a s -> p (a s)")
                dve.tensor_tensor(coef[:], act_out[:, b, :], other, ALU.mult).then_inc(weighed, 1)
                dve.wait_ge(weighed, i + 1)
                if not early:
                    dve.wait_ge(down_done, i - 1)
                dve.tensor_copy(c_hi[:, b, :], coef[:]).then_inc(rounded, 1)
                dve.wait_ge(rounded, i + 1)
                dve.tensor_tensor(c_lo[:, b, :], coef[:], c_hi[:, b, :].bitcast(F32), ALU.subtract
                                  ).then_inc(coef_ready, 1)
                dve.wait_ge(coef_ready, i + 1)

            low_u(0, 0)
            low_v(0, 0)
            steps = 0
            for i in range(2 * lead):
                low_u(i + 1, (i + 1) % 2)
                weigh(i, i % 2, early=(i < 2))
                low_v(i + 1, (i + 1) % 2)
                if ada:
                    for half in halves_at(i):
                        steps += beside.fold(dve, half, half % 2, steps, half // 2)
            with dve.Fori(lead, pairs - 1) as r:
                for b in range(2):
                    low_u(2 * r + (b + 1), 1 - b)
                    weigh(2 * r + b, b)
                    low_v(2 * r + (b + 1), 1 - b)
                    if ada:
                        beside.fold(dve, 2 * r + (b + 2), b, steps + (2 * r + (b - 2 * lead)) * KT, r + 1)
            for i in (n_tiles - 2, n_tiles - 1):
                if i < n_tiles - 1:
                    low_u(i + 1, 1)
                weigh(i, i % 2)
                if i < n_tiles - 1:
                    low_v(i + 1, 1)
                if ada:
                    beside.fold(dve, i + 2, i % 2, steps + (i - 2 * lead) * KT, i // 2 + 1)
            dve.wait_ge(down_done, n_tiles)
            if kept:
                dve.wait_ge(kept_loaded, 32)
            for n in range(2 * TT):
                t, c = n // 2, (n % 2) * CW
                if n >= 2:
                    dve.wait_ge(summed, n - 1)
                dve.tensor_tensor(tmp[:, n % 2, :], py[:, n, :], gate[:, c:c + CW], ALU.mult).then_inc(scaled, 1)
                dve.wait_ge(scaled, n + 1)
                dve.tensor_tensor(x[:, t, c:c + CW], x[:, t, c:c + CW], tmp[:, n % 2, :], ALU.add).then_inc(summed, 1)
        if then:
            st.end_block()
            then(x, v)


def split_h(nc, name, h_t, hi, lo):
    with Stage(nc, name) as st:
        rounded, split = st.sem("rounded"), st.sem("split")
        block = st.block()

        @block.vector
        def _(dve):
            for c in range(0, KT, 2):
                dve.tensor_copy(hi[:, c:c + 2, :], h_t[:, c:c + 2, :]).then_inc(rounded, 1)
            for c in range(0, KT, 2):
                dve.wait_ge(rounded, c // 2 + 1)
                dve.tensor_tensor(lo[:, c:c + 2, :], h_t[:, c:c + 2, :], hi[:, c:c + 2, :].bitcast(F32), ALU.subtract
                                  ).then_inc(split, 1)
            dve.wait_ge(split, KT // 2)


def chunked(source, width, first=0):
    return [(source[j], first + j * CW, CW) for j in range(width // CW)]


def sparse_layer(nc, k, ins, mod, next_mod):
    x = k["x"]
    c = k["silu_c"][:, 0, :]
    with Stage(nc, "l0") as st:
        first_modulation(nc, k, "ada0", (ins["ada_w0"], ins["ada_b0"]), c, mod, 8)
        m = [mod[:, i * D:(i + 1) * D] for i in range(6)]
        with Stage(nc, "l0a") as sa:
            o_t = sa.sb("o_t", [P, KT, S])
            with Stage(nc, "l0b") as sb:
                z = sb.sb("z", [P, TT, SP_IN])
                h_t = sb.sb("h_t", [P, KT, S])
                normed(nc, k, "norm0", x, ins["attn_norm0"], m[0], m[1], h_t)
                tail = SP_IN - 5 * CW
                project(nc, k, "proj0", h_t, chunked(ins["sp_w_in"], 5 * CW) + [(ins["sp_w_in_tail"], 5 * CW, tail)],
                        out=z, ada=(ins["ada_w0"], [(c, mod, 12)], 8, 24))
                finish_modulation(nc, k, "ada0b", ins["ada_b0"], [(mod, 4, 12)])
                segs = [(Z_MQ, 8, ins["moba_q_norm"]), (Z_MK, 8, ins["moba_k_norm"]), (Z_NQ, 8, ins["nsa_q_norm"])]
                segs += [(Z_KV + br * KV_BRANCH, 2, ins["nsa_k_norm"][br]) for br in range(3)]
                head_norm_rope(nc, k, "rope0", z, segs)
                zt = sb.sb("zt", [P, 15, S])
                blocks = [Z_MQ + i * P for i in range(4)] + [Z_MK + i * P for i in range(4)]
                blocks += [Z_NQ + i * P for i in range(4)] + [Z_KV + br * KV_BRANCH for br in range(3)]
                turn(nc, k, "turn0", z, blocks, zt)
                pc_t = sb.sb("pc_t", [NCMP, HEADS, S])
                vc = sb.sb("vc", [NCMP, 2, HEAD])
                gates = sb.sb("gates", [P, TT, 3 * HEADS])
                compress(nc, k, ins, z, zt[:, 8:12, :], pc_t, vc, gates)
                sparse_attention(nc, k, z, zt, pc_t, vc, gates, o_t)
            project(nc, k, "out0", o_t, chunked(ins["sp_w_out"], D), residual=(x, m[2]))
        feed_forward(nc, k, ins, 0, m, (ins["ada_w1"], [(c, next_mod, 12)]))
        finish_modulation(nc, k, "ada1b", ins["ada_b1"], [(next_mod, 0, 12)])


def feed_forward(nc, k, ins, layer, m, ada):
    hi, lo = k["h_hi"], k["h_lo"]
    with Stage(nc, f"ffh{layer}") as sh:
        h_t = sh.sb("h_t", [P, KT, S])
        normed(nc, k, f"fnorm{layer}", k["x"], ins[f"ffn_norm{layer}"], m[3], m[4], h_t)
        split_h(nc, f"fsplit{layer}", h_t, hi, lo)
    streamed_mlp(nc, k, f"ffn{layer}", ins[f"ffn_columns{layer}"], ins[f"ffn_rows{layer}"], "swiglu", (hi, lo),
                 residual=(k["x"][:], m[5]), ada=ada)


def head_norm(nc, k, name, o, gain, factor, gate=None):
    with Stage(nc, name) as st:
        sq = st.sb("sq", [P, TT, D])
        ss = st.sb("ss", [P, TT, HEADS])
        g = st.sb("g", [P, P])
        loaded, gated, mean_ready, root_ready, dve_done = (
            st.sem(n) for n in ("loaded", "gated", "mean_ready", "root_ready", "dve_done"))
        block = st.block()

        def by_head(v):
            return v.rearrange("p t (h d) -> p t h d", h=HEADS)

        @block.sync
        def _(sp):
            sp.dma_start(g[:], gain.partition_broadcast(P)).then_inc(loaded, 16)

        @block.scalar
        def _(act):
            if gate is not None:
                act.activation(gate, gate, ACT.Silu).then_inc(gated, 1)
            act.wait_ge(mean_ready, 1)
            act.activation(ss[:], ss[:], ACT.Sqrt).then_inc(root_ready, 1)

        @block.vector
        def _(dve):
            step = InOrder(dve, dve_done)
            step(dve.tensor_tensor(sq[:], o, o, ALU.mult))
            step(dve.tensor_reduce(ss[:], by_head(sq[:]), AX.X, ALU.add))
            dve.tensor_scalar(ss[:], ss[:], 1.0 / P, EPS, ALU.mult, ALU.add).then_inc(mean_ready, 1)
            dve.wait_ge(loaded, 16)
            step(dve.tensor_scalar(g[:], g[:], factor, None, ALU.mult))
            for t in range(TT):
                v = o[:, t, :].rearrange("p (h d) -> p h d", h=HEADS)
                step(dve.tensor_tensor(v, v, g[:].unsqueeze(1).broadcast_to([P, HEADS, P]), ALU.mult))
            if gate is not None:
                dve.wait_ge(gated, 1)
                step(dve.tensor_tensor(o, o, gate, ALU.mult))
            dve.wait_ge(root_ready, 1)
            step(dve.reciprocal(ss[:], ss[:]))
            step(dve.tensor_tensor(by_head(o), by_head(o), ss[:].unsqueeze(3).broadcast_to([P, TT, HEADS, P]),
                                   ALU.mult))


def diff_attention(nc, k, ins, z, zt, o):
    parts = ((0, P), (P, SC))
    with Stage(nc, "diff") as st:
        lp = st.sb("lp", [P, 4, HEAD])
        lam = st.sb("lam", [P, 2])
        neg_lam = st.sb("neg_lam", [P, 1])
        sc = st.sb("sc", [P, 2, 2, SC])
        pt = st.sb("pt", [P, 2, SC])
        nm = st.sb("nm", [P, 2, TT, 2])
        sm = st.sb("sm", [P, 2, TT, 2])
        ps = st.ps("ps", [P, 2, 2, CW])
        pp = st.ps("pp", [P, 2, CW])
        po = st.ps("po", [P, 2, CW])
        loaded, lam_sum, lam_exp, scored, masked, neg_max, exped, probs, turned, pt_ready, attended, stored, \
            dve_done = (st.sem(n) for n in (
                "loaded", "lam_sum", "lam_exp", "scored", "masked", "neg_max", "exped", "probs", "turned",
                "pt_ready", "attended", "stored", "dve_done"))
        block = st.block()

        @block.sync
        def _(sp):
            sp.dma_start(lp[:].rearrange("p a d -> p (a d)"), ins["diff_lambda"].partition_broadcast(P)
                         ).then_inc(loaded, 16)

        @block.tensor
        def _(pe):
            def scores(h):
                if h >= 2:
                    pe.wait_ge(masked, h - 1)
                for c in range(2):
                    rows = slice(c * HEAD, (c + 1) * HEAD)
                    for t, (lo, hi) in enumerate(parts):
                        last = pe.matmul(ps[:, h % 2, c, lo:hi], zt[rows, h, t * P:(t + 1) * P],
                                         zt[rows, 8 + h, 0:hi - lo], start=True, stop=True)
                last.then_inc(scored, 1)

            def turn_probs(h):
                pe.wait_ge(probs, h + 1)
                if h >= 2:
                    pe.wait_ge(pt_ready, h - 1)
                for c in range(3):
                    last = pe.transpose(pp[:, h % 2, c * P:(c + 1) * P], sc[:, h % 2, 0, c * P:(c + 1) * P],
                                        k["ident"][:])
                last.then_inc(turned, 1)

            def values(h):
                pe.wait_ge(pt_ready, h + 1)
                if h >= 2:
                    pe.wait_ge(stored, h - 1)
                v = [z[:, t, 2 * D + h * P:2 * D + (h + 1) * P] for t in range(TT)]
                pe.matmul(po[:, h % 2, 0:P], pt[:, h % 2, 0:P], v[0], start=True, stop=True)
                pe.matmul(po[:, h % 2, P:2 * P], pt[:, h % 2, P:2 * P], v[0], start=True, stop=False)
                pe.matmul(po[:, h % 2, P:2 * P], pt[:, h % 2, 2 * P:SC], v[1], start=False,
                          stop=True).then_inc(attended, 1)

            for h in range(HEADS + 2):
                if h < HEADS:
                    scores(h)
                if 1 <= h <= HEADS:
                    turn_probs(h - 1)
                if h >= 2:
                    values(h - 2)

        @block.vector
        def _(dve):
            step = InOrder(dve, dve_done)
            dve.wait_ge(loaded, 16)
            step(dve.tensor_tensor(lp[:, 0, :], lp[:, 0, :], lp[:, 1, :], ALU.mult))
            step(dve.tensor_tensor(lp[:, 2, :], lp[:, 2, :], lp[:, 3, :], ALU.mult))
            dve.tensor_reduce(lam[:, 0:1], lp[:, 0, :], AX.X, ALU.add).then_inc(lam_sum, 1)
            dve.tensor_reduce(lam[:, 1:2], lp[:, 2, :], AX.X, ALU.add).then_inc(lam_sum, 1)
            dve.wait_ge(lam_exp, 1)
            step(dve.tensor_tensor(neg_lam[:], lam[:, 1:2], lam[:, 0:1], ALU.subtract))
            step(dve.tensor_scalar(neg_lam[:], neg_lam[:], -DIFF_LAM_INIT, None, ALU.add))

            def mask(h):
                dve.wait_ge(scored, h + 1)
                if h >= 2:
                    dve.wait_ge(turned, h - 1)
                s = sc[:, h % 2]
                dve.scalar_tensor_tensor(s, ps[:, h % 2, :, 0:SC], HEAD ** -0.5,
                                         k["causal"][:].unsqueeze(1).broadcast_to([P, 2, SC]), ALU.mult,
                                         ALU.add).then_inc(masked, 1)
                dve.wait_ge(masked, h + 1)
                for t, (lo, hi) in enumerate(parts):
                    dve.tensor_reduce(nm[:, h % 2, t, :], s[:, :, lo:hi], AX.X, ALU.max,
                                      negate=True).then_inc(neg_max, 1)

            def combine(h):
                dve.wait_ge(exped, 4 * h + 4)
                r = sm[:, h % 2]
                step(dve.reciprocal(r, r))
                step(dve.tensor_scalar(r[:, :, 1], r[:, :, 1], neg_lam[:], None, ALU.mult))
                for t, (lo, hi) in enumerate(parts):
                    last = dve.tensor_scalar(sc[:, h % 2, 1, lo:hi], sc[:, h % 2, 1, lo:hi], sm[:, h % 2, t, 1:2],
                                             None, ALU.mult)
                step(last)
                for t, (lo, hi) in enumerate(parts):
                    last = dve.scalar_tensor_tensor(sc[:, h % 2, 0, lo:hi], sc[:, h % 2, 0, lo:hi],
                                                    sm[:, h % 2, t, 0:1], sc[:, h % 2, 1, lo:hi], ALU.mult, ALU.add)
                last.then_inc(probs, 1)

            for h in range(HEADS + 1):
                if h < HEADS:
                    mask(h)
                if h >= 1:
                    combine(h - 1)

        @block.scalar
        def _(act):
            act.wait_ge(lam_sum, 2)
            act.activation(lam[:], lam[:], ACT.Exp).then_inc(lam_exp, 1)

            def exp(h):
                for t, (lo, hi) in enumerate(parts):
                    act.wait_ge(neg_max, 2 * h + t + 1)
                    for c in range(2):
                        act.activation(sc[:, h % 2, c, lo:hi], sc[:, h % 2, c, lo:hi], ACT.Exp,
                                       bias=nm[:, h % 2, t, c:c + 1],
                                       accum_out=sm[:, h % 2, t, c:c + 1]).then_inc(exped, 1)

            def move_probs(h):
                act.wait_ge(turned, h + 1)
                if h >= 2:
                    act.wait_ge(attended, h - 1)
                act.copy(pt[:, h % 2, :], pp[:, h % 2, 0:SC]).then_inc(pt_ready, 1)

            def store(h):
                act.wait_ge(attended, h + 1)
                act.copy(o[:, :, h * P:(h + 1) * P],
                         po[:, h % 2, 0:2 * P].rearrange("p (t d) -> p t d", t=TT)).then_inc(stored, 1)

            for h in range(HEADS + 2):
                if h < HEADS:
                    exp(h)
                if 1 <= h <= HEADS:
                    move_probs(h - 1)
                if h >= 2:
                    store(h - 2)


def diff_layer(nc, k, ins, mod, next_mod, modc):
    x = k["x"]
    with Stage(nc, "l1") as st:
        m = [mod[:, i * D:(i + 1) * D] for i in range(6)]
        h_t = st.sb("h_t", [P, KT, S])
        with Stage(nc, "l1b") as sb:
            z = sb.sb("z", [P, TT, 3 * D])
            zt = sb.sb("zt", [P, 16, S])
            o = sb.sb("o", [P, TT, D])
            normed(nc, k, "norm1", x, ins["attn_norm1"], m[0], m[1], h_t)
            project(nc, k, "proj1", h_t, chunked(ins["diff_w_in"], 3 * D), out=z)
            head_norm_rope(nc, k, "rope1", z, [(0, 16, ins["diff_q_norm"]), (D, 16, ins["diff_k_norm"])])
            turn(nc, k, "turn1", z, [i * P for i in range(16)], zt)
            diff_attention(nc, k, ins, z, zt, o)
            head_norm(nc, k, "onorm1", o[:], ins["diff_out_norm"], 1.0 - DIFF_LAM_INIT)
            turn(nc, k, "oturn1", o, [i * P for i in range(KT)], h_t)
        project(nc, k, "out1", h_t, chunked(ins["diff_w_out"], D), residual=(x, m[2]))
    silu = k["silu_c"]
    feed_forward(nc, k, ins, 1, m, (ins["ada_w2"], [(silu[:, 1, :], next_mod, 12), (silu[:, 2, :], modc, 4)]))
    finish_modulation(nc, k, "ada2b", ins["ada_b2"], [(next_mod, 0, 12), (modc, 0, 4)])


XC = 2 * S
DH = 2 * DN_HEADS
TILES = 2 * TT


def delta_qkv(nc, k, ins, h_t, q_t, k_t, v_t, y):
    with Stage(nc, "dnqkv") as st:
        ring = 3
        w = st.sb("w", [P, ring, KT * CW])
        taps = st.sb("taps", [P, 3 * KT, DN_CONV])
        psum = st.ps("psum", [P, 4, CW])
        slot_loaded = [st.sem(f"slot_loaded{i}") for i in range(ring)]
        taps_loaded, product, conved, silued, dve_done = (
            st.sem(n) for n in ("taps_loaded", "product", "conved", "silued", "dve_done"))
        blocks = 3 * KT
        block = st.block()

        @block.sync
        def _(sp):
            sp.dma_start(taps[:], ins["dn_conv"]).then_inc(taps_loaded, 16)
            for j in range(blocks // 4):
                if j >= ring:
                    sp.wait_ge(product, 4 * (j - ring + 1))
                sp.dma_start(w[:, j % ring, :], ins["dn_w_qkv"][j]).then_inc(slot_loaded[j % ring], 16)

        @block.tensor
        def _(pe):
            for b in range(blocks):
                j, col = b // 4, (b % 4) * P
                n = S if b < KT else XC
                pe.wait_ge(slot_loaded[j % ring], 16 * (j // ring + 1))
                if b >= 4:
                    pe.wait_ge(conved, b - 3)
                for c in range(KT):
                    last = pe.matmul(psum[:, b % 4, 0:n], w[:, j % ring, c * CW + col:c * CW + col + P],
                                     h_t[:, c, 0:n], start=(c == 0), stop=(c == KT - 1))
                last.then_inc(product, 1)

        @block.vector
        def _(dve):
            step = InOrder(dve, dve_done)
            dve.wait_ge(taps_loaded, 16)
            mid = DN_CONV // 2
            for b in range(blocks):
                dve.wait_ge(product, b + 1)
                if b >= 2:
                    dve.wait_ge(silued, b - 1)
                n = S if b < KT else XC
                step(dve.tensor_scalar(y[:, b % 2, 0:n], psum[:, b % 4, 0:n], taps[:, b, mid:mid + 1], None, ALU.mult))
                for tap in (0, 1, 3, 4):
                    s = tap - mid
                    for lo, hi, row in ((0, S, ROW), (S, XC, S)):
                        if hi > n:
                            continue
                        to = y[:, b % 2, lo:hi].rearrange("p (r w) -> p r w", w=row)[:, :, max(0, -s):row - max(0, s)]
                        of = psum[:, b % 4, lo:hi].rearrange("p (r w) -> p r w", w=row)[
                            :, :, max(0, s):row - max(0, -s)]
                        last = dve.scalar_tensor_tensor(to, of, taps[:, b, tap:tap + 1], to, ALU.mult, ALU.add)
                    if tap < 4:
                        step(last)
                last.then_inc(conved, 1)

        @block.scalar
        def _(act):
            for b in range(blocks):
                kind, h = b // KT, b % KT
                n = S if b < KT else XC
                act.wait_ge(conved, b + 1)
                act.activation((q_t, k_t, v_t)[kind][:, h, 0:n], y[:, b % 2, 0:n], ACT.Silu).then_inc(silued, 1)


def delta_unit(nc, k, q_t, k_t):
    jobs = [(q_t, h, S, P ** -0.5) for h in range(DN_HEADS)] + [(k_t, h, XC, 1.0) for h in range(DN_HEADS)]
    with Stage(nc, "dnunit") as st:
        sq = st.sb("sq", [P, 2, XC])
        root = st.sb("root", [P, 2, XC])
        psum = st.ps("psum", [P, 2, CW])
        squared, summed, plus_eps, rooted, dve_done = (
            st.sem(n) for n in ("squared", "summed", "plus_eps", "rooted", "dve_done"))
        block = st.block()

        @block.scalar
        def _(act):
            def square(i):
                v, h, n, _ = jobs[i]
                if i >= 2:
                    act.wait_ge(summed, i - 1)
                act.activation(sq[:, i % 2, 0:n], v[:, h, 0:n], ACT.Square).then_inc(squared, 1)

            for i in range(len(jobs) + 1):
                if i < len(jobs):
                    square(i)
                if i >= 1:
                    n = jobs[i - 1][2]
                    r = root[:, (i - 1) % 2, 0:n]
                    act.wait_ge(plus_eps, i)
                    act.activation(r, r, ACT.Sqrt).then_inc(rooted, 1)

        @block.tensor
        def _(pe):
            for i, (_, _, n, _) in enumerate(jobs):
                pe.wait_ge(squared, i + 1)
                if i >= 2:
                    pe.wait_ge(plus_eps, i - 1)
                pe.matmul(psum[:, i % 2, 0:n], k["ones"][:], sq[:, i % 2, 0:n], start=True,
                          stop=True).then_inc(summed, 1)

        @block.vector
        def _(dve):
            step = InOrder(dve, dve_done)
            for i in range(len(jobs) + 1):
                if i < len(jobs):
                    n = jobs[i][2]
                    dve.wait_ge(summed, i + 1)
                    dve.tensor_scalar(root[:, i % 2, 0:n], psum[:, i % 2, 0:n], EPS, None, ALU.add).then_inc(plus_eps, 1)
                if i >= 1:
                    v, h, n, factor = jobs[i - 1]
                    r = root[:, (i - 1) % 2, 0:n]
                    dve.wait_ge(rooted, i)
                    step(dve.reciprocal(r, r))
                    step(dve.scalar_tensor_tensor(v[:, h, 0:n], v[:, h, 0:n], factor, r, ALU.mult, ALU.mult))


def delta_gates(nc, k, ins, h_t, dg):
    beta, g_sum, exp_g, exp_rest, exp_last, rows = (dg[n] for n in (
        "beta", "g_sum", "exp_g", "exp_rest", "exp_last", "rows"))
    wide = [P, TILES, DH]
    with Stage(nc, "dngate") as st:
        w = st.sb("w", [P, KT, 2 * DH])
        dt = st.sb("dt", [P, DH])
        la = st.sb("la", [P, DH])
        a = st.sb("a", wide)
        e = st.sb("e", wide)
        pba = st.ps("pba", [P, CW])
        pg = st.ps("pg", [P, CW])
        pl = st.ps("pl", [P, CW])
        pr = st.ps("pr", [P, 2, CW])
        loaded, product, neg_abs, exp_abs, one_plus, logged, g_ready, sums, turned, rest_ready, exps, dve_done = (
            st.sem(n) for n in ("loaded", "product", "neg_abs", "exp_abs", "one_plus", "logged", "g_ready",
                                "sums", "turned", "rest_ready", "exps", "dve_done"))
        block = st.block()

        @block.sync
        def _(sp):
            sp.dma_start(w[:].rearrange("p c n -> p (c n)"), ins["dn_w_ba"]).then_inc(loaded, 16)
            sp.dma_start(dt[:], ins["dn_dt_bias"].partition_broadcast(P)).then_inc(loaded, 16)
            sp.dma_start(la[:], ins["dn_a_log"].partition_broadcast(P)).then_inc(loaded, 16)

        @block.tensor
        def _(pe):
            pe.wait_ge(loaded, 48)
            for t in range(TILES):
                for c in range(KT):
                    last = pe.matmul(pba[:, t * 2 * DH:(t + 1) * 2 * DH], h_t[:, c, t * P:(t + 1) * P], w[:, c, :],
                                     start=(c == 0), stop=(c == KT - 1))
            last.then_inc(product, 1)
            pe.wait_ge(g_ready, 1)
            for t in range(TILES):
                for d in range(2):
                    at = t * DH + d * DN_HEADS
                    pe.matmul(pg[:, at:at + DN_HEADS], k["incl"][:, d, :], a[:, t, d * DN_HEADS:(d + 1) * DN_HEADS],
                              start=True, stop=True)
            pe.matmul(pl[:, 0:TILES * DH], k["ones"][:], a[:].rearrange("p t n -> p (t n)"), start=True,
                      stop=True).then_inc(sums, 1)
            pe.wait_ge(rest_ready, 1)
            for t in range(TILES):
                pe.transpose(pr[0:DH, t // 2, (t % 2) * S:(t % 2) * S + P], g_sum[:, t, :], k["ident"][:])
                last = pe.transpose(pr[0:DH, t // 2, (t % 2) * S + P:(t % 2 + 1) * S], beta[:, t, :], k["ident"][:])
            last.then_inc(turned, 1)

        @block.scalar
        def _(act):
            act.wait_ge(loaded, 48)
            act.activation(la[:], la[:], ACT.Exp).then_inc(exp_abs, 1)
            act.wait_ge(neg_abs, 2)
            act.activation(beta[:], beta[:], ACT.Exp, scale=-1.0).then_inc(exp_abs, 1)
            act.activation(e[:], e[:], ACT.Exp).then_inc(exp_abs, 1)
            act.wait_ge(one_plus, 1)
            act.activation(e[:], e[:], ACT.Ln).then_inc(logged, 1)
            act.wait_ge(rest_ready, 1)
            for v in (exp_g, exp_rest, exp_last):
                act.activation(v[:], v[:], ACT.Exp).then_inc(exps, 1)

        @block.vector
        def _(dve):
            step = InOrder(dve, dve_done)
            dve.wait_ge(product, 1)
            ba = pba[:, 0:TILES * 2 * DH].rearrange("p (t n) -> p t n", t=TILES)
            dve.tensor_copy(beta[:], ba[:, :, 0:DH]).then_inc(neg_abs, 1)
            step(dve.tensor_tensor(a[:], ba[:, :, DH:2 * DH], dt[:].unsqueeze(1).broadcast_to(wide), ALU.add))
            step(dve.tensor_scalar(e[:], a[:], -1.0, None, ALU.mult))
            dve.tensor_tensor(e[:], e[:], a[:], ALU.min).then_inc(neg_abs, 1)
            dve.wait_ge(exp_abs, 3)
            dve.tensor_scalar(e[:], e[:], 1.0, None, ALU.add).then_inc(one_plus, 1)
            step(dve.tensor_scalar(beta[:], beta[:], 1.0, None, ALU.add))
            step(dve.reciprocal(beta[:], beta[:]))
            step(dve.tensor_scalar(a[:], a[:], 0.0, None, ALU.max))
            dve.wait_ge(logged, 1)
            step(dve.tensor_tensor(a[:], a[:], e[:], ALU.add))
            dve.scalar_tensor_tensor(a[:], a[:], -1.0, la[:].unsqueeze(1).broadcast_to(wide), ALU.mult,
                                     ALU.mult).then_inc(g_ready, 1)
            dve.wait_ge(sums, 1)
            total = pl[:, 0:TILES * DH].rearrange("p (t n) -> p t n", t=TILES)
            so_far = pg[:, 0:TILES * DH].rearrange("p (t n) -> p t n", t=TILES)
            step(dve.tensor_copy(g_sum[:], so_far))
            step(dve.tensor_copy(exp_g[:], so_far))
            step(dve.tensor_copy(exp_last[:], total))
            dve.tensor_tensor(exp_rest[:], exp_last[:], g_sum[:], ALU.subtract).then_inc(rest_ready, 1)
            dve.wait_ge(turned, 1)
            dve.wait_ge(exps, 3)
            step(dve.tensor_copy(rows[:].rearrange("n (a b) s -> n a (b s)", a=2), pr[0:DH]))


def delta_matrices(nc, k, dg, q_t, k_t, at_m, qd):
    quads = [(t, g, d) for t in range(TILES) for g in range(2) for d in range(2)]
    n_jobs = len(quads)
    with Stage(nc, "dnmat") as st:
        dt = st.sb("dt", [P, 2, 4, P])
        pgram = st.ps("pgram", [P, CW])
        pkq = st.ps("pkq", [P, CW])
        prow = st.ps("prow", [P, 2, 4, S])
        sel = st.sb("sel", [DH, DH, P])
        sel_ready, grams, row_sums, diffs, decays, used, dve_done = (
            st.sem(n) for n in ("sel_ready", "grams", "row_sums", "diffs", "decays", "used", "dve_done"))
        block = st.block()

        @block.gpsimd
        def _(pool):
            pool.memset(sel[:], 1.0).then_inc(sel_ready, 1)
            pool.wait_ge(sel_ready, 1)
            pool.affine_select(out=sel[:], in_=sel[:], compare_op=ALU.is_equal, fill=0.0, base=0,
                               pattern=[[-1, DH], [0, P]], channel_multiplier=1).then_inc(sel_ready, 1)

        @block.tensor
        def _(pe):
            pe.wait_ge(sel_ready, 2)
            for i, (t, g, d) in enumerate(quads):
                if i >= 2:
                    pe.wait_ge(used, i - 1)
                for h in range(4):
                    last = pe.matmul(prow[:, i % 2, h, :], sel[:, d * DN_HEADS + g * 4 + h, :], dg["rows"][:, t, :],
                                     start=True, stop=True)
                last.then_inc(row_sums, 1)
                if d == 0:
                    if i >= 2:
                        pe.wait_ge(used, i)
                    for h in range(4):
                        key = k_t[:, g * 4 + h, t * P:(t + 1) * P]
                        last = pe.matmul(pgram[:, h * P:(h + 1) * P], key, key, start=True, stop=True)
                    if t < TT:
                        for h in range(4):
                            last = pe.matmul(pkq[:, h * P:(h + 1) * P], k_t[:, g * 4 + h, t * P:(t + 1) * P],
                                             q_t[:, g * 4 + h, t * P:(t + 1) * P], start=True, stop=True)
                    last.then_inc(grams, 1)

        @block.vector
        def _(dve):
            step = InOrder(dve, dve_done)
            four = [P, 4, P]

            def diff(i):
                t, g, d = quads[i]
                gs = dg["g_sum"][:, t, d * DN_HEADS + g * 4:d * DN_HEADS + g * 4 + 4]
                dve.wait_ge(row_sums, i + 1)
                step(dve.tensor_tensor(dt[:, i % 2], prow[:, i % 2, :, 0:P], gs.unsqueeze(2).broadcast_to(four),
                                       ALU.subtract))
                dve.tensor_tensor(dt[:, i % 2], dt[:, i % 2],
                                  k["decay_mask"][:, d, :].unsqueeze(1).broadcast_to(four), ALU.add).then_inc(diffs, 1)

            def matrices(i):
                t, g, d = quads[i]
                m = at_m[:, t, d, g * 4:g * 4 + 4, :]
                dve.wait_ge(decays, i + 1)
                dve.wait_ge(grams, i // 2 + 1)
                gram = pgram[:].rearrange("p (h s) -> p h s", h=4)
                step(dve.tensor_tensor(m, gram, dt[:, i % 2], ALU.mult))
                step(dve.tensor_tensor(m, m, k["strict"][:, d, :].unsqueeze(1).broadcast_to(four), ALU.mult))
                if t < TT:
                    step(dve.tensor_tensor(qd[:, t, d, g * 4:g * 4 + 4, :], pkq[:].rearrange("p (h s) -> p h s", h=4),
                                           dt[:, i % 2], ALU.mult))
                dve.tensor_tensor(m, m, prow[:, i % 2, :, P:S], ALU.mult).then_inc(used, 1)
                dve.wait_ge(used, i + 1)

            for i in range(n_jobs + 1):
                if i < n_jobs:
                    diff(i)
                if i >= 1:
                    matrices(i - 1)

        @block.scalar
        def _(act):
            for i in range(n_jobs):
                act.wait_ge(diffs, i + 1)
                act.activation(dt[:, i % 2], dt[:, i % 2], ACT.Exp).then_inc(decays, 1)


def delta_inverse(nc, k, at_m):
    groups = [(t, d, g) for t in range(TILES) for d in range(2) for g in range(2)]
    levels = 6
    steps = [(pair, level, which) for pair in range(len(groups) // 2) for level in range(levels + 1)
             for which in range(2)]
    with Stage(nc, "dninv") as st:
        pw = st.sb("pw", [P, 2, 4, P])
        pwt = st.sb("pwt", [P, 2, 4, P])
        pp = st.ps("pp", [P, 2, CW])
        pt = st.ps("pt", [P, 2, CW])
        pi = st.ps("pi", [P, 2, CW])
        powers, power_ready, t_power_ready, product, inverse_ready = (
            st.sem(n) for n in ("powers", "power_ready", "t_power_ready", "product", "inverse_ready"))
        block = st.block()

        def inverse(pair, which):
            t, d, g = groups[2 * pair + which]
            return at_m[:, t, d, g * 4:g * 4 + 4, :]

        @block.tensor
        def _(pe):
            def power(n):
                pair, level, b = steps[n]
                m = inverse(pair, b)
                if n >= 2:
                    pe.wait_ge(power_ready, n - 1)
                    pe.wait_ge(t_power_ready, n - 1)
                for h in range(4):
                    cols = slice(h * P, (h + 1) * P)
                    if level == 0:
                        last = pe.transpose(pp[:, b, cols], m[:, h, :], k["ident"][:])
                    else:
                        pe.matmul(pp[:, b, cols], pwt[:, b, h, :], pw[:, b, h, :], start=True, stop=True)
                        last = pe.matmul(pt[:, b, cols], pw[:, b, h, :], pwt[:, b, h, :], start=True, stop=True)
                last.then_inc(powers, 1)

            def apply(n):
                pair, level, b = steps[n]
                if level == 0:
                    return
                m = inverse(pair, b)
                pe.wait_ge(power_ready, n + 1)
                pe.wait_ge(inverse_ready, n - 1)
                for h in range(4):
                    last = pe.matmul(pi[:, b, h * P:(h + 1) * P], pw[:, b, h, :], m[:, h, :], start=True, stop=True)
                last.then_inc(product, 1)

            for n in range(len(steps) + 1):
                if n < len(steps):
                    power(n)
                if n >= 1:
                    apply(n - 1)

        def products_before(n):
            return sum(1 for _, level, _ in steps[:n] if level)

        @block.scalar
        def _(act):
            for n, (pair, level, b) in enumerate(steps):
                act.wait_ge(powers, n + 1)
                if n >= 2:
                    act.wait_ge(product, products_before(n - 1)) if products_before(n - 1) else None
                act.copy(pw[:, b], pp[:, b, :].rearrange("p (h s) -> p h s", h=4)).then_inc(power_ready, 1)

        @block.vector
        def _(dve):
            def t_power(n):
                pair, level, b = steps[n]
                m = inverse(pair, b)
                dve.wait_ge(powers, n + 1)
                if level == 0:
                    dve.tensor_copy(pwt[:, b], m).then_inc(t_power_ready, 1)
                else:
                    dve.tensor_copy(pwt[:, b], pt[:, b, :].rearrange("p (h s) -> p h s", h=4)
                                    ).then_inc(t_power_ready, 1)

            def factor(n):
                pair, level, b = steps[n]
                m = inverse(pair, b)
                if level == 0:
                    dve.wait_ge(t_power_ready, n + 1)
                    dve.scalar_tensor_tensor(m, m, -1.0, k["ident"][:].unsqueeze(1).broadcast_to([P, 4, P]), ALU.mult,
                                             ALU.add).then_inc(inverse_ready, 1)
                else:
                    dve.wait_ge(product, products_before(n + 1))
                    dve.wait_ge(inverse_ready, n - 1)
                    dve.tensor_tensor(m, m, pi[:, b, :].rearrange("p (h s) -> p h s", h=4), ALU.add
                                      ).then_inc(inverse_ready, 1)

            for n in range(len(steps) + 1):
                if n < len(steps):
                    t_power(n)
                if n >= 1:
                    factor(n - 1)


def delta_recurrence(nc, k, dg, q_t, k_t, k_tok, v_tok, inv_t, qd, o):
    order = {0: [2, 3, 0, 1], 1: [3, 2, 1, 0]}
    jobs = [(order[d][s], d, g) for s in range(TILES) for d in range(2) for g in range(2)]
    n_jobs = len(jobs)
    with Stage(nc, "dnrec") as st:
        state = st.sb("state", [P, 2, 2, 4, P])
        rhs = st.sb("rhs", [P, 2, 4, P])
        kd = st.sb("kd", [P, 2, 4, P])
        vn = st.sb("vn", [P, 2, 4, P])
        tmp = st.sb("tmp", [P, 4, P])
        pks = st.ps("pks", [P, 2, CW])
        pqs = st.ps("pqs", [P, CW])
        pvn = st.ps("pvn", [P, 2, CW])
        psu = st.ps("psu", [P, 2, CW])
        poi = st.ps("poi", [P, CW])
        zeroed, recalled, rhs_ready, kd_ready, v_new, vn_ready, updated, state_ready, out_done, dve_done = (
            st.sem(n) for n in ("zeroed", "recalled", "rhs_ready", "kd_ready", "v_new", "vn_ready", "updated",
                                "state_ready", "out_done", "dve_done"))
        block = st.block()

        def four(ap):
            return ap.rearrange("p (h s) -> p h s", h=4)

        def factor(what, i):
            t, d, g = jobs[i]
            v = dg[what][:, t, d * DN_HEADS + g * 4:d * DN_HEADS + g * 4 + 4]
            return v.unsqueeze(2).broadcast_to([P, 4, P])

        def outs(i):
            return sum(1 for t, _, _ in jobs[:i] if t < TT)

        @block.tensor
        def _(pe):
            def recall(i):
                t, d, g = jobs[i]
                pe.wait_ge(zeroed, 2)
                if i >= 4:
                    pe.wait_ge(state_ready, i - 3)
                if i >= 2:
                    pe.wait_ge(rhs_ready, i - 1)
                for h in range(4):
                    last = pe.matmul(pks[:, i % 2, h * P:(h + 1) * P], k_t[:, g * 4 + h, t * P:(t + 1) * P],
                                     state[:, d, g, h, :], start=True, stop=True)
                if t < TT:
                    if outs(i) >= 1:
                        pe.wait_ge(out_done, outs(i))
                    for h in range(4):
                        last = pe.matmul(pqs[:, h * P:(h + 1) * P], q_t[:, g * 4 + h, t * P:(t + 1) * P],
                                         state[:, d, g, h, :], start=True, stop=True)
                last.then_inc(recalled, 1)

            def solve(i):
                t, d, g = jobs[i]
                pe.wait_ge(rhs_ready, i + 1)
                if i >= 2:
                    pe.wait_ge(vn_ready, i - 1)
                for h in range(4):
                    last = pe.matmul(pvn[:, i % 2, h * P:(h + 1) * P], inv_t[:, t, d, g * 4 + h, :],
                                     rhs[:, i % 2, h, :], start=True, stop=True)
                last.then_inc(v_new, 1)

            def update(i):
                t, d, g = jobs[i]
                pe.wait_ge(vn_ready, i + 1)
                pe.wait_ge(kd_ready, i + 1)
                if i >= 2:
                    pe.wait_ge(state_ready, i - 1)
                for h in range(4):
                    last = pe.matmul(psu[:, i % 2, h * P:(h + 1) * P], kd[:, i % 2, h, :], vn[:, i % 2, h, :],
                                     start=True, stop=True)
                if t < TT:
                    if outs(i) >= 1:
                        pe.wait_ge(out_done, outs(i))
                    for h in range(4):
                        last = pe.matmul(poi[:, h * P:(h + 1) * P], qd[:, t, d, g * 4 + h, :], vn[:, i % 2, h, :],
                                         start=True, stop=True)
                last.then_inc(updated, 1)

            for i in range(n_jobs):
                recall(i)
                solve(i)
                update(i)

        @block.gpsimd
        def _(pool):
            pool.memset(state[:], 0.0).then_inc(zeroed, 1)
            pool.memset(o, 0.0).then_inc(zeroed, 1)
            for i, (t, d, g) in enumerate(jobs):
                if i >= 2:
                    pool.wait_ge(updated, i - 1)
                pool.tensor_tensor(kd[:, i % 2], k_tok[:, t, g * 4 * P:(g + 1) * 4 * P].rearrange(
                    "p (h s) -> p h s", h=4), factor("exp_rest", i), ALU.mult).then_inc(kd_ready, 1)

        @block.scalar
        def _(act):
            for i in range(n_jobs):
                act.wait_ge(v_new, i + 1)
                if i >= 2:
                    act.wait_ge(updated, i - 1)
                act.copy(vn[:, i % 2], four(pvn[:, i % 2, :])).then_inc(vn_ready, 1)

        @block.vector
        def _(dve):
            step = InOrder(dve, dve_done)
            dve.wait_ge(zeroed, 2)
            for i, (t, d, g) in enumerate(jobs):
                cols = slice(g * 4 * P, (g + 1) * 4 * P)
                dve.wait_ge(recalled, i + 1)
                if i >= 2:
                    dve.wait_ge(v_new, i - 1)
                r = rhs[:, i % 2]
                step(dve.tensor_tensor(r, four(pks[:, i % 2, :]), factor("exp_g", i), ALU.mult))
                step(dve.tensor_tensor(r, four(v_tok[:, t, cols]), r, ALU.subtract))
                dve.tensor_tensor(r, r, factor("beta", i), ALU.mult).then_inc(rhs_ready, 1)
                s = state[:, d, g]
                step(dve.tensor_tensor(s, s, factor("exp_last", i), ALU.mult))
                if t < TT:
                    step(dve.tensor_tensor(tmp[:], four(pqs[:]), factor("exp_g", i), ALU.mult))
                    step(dve.tensor_tensor(four(o[:, t, cols]), four(o[:, t, cols]), tmp[:], ALU.add))
                dve.wait_ge(updated, i + 1)
                dve.tensor_tensor(s, s, four(psu[:, i % 2, :]), ALU.add).then_inc(state_ready, 1)
                if t < TT:
                    dve.tensor_tensor(four(o[:, t, cols]), four(o[:, t, cols]), four(poi[:]), ALU.add
                                      ).then_inc(out_done, 1)
                    dve.wait_ge(out_done, outs(i + 1))


def turn_back(nc, k, name, v_t, out):
    with Stage(nc, name) as st:
        banks = 6
        psum = st.ps("psum", [P, banks, CW])
        turned, copied, moved = st.sem("turned"), st.sem("copied"), st.sem("moved")
        jobs = [(t, g) for t in range(TILES) for g in range(2)]
        block = st.block()

        @block.tensor
        def _(pe):
            for n, (t, g) in enumerate(jobs):
                if n >= banks:
                    prior = n - banks
                    pe.wait_ge(copied if prior % 2 == 0 else moved, prior // 2 + 1)
                for h in range(4):
                    last = pe.transpose(psum[:, n % banks, h * P:(h + 1) * P],
                                        v_t[:, g * 4 + h, t * P:(t + 1) * P], k["ident"][:])
                last.then_inc(turned, 1)

        @block.vector
        def _(dve):
            for n in range(0, len(jobs), 2):
                t, g = jobs[n]
                dve.wait_ge(turned, n + 1)
                dve.tensor_copy(out[:, t, g * CW:(g + 1) * CW], psum[:, n % banks, :]).then_inc(copied, 1)

        @block.scalar
        def _(act):
            for n in range(1, len(jobs), 2):
                t, g = jobs[n]
                act.wait_ge(turned, n + 1)
                act.copy(out[:, t, g * CW:(g + 1) * CW], psum[:, n % banks, :]).then_inc(moved, 1)


def delta_layer(nc, k, ins, mod, modc, free):
    x = k["x"]
    m = [mod[:, i * D:(i + 1) * D] for i in range(6)]
    with Stage(nc, "dn") as st:
        o = modc[:].rearrange("p (t d) -> p t d", t=TT)
        gate = mod[:, 0:2 * D].rearrange("p (t d) -> p t d", t=TT)
        with Stage(nc, "dna") as sa:
            q_t = free[:, TILES * D:6 * D].rearrange("p (h s) -> p h s", h=DN_HEADS)
            k_t = sa.sb("k_t", [P, DN_HEADS, XC])
            v_tok = sa.sb("v_tok", [P, TILES, D])
            dg = {n: sa.sb(n, [P, TILES, DH]) for n in ("beta", "g_sum", "exp_g", "exp_rest", "exp_last")}
            dg["rows"] = sa.sb("rows", [DH, TILES, S])
            with Stage(nc, "dnb") as sb:
                h_t = sb.sb("h_t", [P, KT, XC])
                with Stage(nc, "dnc") as sc:
                    ctx = sc.sb("ctx", [P, TT, D])
                    loaded = sc.sem("loaded")
                    block = nc.Block()
                    with block as block:
                        @block.sync
                        def _(sp):
                            sp.dma_start(ctx[:], ins["ctx"].rearrange("(t p) d -> p t d", p=P)).then_inc(loaded, 16)
                            sp.wait_ge(loaded, 16)
                    normed(nc, k, "dnorm", x, ins["norm_g2"][0], m[0], m[1], h_t[:, :, 0:S])
                    normed(nc, k, "dcnorm", ctx, ins["norm_g2"][0], modc[:, 0:D], modc[:, D:2 * D], h_t[:, :, S:XC])
                with Stage(nc, "dnd") as sd:
                    v_t = sd.sb("v_t", [P, DN_HEADS, XC])
                    delta_qkv(nc, k, ins, h_t, q_t, k_t, v_t, v_tok[:, 0, :].rearrange("p (a n) -> p a n", a=2))
                    turn_back(nc, k, "dnv", v_t, v_tok)
                delta_unit(nc, k, q_t, k_t)
                project(nc, k, "dngp", h_t, chunked(ins["dn_w_gate"], D), out=gate)
                delta_gates(nc, k, ins, h_t, dg)
            k_tok = free[:, 0:TILES * D].rearrange("p (t d) -> p t d", t=TILES)
            turn_back(nc, k, "dnk", k_t, k_tok)
            at_m = sa.sb("at_m", [P, TILES, 2, DN_HEADS, P])
            qd = sa.sb("qd", [P, TT, 2, DN_HEADS, P])
            delta_matrices(nc, k, dg, q_t, k_t, at_m, qd)
            delta_inverse(nc, k, at_m)
            delta_recurrence(nc, k, dg, q_t, k_t, k_tok, v_tok, at_m, qd, o)
        h_t = st.sb("o_t", [P, KT, S])
        head_norm(nc, k, "dnon", o, ins["dn_norm_g"], 1.0, gate=gate)
        turn(nc, k, "dnot", o, [i * P for i in range(KT)], h_t)
        project(nc, k, "dnout", h_t, chunked(ins["dn_w_out"], D), residual=(x, m[2]))


def peer_scores(nc, k, ins, h_t, scores):
    with Stage(nc, "pq") as st:
        ring = 3
        w = st.sb("w", [P, ring, KT * CW])
        q_t = st.sb("q_t", [P, 16, S])
        keys = st.sb("keys", [P, 16, NKEYS])
        psum = st.ps("psum", [P, 4, CW])
        pscore = st.ps("pscore", [P, 2, CW])
        slot_loaded = [st.sem(f"slot_loaded{i}") for i in range(ring)]
        keys_loaded, product, q_ready, scored, stored = (
            st.sem(n) for n in ("keys_loaded", "product", "q_ready", "scored", "stored"))
        block = st.block()

        @block.sync
        def _(sp):
            for j in range(4):
                if j >= ring:
                    sp.wait_ge(product, 4 * (j - ring + 1))
                sp.dma_start(w[:, j % ring, :], ins["peer_w_q"][j]).then_inc(slot_loaded[j % ring], 16)
            sp.dma_start(keys[:], ins["peer_keys"]).then_inc(keys_loaded, 16)

        @block.tensor
        def _(pe):
            for b in range(16):
                j, col = b // 4, (b % 4) * P
                pe.wait_ge(slot_loaded[j % ring], 16 * (j // ring + 1))
                if b >= 4:
                    pe.wait_ge(q_ready, b - 3)
                for c in range(KT):
                    last = pe.matmul(psum[:, b % 4, 0:S], w[:, j % ring, c * CW + col:c * CW + col + P],
                                     h_t[:, c, :], start=(c == 0), stop=(c == KT - 1))
                last.then_inc(product, 1)
            pe.wait_ge(keys_loaded, 16)
            pe.wait_ge(q_ready, 16)
            for n in range(8):
                t, quad = n // 4, n % 4
                if n >= 2:
                    pe.wait_ge(stored, n - 1)
                for b in range(4):
                    hp = quad * 4 + b
                    last = pe.matmul(pscore[:, n % 2, b * P:(b + 1) * P], q_t[:, hp, t * P:(t + 1) * P],
                                     keys[:, hp, :], start=True, stop=True)
                last.then_inc(scored, 1)

        @block.scalar
        def _(act):
            for b in range(16):
                act.wait_ge(product, b + 1)
                act.copy(q_t[:, b, :], psum[:, b % 4, 0:S]).then_inc(q_ready, 1)
            for n in range(8):
                t, quad = n // 4, n % 4
                act.wait_ge(scored, n + 1)
                act.copy(scores[:, t, quad * 4:quad * 4 + 4, :],
                         pscore[:, n % 2, :].rearrange("p (b s) -> p b s", b=4)).then_inc(stored, 1)


def peer_route(nc, k, scores, chosen):
    with Stage(nc, "route") as st:
        val = st.sb("val", [P, TT, 16, TOPK])
        idx = st.sb("idx", [P, TT, 16, TOPK], U32)
        idx_f = st.sb("idx_f", [P, TT, 16, TOPK])
        cand = st.sb("cand", [P, PHEADS, TOPK, TOPK])
        left = st.sb("left", [P, 2, TOPK * TOPK])
        top = st.sb("top", [P, TT, PHEADS, TOPK])
        pos = st.sb("pos", [P, TT, PHEADS, TOPK], U32)
        ab = st.sb("ab", [P, 2, PHEADS * TOPK], U32)
        ab_f = st.sb("ab_f", [P, 2, PHEADS * TOPK])
        hot = st.sb("hot", [P, PHEADS, TOPK, TOPK])
        pick = st.sb("pick", [P, TT, 3, P])
        total = st.sb("total", [P, PHEADS])
        psum = st.ps("psum", [P, 2, CW])
        shifted, exped, picked, turned, dve_done = (
            st.sem(n) for n in ("shifted", "exped", "picked", "turned", "dve_done"))
        block = st.block()

        @block.vector
        def _(dve):
            step = InOrder(dve, dve_done)

            def top16(values, spare, out_v, out_i):
                step(dve.max(out_v[:, 0:8], values))
                step(dve.match_replace(spare, out_v[:, 0:8], values, NEG))
                step(dve.max(out_v[:, 8:16], spare))
                step(dve.max_index(out_i[:, 0:8], out_v[:, 0:8], values))
                step(dve.max_index(out_i[:, 8:16], out_v[:, 8:16], spare))

            for t in range(TT):
                for hp in range(16):
                    top16(scores[:, t, hp, :], left[:, hp % 2, 0:P], val[:, t, hp, :], idx[:, t, hp, :])
            step(dve.tensor_copy(idx_f[:], idx[:]))
            for t in range(TT):
                v = val[:, t].rearrange("p (h two) n -> p h two n", two=2)
                four_d = [P, PHEADS, TOPK, TOPK]
                step(dve.tensor_tensor(cand[:], v[:, :, 0, :].unsqueeze(3).broadcast_to(four_d),
                                       v[:, :, 1, :].unsqueeze(2).broadcast_to(four_d), ALU.add))
                for h in range(PHEADS):
                    top16(cand[:, h].rearrange("p a b -> p (a b)"), left[:, h % 2, :], top[:, t, h, :], pos[:, t, h, :])
                flat = pos[:, t].rearrange("p h n -> p (h n)")
                step(dve.tensor_scalar(ab[:, 0, :], flat, 4, None, ALU.logical_shift_right))
                step(dve.tensor_scalar(ab[:, 1, :], flat, TOPK - 1, None, ALU.bitwise_and))
                step(dve.tensor_copy(ab_f[:], ab[:]))
                of = idx_f[:, t].rearrange("p (h two) n -> p h two n", two=2)
                for part in range(2):
                    step(dve.tensor_tensor(hot[:].rearrange("p h n a -> p (h n) a"),
                                           ab_f[:, part, :].unsqueeze(2).broadcast_to([P, P, TOPK]),
                                           k["iota"][:, 0:TOPK].unsqueeze(1).broadcast_to([P, P, TOPK]), ALU.is_equal))
                    step(dve.tensor_tensor(hot[:], hot[:], of[:, :, part, :].unsqueeze(2).broadcast_to(four_d), ALU.mult))
                    step(dve.tensor_reduce(pick[:, t, part, :], hot[:].rearrange("p h n a -> p (h n) a"), AX.X, ALU.add))
                gate = pick[:, t, 2, :].rearrange("p (h n) -> p h n", h=PHEADS)
                three = [P, PHEADS, TOPK]
                dve.tensor_tensor(gate, top[:, t], top[:, t, :, 0:1].broadcast_to(three), ALU.subtract).then_inc(shifted, 1)
                dve.wait_ge(exped, t + 1)
                step(dve.tensor_reduce(total[:], gate, AX.X, ALU.add))
                step(dve.reciprocal(total[:], total[:]))
                dve.tensor_tensor(gate, gate, total[:].unsqueeze(2).broadcast_to(three), ALU.mult).then_inc(picked, 1)
            for t in range(TT):
                dve.wait_ge(turned, t + 1)
                step(dve.tensor_copy(chosen[:, :, t * P:(t + 1) * P],
                                     psum[:, t, 0:3 * P].rearrange("p (c s) -> p c s", c=3)))

        @block.scalar
        def _(act):
            for t in range(TT):
                act.wait_ge(shifted, t + 1)
                act.activation(pick[:, t, 2, :], pick[:, t, 2, :], ACT.Exp).then_inc(exped, 1)

        @block.tensor
        def _(pe):
            for t in range(TT):
                pe.wait_ge(picked, t + 1)
                for c in range(3):
                    last = pe.transpose(psum[:, t, c * P:(c + 1) * P], pick[:, t, c, :], k["ident"][:])
                last.then_inc(turned, 1)


def peer_table(nc, k, chosen, table):
    per = 4
    quads = S // per
    with Stage(nc, "table") as st:
        first = st.sb("first", [P, 2, per, NKEYS])
        second = st.sb("second", [P, 2, per, NKEYS])
        psum = st.ps("psum", [P, 4, CW])
        hot, product, stored = (st.sem(n) for n in ("hot", "product", "stored"))
        block = st.block()

        @block.vector
        def _(dve):
            def one_hot(i, b, early=False):
                if not early:
                    dve.wait_ge(product, i - 1)
                for j in range(per):
                    at = [chosen[:, c, bass.ds(i * per + j, 1)] for c in range(3)]
                    dve.tensor_scalar(first[:, b, j, :], k["iota"][:], at[0], None, ALU.is_equal)
                    last = dve.tensor_scalar(second[:, b, j, :], k["iota"][:], at[1], at[2], ALU.is_equal, ALU.mult)
                last.then_inc(hot, 1)

            one_hot(0, 0, early=True)
            one_hot(1, 1, early=True)
            with dve.Fori(1, quads // 2) as r:
                for b in range(2):
                    one_hot(r * 2 + b, b)

        @block.tensor
        def _(pe):
            def products(i, b, bank, early=False):
                pe.wait_ge(hot, i + 1)
                if not early:
                    pe.wait_ge(stored, i - 3)
                for j in range(per):
                    last = pe.matmul(psum[:, bank, j * P:(j + 1) * P], first[:, b, j, :], second[:, b, j, :],
                                     start=True, stop=True)
                last.then_inc(product, 1)

            for i in range(4):
                products(i, i % 2, i, early=True)
            with pe.Fori(1, quads // 4) as r:
                for b in range(4):
                    products(r * 4 + b, b % 2, b)

        @block.scalar
        def _(act):
            with act.Fori(0, quads // 4) as r:
                for b in range(4):
                    act.wait_ge(product, r * 4 + (b + 1))
                    act.copy(table[:, :, bass.ds((r * 4 + b) * per, per)].rearrange("p n t -> p t n"),
                             psum[:, b, :].rearrange("p (t n) -> p t n", t=per)).then_inc(stored, 1)


def final_norm(nc, ins, x, g, junk, out):
    with Stage(nc, "final") as st:
        ss = st.sb("ss", [P, TT])
        loaded, squared, mean_ready, root_ready, ready, stored, dve_done = (
            st.sem(n) for n in ("loaded", "squared", "mean_ready", "root_ready", "ready", "stored", "dve_done"))
        block = st.block()

        @block.sync
        def _(sp):
            sp.dma_start(g, ins["final_g"].partition_broadcast(P)).then_inc(loaded, 16)
            for t in range(TT):
                sp.wait_ge(ready, t + 1)
                sp.dma_start(out[t * P:(t + 1) * P, :], x[:, t, :]).then_inc(stored, 16)
            sp.wait_ge(stored, 16 * TT)

        @block.scalar
        def _(act):
            for t in range(TT):
                act.activation(junk, x[:, t, :], ACT.Square, accum_out=ss[:, t:t + 1]).then_inc(squared, 1)
                act.wait_ge(squared, t + 1)
            act.wait_ge(mean_ready, 1)
            act.activation(ss[:], ss[:], ACT.Sqrt).then_inc(root_ready, 1)

        @block.vector
        def _(dve):
            step = InOrder(dve, dve_done)
            dve.wait_ge(squared, TT)
            dve.tensor_scalar(ss[:], ss[:], 1.0 / D, EPS, ALU.mult, ALU.add).then_inc(mean_ready, 1)
            dve.wait_ge(root_ready, 1)
            step(dve.reciprocal(ss[:], ss[:]))
            dve.wait_ge(loaded, 16)
            for t in range(TT):
                dve.scalar_tensor_tensor(x[:, t, :], x[:, t, :], ss[:, t:t + 1], g, ALU.mult,
                                         ALU.mult).then_inc(ready, 1)


def keep(nc, copies):
    with Stage(nc, "keep") as st:
        stored = st.sem("stored")
        block = st.block()

        @block.sync
        def _(sp):
            for dram, tile in copies:
                sp.dma_start(dram, tile).then_inc(stored, 16)
            sp.wait_ge(stored, 16 * len(copies))




def program(nc, ins, out):
    x_kept = nc.dram_tensor("x_kept", (P, TT, D), F32, kind="Internal").ap()
    gate_kept = nc.dram_tensor("gate_kept", (P, D), F32, kind="Internal").ap()
    with Stage(nc, "all") as pst:
        k = {name: pst.sb(name, [P, P]) for name in ("ident", "ones", "iota")}
        h_hi, h_lo = (pst.sb(n, [P, KT, S], F32R) for n in ("h_hi", "h_lo"))
        k["h_hi"], k["h_lo"] = h_hi, h_lo
        chosen = pst.sb("chosen", [P, 3, S])
        with Stage(nc, "main") as ms:
            constants(nc, ms, ins, k)
            mods = [ms.sb(f"mod{i}", [P, 6 * D]) for i in range(2)]
            modc = ms.sb("modc", [P, 2 * D])
            sparse_layer(nc, k, ins, mods[0], mods[1])
            diff_layer(nc, k, ins, mods[1], mods[0], modc)
            mod = mods[0]
            delta_layer(nc, k, ins, mod, modc, mods[1])
            m = [mod[:, i * D:(i + 1) * D] for i in range(6)]
            h_t = modc[:].rearrange("p (c s) -> p c s", c=KT)
            normed(nc, k, "pnorm", k["x"], ins["norm_g2"][1], m[3], m[4], h_t)
            keep(nc, [(x_kept, k["x"][:]), (gate_kept, m[5])])
            with Stage(nc, "pr") as ps:
                scores = ps.sb("scores", [P, TT, 16, NKEYS])
                peer_scores(nc, k, ins, h_t, scores)
                peer_route(nc, k, scores, chosen)
            split_h(nc, "psplit", h_t, h_hi, h_lo)
        with Stage(nc, "peer") as st:
            table = st.sb("table", [P, NKEYS, S])
            peer_table(nc, k, chosen, table)
            streamed_mlp(nc, k, "experts", ins["peer_u"], ins["peer_v"], "peer", (h_hi, h_lo),
                         kept=(x_kept, gate_kept), table=table, then=lambda x, rest: final_norm(nc, ins, x, rest[:, 0, :], rest[:, 1, :], out))




def _column_tiles(w, width=CW):
    n = w.shape[1] // width
    return w.reshape(KT, P, n, width).transpose(2, 1, 0, 3).reshape(n, P, KT * width)


def _hidden_tiles(matrices):
    n = matrices[0].shape[1] // P
    return np.concatenate([m.reshape(KT, P, n, P).transpose(2, 1, 0, 3).reshape(n, P, KT * P) for m in matrices],
                          axis=2)


def _layout(a):
    a = {name: np.asarray(v) for name, v in a.items()}
    slots = np.array([b + 4 * g for b in range(4) for g in range(2)])
    w = a["sp_w_in"][0]
    nq = w[:, Z_NQ:Z_KV].reshape(D, HEADS, HEAD)[:, slots].reshape(D, -1)
    ng = w[:, Z_GATE:].reshape(D, 3, HEADS)[:, :, slots].reshape(D, -1)
    w = np.concatenate([w[:, :Z_NQ], nq, w[:, Z_KV:Z_GATE], ng], axis=1)
    out = {"x": a["x"][0], "positions": a["positions"].reshape(TT, P).T, "sp_w_in": _column_tiles(w[:, :5 * CW]),
           "sp_w_in_tail": _column_tiles(w[:, 5 * CW:], SP_IN - 5 * CW)[0]}
    wo = a["sp_w_out"][0].reshape(2, HEADS, HEAD, D)
    wo = np.concatenate([wo[0], wo[1][slots]]).reshape(D, D)
    out["sp_w_out"] = _column_tiles(wo)
    for i in range(2):
        out[f"ada_w{i}"] = _column_tiles(a["ada_w"][i], CW // 2).reshape(24, P, KT, CW // 2)
        out[f"ada_b{i}"] = a["ada_b"][i]
        out[f"attn_norm{i}"] = a["attn_norm"][i]
        out[f"ffn_norm{i}"] = a["ffn_norm"][i]
        out[f"ffn_columns{i}"] = _hidden_tiles([a["ffn_w_gate"][i], a["ffn_w_up"][i]])
        out[f"ffn_rows{i}"] = a["ffn_w_down"][i].reshape(FFN_CHUNKS, P, D)
    out["c"] = a["c"].reshape(KT, P).T
    out["moba_q_norm"], out["moba_k_norm"] = a["moba_q_norm"][0], a["moba_k_norm"][0]
    out["nsa_q_norm"], out["nsa_k_norm"] = a["nsa_q_norm"][0], a["nsa_k_norm"][0]
    out["cmp_pos"] = a["nsa_cmp_pos"][0].transpose(2, 0, 1)
    out["cmp_w1"] = a["nsa_cmp_w1"][0].transpose(0, 2, 1, 3)
    out["cmp_w2"] = a["nsa_cmp_w2"][0].reshape(2, 2, P, HEAD).transpose(2, 0, 1, 3)
    out["diff_w_in"], out["diff_w_out"] = _column_tiles(a["diff_w_in"][0]), _column_tiles(a["diff_w_out"][0])
    out["diff_q_norm"], out["diff_k_norm"] = a["diff_q_norm"][0], a["diff_k_norm"][0]
    out["diff_lambda"], out["diff_out_norm"] = a["diff_lambda"][0].reshape(-1), a["diff_out_norm"][0]
    out["ada_w2"], out["ada_b2"] = _column_tiles(a["ada_w_2"][0], CW // 2).reshape(24, P, KT, CW // 2), a["ada_b_2"][0]
    out["c2"], out["c_ctx2"] = a["c_2"].reshape(KT, P).T, a["c_ctx_2"].reshape(KT, P).T
    out["ctx"], out["norm_g2"] = a["ctx_2"][0], a["norm_g_2"][0]
    dn = a["dn_w_in_2"][0]
    out["dn_w_qkv"] = _column_tiles(dn[:, :3 * D])
    out["dn_w_gate"] = _column_tiles(dn[:, 3 * D:4 * D])
    out["dn_w_ba"] = _column_tiles(dn[:, 4 * D:], 4 * DN_HEADS)[0]
    out["dn_conv"] = a["dn_conv_w_2"][0].reshape(DN_CONV, 3 * KT, P).transpose(2, 1, 0)
    out["dn_a_log"], out["dn_dt_bias"] = a["dn_a_log_2"][0].reshape(-1), a["dn_dt_bias_2"][0].reshape(-1)
    out["dn_norm_g"], out["dn_w_out"] = a["dn_norm_g_2"][0], _column_tiles(a["dn_w_out_2"][0])
    out["peer_w_q"] = _column_tiles(a["peer_w_q_2"][0])
    out["peer_keys"] = a["peer_keys_2"][0].reshape(16, NKEYS, P).transpose(2, 0, 1)
    out["peer_u"] = a["peer_u_2"][0].reshape(NKEYS, NKEYS, KT, P).transpose(1, 3, 2, 0).reshape(NKEYS, P, KT * P)
    out["peer_v"] = a["peer_v_2"][0].reshape(NKEYS, NKEYS, D).transpose(1, 0, 2)
    out["final_g"] = a["final_g_2"]
    return {name: np.ascontiguousarray(v) for name, v in out.items()}


def kernel(**inputs):
    import concourse.bacc as _bacc
    from concourse.bass_utils import run_bass_kernel_spmd as _run

    nc = _bacc.Bacc("TRN2", target_bir_lowering=False, num_devices=1)
    arrays, aps = {}, {}
    for name, a in _layout(inputs).items():
        arrays[f"in_{name}"] = a
        aps[name] = nc.dram_tensor(f"in_{name}", a.shape, mybir.dt.from_np(a.dtype), kind="ExternalInput").ap()
    out = nc.dram_tensor("out_x", (S, D), F32, kind="ExternalOutput").ap()
    program(nc, aps, out)
    r = _run(nc, [arrays], core_ids=[0])
    return r.results[0]["out_x"].reshape(1, S, D)
```

```python
import math
from contextlib import ExitStack

import concourse.bass as bass
import numpy as np
from concourse import mybir

ALU = mybir.AluOpType
ACT = mybir.ActivationFunctionType
AX = mybir.AxisListType
F32 = mybir.dt.float32
F32R = mybir.dt.float32r
I32 = mybir.dt.int32
U32 = mybir.dt.uint32

P = 128
D = 1024
KT = D // P
S = 256
TT = S // P
EPS = 1e-6
NEG = -1e30
CW = 512
WIDE = CW // 2

HEAD = 64
ROT = HEAD // 4
HALF = ROT // 2
ROPE_THETA = 500000.0
HEADS = 8
FFN = 2816
FFN_CHUNKS = FFN // P

CMP_LEN, CMP_STRIDE, CMP_HIDDEN = 32, 16, 256
NCMP = (S - CMP_LEN) // CMP_STRIDE + 1
SP_IN = 2840
Z_MQ, Z_MK, Z_MV, Z_NQ, Z_KV, Z_GATE = 0, 512, 1024, 1536, 2048, 2816
KV_BRANCH, KV_VALUE = 256, 128

DIFF_LAM_INIT = 0.8 - 0.6 * float(np.exp(-0.3 * 1))

DN_HEADS = 8
DN_CONV = 5
ROW = 64
NKEYS = 128
TOPK = 16
PHEADS = 8

SC = 384


class Stage:

    def __init__(self, nc, name):
        self.nc, self.name, self.stack, self.sems = nc, name, ExitStack(), []

    def __enter__(self):
        self.stack.callback(self.clear)
        return self

    def clear(self):
        for sem in self.sems:
            self.nc.gpsimd.sem_clear(sem)
            self.nc.release_semaphore(sem)

    def __exit__(self, *error):
        return self.stack.__exit__(*error)

    def sb(self, name, shape, dtype=F32):
        return self.stack.enter_context(self.nc.sbuf_tensor(f"{self.name}_{name}", shape, dtype))

    def ps(self, name, shape):
        return self.stack.enter_context(self.nc.psum_tensor(f"{self.name}_{name}", shape, F32))

    def sem(self, name):
        self.sems.append(self.nc.alloc_semaphore(f"{self.name}_{name}"))
        return self.sems[-1]

    def block(self):
        self.engines = self.stack.enter_context(ExitStack())
        return self.engines.enter_context(self.nc.Block())

    def end_block(self):
        self.engines.close()


class InOrder:

    def __init__(self, engine, done):
        self.engine, self.done, self.n = engine, done, 0

    def __call__(self, instruction):
        instruction.then_inc(self.done, 1)
        self.n += 1
        self.engine.wait_ge(self.done, self.n)


class Counted:

    def __init__(self, engine, done):
        self.engine, self.done, self.n = engine, done, 0

    def at(self, instruction):
        instruction.then_inc(self.done, 1)
        self.n += 1
        return self.n

    def wait(self, n):
        if n:
            self.engine.wait_ge(self.done, n)


def constants(nc, pst, ins, k):
    k.update({
        "causal": pst.sb("causal", [P, SC]),
        "incl": pst.sb("incl", [P, 2, P]),
        "strict": pst.sb("strict", [P, 2, P]),
        "decay_mask": pst.sb("decay_mask", [P, 2, P]),
        "cmp_mask": pst.sb("cmp_mask", [P, TT, NCMP]),
        "cmp_valid": pst.sb("cmp_valid", [P, TT, NCMP]),
        "cos": pst.sb("cos", [P, TT, HALF]),
        "sin": pst.sb("sin", [P, TT, HALF]),
        "silu_c": pst.sb("silu_c", [P, 3, KT]),
        "x": pst.sb("x", [P, TT, D]),
    })
    with Stage(nc, "const") as st:
        pos_i = st.sb("pos_i", [P, TT], I32)
        pos = st.sb("pos", [P, TT])
        freq = st.sb("freq", [P, HALF])
        ang = st.sb("ang", [P, TT, HALF])
        turns = st.sb("turns", [P, TT, HALF])
        rest = st.sb("rest", [P, 2, TT, HALF])
        loaded, c_loaded, filled, freq_set, reduced, tables, dve_done = (
            st.sem(n) for n in ("loaded", "c_loaded", "filled", "freq_set", "reduced", "tables", "dve_done"))
        block = st.block()

        @block.sync
        def _(sp):
            sp.dma_start(k["x"][:], ins["x"].rearrange("(t p) d -> p t d", p=P)).then_inc(loaded, 16)
            sp.dma_start(pos_i[:], ins["positions"]).then_inc(loaded, 16)
            for v, name in enumerate(("c", "c2", "c_ctx2")):
                sp.dma_start(k["silu_c"][:, v, :], ins[name]).then_inc(c_loaded, 16)
            sp.wait_ge(loaded, 32)

        @block.gpsimd
        def _(pool):
            step = InOrder(pool, filled)
            for c in range(HALF):
                inv = np.float32(1.0) / np.float32(ROPE_THETA) ** np.float32(2 * c / ROT)
                pool.memset(freq[:, c:c + 1], float(inv)).then_inc(freq_set, 1)
            step(pool.memset(k["ident"][:], 0.0))
            step(pool.affine_select(out=k["ident"][:], in_=k["ident"][:], compare_op=ALU.not_equal, fill=1.0,
                                    base=0, pattern=[[-1, P]], channel_multiplier=1))
            step(pool.memset(k["ones"][:], 1.0))
            step(pool.iota(k["iota"][:], pattern=[[1, P]], base=0, channel_multiplier=0,
                           allow_small_or_imprecise_dtypes=True))
            step(pool.memset(k["causal"][:], 0.0))
            for lo, base in ((0, 0), (P, P)):
                width = P if lo == 0 else S
                step(pool.affine_select(out=k["causal"][:, lo:lo + width], in_=k["causal"][:, lo:lo + width],
                                        compare_op=ALU.is_ge, fill=NEG, base=base, pattern=[[-1, width]],
                                        channel_multiplier=1))
            for d, sign in ((0, 1), (1, -1)):
                for name, base, fill, start in (("incl", 0, 0.0, 1.0), ("strict", -1, 0.0, 1.0),
                                                ("decay_mask", 0, NEG, 0.0)):
                    v = k[name][:, d, :]
                    step(pool.memset(v, start))
                    step(pool.affine_select(out=v, in_=v, compare_op=ALU.is_ge, fill=fill, base=base,
                                            pattern=[[sign, P]], channel_multiplier=-sign))
            for name, fill, start in (("cmp_mask", NEG, 0.0), ("cmp_valid", 0.0, 1.0)):
                step(pool.memset(k[name][:], start))
                for t in range(TT):
                    step(pool.affine_select(out=k[name][:, t, :], in_=k[name][:, t, :], compare_op=ALU.is_ge,
                                            fill=fill, base=t * P - (CMP_LEN - 1), pattern=[[-CMP_STRIDE, NCMP]],
                                            channel_multiplier=1))

        @block.vector
        def _(dve):
            step = InOrder(dve, dve_done)
            two_pi = 2 * math.pi
            hi = float(np.float32(6.28125))
            mid = float(np.float32(two_pi - hi))
            lo = two_pi - hi - mid
            magic = 1.5 * 2.0 ** 23
            dve.wait_ge(loaded, 32)
            dve.wait_ge(freq_set, HALF)
            step(dve.tensor_copy(pos[:], pos_i[:]))
            step(dve.tensor_tensor(ang[:], pos[:].unsqueeze(2).broadcast_to([P, TT, HALF]),
                                   freq[:].unsqueeze(1).broadcast_to([P, TT, HALF]), ALU.mult))
            for n, shift in ((0, 0.0), (1, 0.25)):
                step(dve.tensor_scalar(turns[:], ang[:], 1 / two_pi, shift, ALU.mult, ALU.add))
                step(dve.tensor_scalar(turns[:], turns[:], magic, None, ALU.add))
                step(dve.tensor_scalar(turns[:], turns[:], -magic, None, ALU.add))
                r = rest[:, n]
                step(dve.scalar_tensor_tensor(r, turns[:], -hi, ang[:], ALU.mult, ALU.add))
                step(dve.scalar_tensor_tensor(r, turns[:], -mid, r, ALU.mult, ALU.add))
                step(dve.scalar_tensor_tensor(r, turns[:], -lo, r, ALU.mult, ALU.add))
                step(dve.tensor_scalar(r, r, shift * two_pi, None, ALU.add))
                step(dve.tensor_scalar(r, r, 3.1415925, -3.1415925, ALU.min, ALU.max))
            dve.tensor_copy(turns[:], rest[:, 0]).then_inc(reduced, 1)

        @block.scalar
        def _(act):
            act.wait_ge(c_loaded, 48)
            act.activation(k["silu_c"][:], k["silu_c"][:], ACT.Silu).then_inc(tables, 1)
            act.wait_ge(reduced, 1)
            act.activation(k["sin"][:], rest[:, 0], ACT.Sin).then_inc(tables, 1)
            act.activation(k["cos"][:], rest[:, 1], ACT.Sin).then_inc(tables, 1)
            act.wait_ge(tables, 3)


class Modulation:

    def __init__(self, nc, k, st, weights, bias, vectors, first=0):
        self.nc, self.k, self.weights, self.bias, self.vectors, self.first = nc, k, weights, bias, vectors, first
        self.w = st.sb("ada_w", [P, 2, KT, CW // 2])
        self.w_loaded = [st.sem(f"ada_w_loaded{i}") for i in range(2)]
        self.folded = st.sem("ada_folded")
        self.step_done = st.sem("ada_step_done")

    def load(self, sp, half, slot, early=False):
        if not early:
            sp.wait_ge(self.folded, half - (self.first + 1))
        source = self.weights[half] if isinstance(half, int) else \
            self.weights[bass.ds(half, 1)].rearrange("a p c n -> p (a c) n")
        sp.dma_start(self.w[:, slot], source).then_inc(self.w_loaded[slot], 16)

    def fold(self, dve, half, slot, steps_before, rounds_before):
        dve.wait_ge(self.w_loaded[slot], 16 * rounds_before + 16)
        n = 0
        for silu_c, row, _ in [v for v in self.vectors if not isinstance(half, int) or half < 2 * v[2]]:
            if not isinstance(half, int) and row is not self.vectors[0][1]:
                continue
            width = CW // 2
            acc = row[:, half * width:(half + 1) * width] if isinstance(half, int) else \
                row[:, bass.ds(half * width, width)]
            for c in range(KT):
                if c == 0:
                    last = dve.tensor_scalar(acc, self.w[:, slot, c, :], silu_c[:, c:c + 1], None, ALU.mult)
                else:
                    dve.wait_ge(self.step_done, steps_before + n)
                    last = dve.scalar_tensor_tensor(acc, self.w[:, slot, c, :], silu_c[:, c:c + 1], acc, ALU.mult,
                                                    ALU.add)
                last.then_inc(self.step_done, 1)
                n += 1
        dve.wait_ge(self.step_done, steps_before + n)
        dve.sem_inc(self.folded, 1)
        return n


def finish_modulation(nc, k, name, bias, rows):
    jobs = [(row, j) for row, lo, hi in rows for j in range(lo, hi)]
    with Stage(nc, name) as st:
        b = st.sb("b", [P, 6 * D])
        psum = st.ps("psum", [P, 4, CW])
        loaded = [st.sem(f"loaded{i}") for i in range(len(jobs))]
        summed, added = st.sem("summed"), st.sem("added")
        block = st.block()

        @block.sync
        def _(sp):
            for n, (row, j) in enumerate(jobs):
                cols = slice(j * CW, (j + 1) * CW)
                if (row, j) == jobs[n] and j not in [x for _, x in jobs[:n]]:
                    sp.dma_start(b[:, cols], bias[cols].partition_broadcast(P)).then_inc(loaded[n], 16)

        @block.tensor
        def _(pe):
            for n, (row, j) in enumerate(jobs):
                if n >= 4:
                    pe.wait_ge(added, n - 3)
                pe.matmul(psum[:, n % 4, :], k["ones"][:], row[:, j * CW:(j + 1) * CW], start=True,
                          stop=True).then_inc(summed, 1)

        @block.vector
        def _(dve):
            first_use = {}
            for n, (row, j) in enumerate(jobs):
                first_use.setdefault(j, n)
                cols = slice(j * CW, (j + 1) * CW)
                dve.wait_ge(loaded[first_use[j]], 16)
                dve.wait_ge(summed, n + 1)
                dve.tensor_tensor(row[:, cols], psum[:, n % 4, :], b[:, cols], ALU.add).then_inc(added, 1)


def first_modulation(nc, k, name, weights, silu_c, row, halves):
    with Stage(nc, name) as st:
        ring = 4
        width = CW // 2
        w = st.sb("w", [P, ring, KT, width])
        cb = st.sb("cb", [P, KT, P])
        b = st.sb("b", [P, halves * width])
        psum = st.ps("psum", [P, 4, CW])
        slot_loaded = [st.sem(f"slot_loaded{i}") for i in range(ring)]
        c_ready, product, added, b_loaded = (st.sem(n) for n in ("c_ready", "product", "added", "b_loaded"))
        source, bias = weights
        block = st.block()

        @block.sync
        def _(sp):
            for j in range(halves):
                if j >= ring:
                    sp.wait_ge(product, j - ring + 1)
                sp.dma_start(w[:, j % ring], source[j]).then_inc(slot_loaded[j % ring], 16)

        @block.scalar
        def _(act):
            act.dma_start(b[:], bias[0:halves * width].partition_broadcast(P)).then_inc(b_loaded, 16)

        @block.vector
        def _(dve):
            dve.tensor_copy(cb[:], silu_c.unsqueeze(2).broadcast_to([P, KT, P])).then_inc(c_ready, 1)
            dve.wait_ge(b_loaded, 16)
            for n in range(halves):
                cols = slice(n * width, (n + 1) * width)
                dve.wait_ge(product, n + 1)
                dve.tensor_tensor(row[:, cols], psum[:, n % 4, 0:width], b[:, cols], ALU.add).then_inc(added, 1)

        @block.tensor
        def _(pe):
            pe.wait_ge(c_ready, 1)
            for n in range(halves):
                pe.wait_ge(slot_loaded[n % ring], 16 * (n // ring + 1))
                if n >= 4:
                    pe.wait_ge(added, n - 3)
                for t in range(KT):
                    last = pe.matmul(psum[:, n % 4, 0:width], cb[:, t, :], w[:, n % ring, t, :],
                                     start=(t == 0), stop=(t == KT - 1))
                last.then_inc(product, 1)


def normed(nc, k, name, x, gain, shift, scale, out_t):
    with Stage(nc, name) as st:
        g = st.sb("gain", [P, D])
        h = st.sb("h", [P, TT, D])
        junk = st.sb("junk", [P, D])
        ss = st.sb("ss", [P, TT])
        psum = st.ps("psum", [P, 4, CW])
        loaded, squared, mean_ready, root_ready, h_ready, turned, copied, dve_done, psum_copied = (
            st.sem(n) for n in ("loaded", "squared", "mean_ready", "root_ready", "h_ready", "turned",
                                "copied", "dve_done", "psum_copied"))
        block = st.block()
        groups = [(t, half) for t in range(TT) for half in range(2)]

        @block.sync
        def _(sp):
            sp.dma_start(g[:], gain.partition_broadcast(P)).then_inc(loaded, 16)

        @block.scalar
        def _(act):
            for t in range(TT):
                act.activation(junk[:], x[:, t, :], ACT.Square, accum_out=ss[:, t:t + 1]).then_inc(squared, 1)
                act.wait_ge(squared, t + 1)
            act.wait_ge(mean_ready, 1)
            act.activation(ss[:], ss[:], ACT.Sqrt).then_inc(root_ready, 1)
            for n in (1, 3):
                t, half = groups[n]
                act.wait_ge(turned, n + 1)
                act.copy(out_t[:, 4 * half:4 * half + 4, t * P:(t + 1) * P],
                         psum[:, n, :].rearrange("p (c q) -> p c q", c=4)).then_inc(psum_copied, 1)

        @block.vector
        def _(dve):
            step = InOrder(dve, dve_done)
            dve.wait_ge(loaded, 16)
            if scale is not None:
                step(dve.scalar_tensor_tensor(g[:], scale, 1.0, g[:], ALU.add, ALU.mult))
            dve.wait_ge(squared, TT)
            dve.tensor_scalar(ss[:], ss[:], 1.0 / D, EPS, ALU.mult, ALU.add).then_inc(mean_ready, 1)
            dve.wait_ge(root_ready, 1)
            step(dve.reciprocal(ss[:], ss[:]))
            for t in range(TT):
                step(dve.scalar_tensor_tensor(h[:, t, :], x[:, t, :], ss[:, t:t + 1], g[:], ALU.mult, ALU.mult))
                dve.tensor_tensor(h[:, t, :], h[:, t, :], shift, ALU.add).then_inc(h_ready, 1)
            for n in (0, 2):
                t, half = groups[n]
                dve.wait_ge(turned, n + 1)
                dve.tensor_copy(out_t[:, 4 * half:4 * half + 4, t * P:(t + 1) * P],
                                psum[:, n, :].rearrange("p (c q) -> p c q", c=4)).then_inc(copied, 1)

        @block.tensor
        def _(pe):
            for n, (t, half) in enumerate(groups):
                pe.wait_ge(h_ready, t + 1)
                for c in range(4):
                    last = pe.transpose(psum[:, n, c * P:(c + 1) * P],
                                        h[:, t, (4 * half + c) * P:(4 * half + c + 1) * P], k["ident"][:])
                last.then_inc(turned, 1)


def turn(nc, k, name, z, blocks, out_t):
    with Stage(nc, name) as st:
        banks = 6
        psum = st.ps("psum", [P, banks, CW])
        turned, copied = st.sem("turned"), st.sem("copied")
        moved = st.sem("moved")
        pairs = [blocks[i:i + 2] for i in range(0, len(blocks), 2)]
        block = st.block()

        def bank_free(pe, n):
            if n >= banks:
                prior = n - banks
                pe.wait_ge(copied if prior % 2 == 0 else moved, prior // 2 + 1)

        def source(n):
            w = len(pairs[n])
            return (out_t[:, 2 * n:2 * n + w, :],
                    psum[:, n % banks, 0:w * S].rearrange("p (b q) -> p b q", b=w))

        @block.tensor
        def _(pe):
            for n, pair in enumerate(pairs):
                bank_free(pe, n)
                for b, col in enumerate(pair):
                    for t in range(TT):
                        last = pe.transpose(psum[:, n % banks, b * S + t * P:b * S + (t + 1) * P],
                                            z[:, t, col:col + P], k["ident"][:])
                last.then_inc(turned, 1)

        @block.vector
        def _(dve):
            for n in range(0, len(pairs), 2):
                dve.wait_ge(turned, n + 1)
                dve.tensor_copy(*source(n)).then_inc(copied, 1)

        @block.scalar
        def _(act):
            for n in range(1, len(pairs), 2):
                act.wait_ge(turned, n + 1)
                act.copy(*source(n)).then_inc(moved, 1)


def project(nc, k, name, h_t, chunks, residual=None, out=None, ada=None):
    with Stage(nc, name) as st:
        beside = Modulation(nc, k, st, ada[0], None, ada[1], first=ada[2]) if ada else None
        halves = list(range(ada[2], ada[3])) if ada else []
        ring = 3
        h_hi, h_lo = k["h_hi"], k["h_lo"]
        w = st.sb("w", [P, ring, KT * WIDE])
        w_hi, w_lo = (st.sb(n, [P, 2, KT * WIDE], F32R) for n in ("w_hi", "w_lo"))
        tmp = st.sb("tmp", [P, 2, WIDE])
        psum = st.ps("psum", [P, 4, CW])
        slot_loaded = [st.sem(f"slot_loaded{i}") for i in range(ring)]
        h_hi_ready, h_split, w_hi_ready, w_split, product, taken, scaled, moved = (st.sem(n) for n in (
            "h_hi_ready", "h_split", "w_hi_ready", "w_split", "product", "taken", "scaled", "moved"))
        jobs = [(j, t) for j in range(len(chunks)) for t in range(TT)]
        block = st.block()

        def halves_at(j, of):
            return range(j * len(halves) // of, (j + 1) * len(halves) // of)

        def low_w(engine, j):
            engine.wait_ge(w_hi_ready, j + 1)
            n = KT * chunks[j][2]
            engine.tensor_tensor(w_lo[:, j % 2, 0:n], w[:, j % ring, 0:n], w_hi[:, j % 2, 0:n].bitcast(F32),
                                 ALU.subtract).then_inc(w_split, 1)

        @block.sync
        def _(sp):
            for j, (source, col, width) in enumerate(chunks):
                if j >= ring:
                    sp.wait_ge(w_split, j - ring + 1)
                sp.dma_start(w[:, j % ring, 0:KT * width], source).then_inc(slot_loaded[j % ring], 16)
                for n in halves_at(j, len(chunks)):
                    beside.load(sp, halves[n], n % 2, early=(n < 2))

        @block.tensor
        def _(pe):
            pe.wait_ge(h_split, KT // 2)
            for n, (j, t) in enumerate(jobs):
                width = chunks[j][2]
                pe.wait_ge(w_split, j + 1)
                if n >= 4 and residual is not None:
                    pe.wait_ge(scaled, n - 3)
                if n >= 4 and residual is None:
                    pe.wait_ge(taken if n % 2 == 0 else moved, n // 2 - 1)
                bank = psum[:, n % 4, 0:width]
                for c in range(KT):
                    cols, tokens = slice(c * width, (c + 1) * width), slice(t * P, (t + 1) * P)
                    pe.matmul(bank, h_hi[:, c, tokens], w_hi[:, j % 2, cols], start=(c == 0), stop=False)
                    pe.matmul(bank, h_hi[:, c, tokens], w_lo[:, j % 2, cols], start=False, stop=False)
                    last = pe.matmul(bank, h_lo[:, c, tokens], w_hi[:, j % 2, cols], start=False, stop=(c == KT - 1))
                last.then_inc(product, 1)

        if ada:
            @block.gpsimd
            def _(pool):
                for j in range(len(chunks)):
                    low_w(pool, j)

        @block.vector
        def _(dve):
            for c in range(0, KT, 2):
                dve.wait_ge(h_hi_ready, c // 2 + 1)
                dve.tensor_tensor(h_lo[:, c:c + 2, :], h_t[:, c:c + 2, :], h_hi[:, c:c + 2, :].bitcast(F32),
                                  ALU.subtract).then_inc(h_split, 1)
            if not ada:
                low_w(dve, 0)
            steps = 0
            for n, (j, t) in enumerate(jobs):
                if not ada and t == 0 and j + 1 < len(chunks):
                    low_w(dve, j + 1)
                for m in halves_at(n, len(jobs)):
                    steps += beside.fold(dve, halves[m], m % 2, steps, m // 2)
                col, width = chunks[j][1:]
                if residual is None:
                    if n % 2 == 0:
                        dve.wait_ge(product, n + 1)
                        dve.tensor_copy(out[:, t, col:col + width], psum[:, n % 4, 0:width]).then_inc(taken, 1)
                    continue
                x, gate = residual
                dve.wait_ge(product, n + 1)
                if n >= 2:
                    dve.wait_ge(taken, n - 1)
                dve.tensor_tensor(tmp[:, n % 2, 0:width], psum[:, n % 4, 0:width], gate[:, col:col + width],
                                  ALU.mult).then_inc(scaled, 1)
                dve.wait_ge(scaled, n + 1)
                dve.tensor_tensor(x[:, t, col:col + width], x[:, t, col:col + width], tmp[:, n % 2, 0:width],
                                  ALU.add).then_inc(taken, 1)

        @block.scalar
        def _(act):
            def high_w(j):
                act.wait_ge(slot_loaded[j % ring], 16 * (j // ring + 1))
                if j >= 2:
                    act.wait_ge(product, TT * (j - 1))
                n = KT * chunks[j][2]
                act.copy(w_hi[:, j % 2, 0:n], w[:, j % ring, 0:n]).then_inc(w_hi_ready, 1)

            for c in range(0, KT, 2):
                act.copy(h_hi[:, c:c + 2, :], h_t[:, c:c + 2, :]).then_inc(h_hi_ready, 1)
            high_w(0)
            for n, (j, t) in enumerate(jobs):
                if t == 0 and j + 1 < len(chunks):
                    high_w(j + 1)
                col, width = chunks[j][1:]
                if residual is None and n % 2 == 1:
                    act.wait_ge(product, n + 1)
                    act.copy(out[:, t, col:col + width], psum[:, n % 4, 0:width]).then_inc(moved, 1)


def head_norm_rope(nc, k, name, z, segments):
    with Stage(nc, name) as st:
        total = sum(n for _, n, _ in segments)
        most = max(n for _, n, _ in segments)
        sq = st.sb("sq", [P, TT, most, HEAD])
        ss = st.sb("ss", [P, TT, total])
        gains = st.sb("gains", [P, len(segments), HEAD])
        rot = [st.sb(f"rot{i}", [P, TT, most, HALF]) for i in range(4)]
        loaded, mean_ready, root_ready, dve_done = (
            st.sem(n) for n in ("loaded", "mean_ready", "root_ready", "dve_done"))
        block = st.block()

        @block.sync
        def _(sp):
            for s, (_, _, gain) in enumerate(segments):
                sp.dma_start(gains[:, s, :], gain.partition_broadcast(P)).then_inc(loaded, 16)

        @block.scalar
        def _(act):
            act.wait_ge(mean_ready, 1)
            act.activation(ss[:], ss[:], ACT.Sqrt).then_inc(root_ready, 1)

        @block.vector
        def _(dve):
            step = InOrder(dve, dve_done)

            def heads(s):
                col, n, _ = segments[s]
                return z[:, :, col:col + n * HEAD].rearrange("p t (n d) -> p t n d", d=HEAD)

            at = 0
            for s, (_, n, _) in enumerate(segments):
                step(dve.tensor_tensor(sq[:, :, 0:n, :], heads(s), heads(s), ALU.mult))
                step(dve.tensor_reduce(ss[:, :, at:at + n], sq[:, :, 0:n, :], AX.X, ALU.add))
                at += n
            dve.tensor_scalar(ss[:], ss[:], 1.0 / HEAD, EPS, ALU.mult, ALU.add).then_inc(mean_ready, 1)
            dve.wait_ge(loaded, 16 * len(segments))
            dve.wait_ge(root_ready, 1)
            step(dve.reciprocal(ss[:], ss[:]))
            at = 0
            for s, (_, n, _) in enumerate(segments):
                v = heads(s)
                rs = ss[:, :, at:at + n].unsqueeze(3).broadcast_to([P, TT, n, HEAD])
                at += n
                step(dve.tensor_tensor(v, v, rs, ALU.mult))
                for t in range(TT):
                    g = gains[:, s, :].unsqueeze(1).broadcast_to([P, n, HEAD])
                    step(dve.tensor_tensor(v[:, t], v[:, t], g, ALU.mult))
                t1, t2 = v[:, :, :, 0:HALF], v[:, :, :, HALF:ROT]
                cos = k["cos"][:].unsqueeze(2).broadcast_to([P, TT, n, HALF])
                sin = k["sin"][:].unsqueeze(2).broadcast_to([P, TT, n, HALF])
                for r, (a, b) in enumerate(((t1, cos), (t2, sin), (t2, cos), (t1, sin))):
                    step(dve.tensor_tensor(rot[r][:, :, 0:n, :], a, b, ALU.mult))
                step(dve.tensor_tensor(t1, rot[0][:, :, 0:n, :], rot[1][:, :, 0:n, :], ALU.subtract))
                step(dve.tensor_tensor(t2, rot[2][:, :, 0:n, :], rot[3][:, :, 0:n, :], ALU.add))


def compress(nc, k, ins, z, q_t, pc_t, vc, gates, ada):
    G = 2
    N = G * NCMP
    with Stage(nc, "cmp") as st:
        beside = Modulation(nc, k, st, ada[0], None, ada[1], first=ada[2])
        halves = list(range(ada[2], ada[3]))
        w1 = st.sb("w1", [HEAD, CMP_LEN, CMP_HIDDEN])
        w2 = st.sb("w2", [P, 2, 2, HEAD])
        pos_t = st.sb("pos_t", [HEAD, 2, CMP_LEN])
        tok_t = st.sb("tok_t", [HEAD, 2, G, S])
        blk = st.sb("blk", [HEAD, 2, CMP_LEN, N])
        hid = st.sb("hid", [P, 2, 2, N])
        kc_t = st.sb("kc_t", [P, G, NCMP])
        sc = st.sb("sc", [P, TT, HEADS, NCMP])
        mx = st.sb("mx", [P, TT, HEADS])
        sm = st.sb("sm", [P, TT, HEADS])
        pt = [st.ps(f"pt{i}", [P, CW]) for i in range(2)]
        ph = st.ps("ph", [P, 2, CW])
        pk = st.ps("pk", [P, CW])
        pv = st.ps("pv", [P, CW])
        psc = st.ps("psc", [P, CW])
        w1_loaded = [st.sem(f"w1_loaded{e}") for e in range(2)]
        loaded, e_sum, turned, tok_ready, blk_ready, hid_ready, small, kv_ready, scored, \
            shifted, exped, gate_e, p_ready, p_turned, p_half, dve_done = (st.sem(n) for n in (
                "loaded", "e_sum", "turned", "tok_ready", "blk_ready", "hid_ready", "small",
                "kv_ready", "scored", "shifted", "exped", "gate_e", "p_ready", "p_turned", "p_half", "dve_done"))
        block = st.block()

        @block.sync
        def _(sp):
            sp.dma_start(pos_t[:], ins["cmp_pos"]).then_inc(loaded, 16)
            sp.dma_start(w2[:], ins["cmp_w2"]).then_inc(loaded, 16)
            for kv in range(2):
                for e in range(2):
                    cols = slice(e * P, (e + 1) * P)
                    if kv:
                        sp.wait_ge(e_sum, e + 1)
                    sp.dma_start(w1[:, :, cols], ins["cmp_w1"][kv][:, :, cols]).then_inc(w1_loaded[e], 16)
                for half in halves[kv:kv + 1]:
                    beside.load(sp, half, half % 2, early=True)
            for half in halves[2:]:
                beside.load(sp, half, half % 2)

        @block.tensor
        def _(pe):
            for kv in range(2):
                for g in range(G):
                    for t in range(TT):
                        col = Z_KV + kv * KV_VALUE + g * HEAD
                        last = pe.transpose(pt[kv][0:HEAD, g * S + t * P:g * S + (t + 1) * P],
                                            z[:, t, col:col + HEAD], k["ident"][:])
                last.then_inc(turned, 1)
            pe.wait_ge(blk_ready, 2 * G)
            for kv in range(2):
                for e in range(2):
                    pe.wait_ge(w1_loaded[e], 16 * (kv + 1))
                    for l in range(CMP_LEN):
                        last = pe.matmul(ph[:, kv, e * N:(e + 1) * N], w1[:, l, e * P:(e + 1) * P],
                                         blk[:, kv, l, :], start=(l == 0), stop=(l == CMP_LEN - 1))
                    last.then_inc(e_sum, 1)
            pe.wait_ge(hid_ready, 2)
            pe.wait_ge(loaded, 32)
            for g in range(G):
                for e in range(2):
                    pe.matmul(pk[g * HEAD:(g + 1) * HEAD, 0:NCMP], w2[:, 0, e, :],
                              hid[:, 0, e, g * NCMP:(g + 1) * NCMP], start=(e == 0), stop=(e == 1))
            for g in range(G):
                for e in range(2):
                    last = pe.matmul(pv[0:NCMP, g * HEAD:(g + 1) * HEAD], hid[:, 1, e, g * NCMP:(g + 1) * NCMP],
                                     w2[:, 1, e, :], start=(e == 0), stop=(e == 1))
            last.then_inc(small, 1)
            pe.wait_ge(kv_ready, G + 1)
            for t in range(TT):
                for b in range(HEADS // G):
                    at = (t * HEADS + b * G) * NCMP
                    last = pe.matmul(psc[:, at:at + N], q_t[:, b, t * P:(t + 1) * P],
                                     kc_t[:].rearrange("p g n -> p (g n)"), start=True, stop=True)
            last.then_inc(scored, 1)
            pe.wait_ge(p_ready, 1)
            for quarter in range(4):
                if quarter >= 2:
                    pe.wait_ge(p_half, quarter - 1)
                for h in (2 * quarter, 2 * quarter + 1):
                    for t in range(TT):
                        last = pe.transpose(pt[quarter % 2][0:NCMP, (h % 2) * S + t * P:(h % 2) * S + (t + 1) * P],
                                            sc[:, t, h, :], k["ident"][:])
                last.then_inc(p_turned, 1)

        @block.scalar
        def _(act):
            act.activation(gates[:], z[:, :, Z_GATE:Z_GATE + 3 * HEADS], ACT.Exp, scale=-1.0).then_inc(gate_e, 1)
            for kv in range(2):
                act.wait_ge(e_sum, 2 * (kv + 1))
                act.activation(hid[:, kv].rearrange("p e n -> p (e n)"), ph[:, kv, 0:2 * N],
                               ACT.Silu).then_inc(hid_ready, 1)
            act.wait_ge(shifted, 1)
            act.activation(sc[:], sc[:], ACT.Exp).then_inc(exped, 1)

        @block.vector
        def _(dve):
            step = InOrder(dve, dve_done)
            folds = 0

            def fold(first, last):
                nonlocal folds
                for n in range(first, last):
                    folds += beside.fold(dve, halves[n], halves[n] % 2, folds, n // 2)

            dve.wait_ge(gate_e, 1)
            step(dve.tensor_scalar(gates[:], gates[:], 1.0, None, ALU.add))
            step(dve.memset(kc_t[:], 0.0))
            step(dve.reciprocal(gates[:], gates[:]))
            dve.wait_ge(loaded, 32)
            for kv in range(2):
                dve.wait_ge(turned, kv + 1)
                step(dve.tensor_copy(tok_t[:, kv].rearrange("d g s -> d (g s)"), pt[kv][0:HEAD, :]))
                for g in range(G):
                    for n in range(NCMP):
                        last = dve.tensor_tensor(blk[:, kv, :, g * NCMP + n],
                                                 tok_t[:, kv, g, n * CMP_STRIDE:n * CMP_STRIDE + CMP_LEN],
                                                 pos_t[:, kv, :], ALU.add)
                    last.then_inc(blk_ready, 1)
            fold(0, 6)
            dve.wait_ge(small, 1)
            for g in range(G):
                rows = slice(g * HEAD, (g + 1) * HEAD)
                dve.tensor_copy(kc_t[rows, g, :], pk[rows, 0:NCMP]).then_inc(kv_ready, 1)
            dve.tensor_copy(vc[:].rearrange("n g d -> n (g d)"), pv[0:NCMP, 0:G * HEAD]).then_inc(kv_ready, 1)
            dve.wait_ge(scored, 1)
            for t in range(TT):
                step(dve.scalar_tensor_tensor(
                    sc[:, t], psc[:, t * HEADS * NCMP:(t + 1) * HEADS * NCMP].rearrange("p (h n) -> p h n", h=HEADS),
                    HEAD ** -0.5, k["cmp_mask"][:, t, :].unsqueeze(1).broadcast_to([P, HEADS, NCMP]),
                    ALU.mult, ALU.add))
            wide = [P, TT, HEADS, NCMP]
            step(dve.tensor_reduce(mx[:], sc[:], AX.X, ALU.max))
            dve.tensor_tensor(sc[:], sc[:], mx[:].unsqueeze(3).broadcast_to(wide), ALU.subtract).then_inc(shifted, 1)
            fold(6, 7)
            dve.wait_ge(exped, 1)
            step(dve.tensor_reduce(sm[:], sc[:], AX.X, ALU.add))
            step(dve.reciprocal(sm[:], sm[:]))
            step(dve.tensor_tensor(sm[:], sm[:], gates[:, :, 0:HEADS], ALU.mult))
            step(dve.tensor_tensor(sc[:], sc[:], k["cmp_valid"][:].unsqueeze(2).broadcast_to(wide), ALU.mult))
            dve.tensor_tensor(sc[:], sc[:], sm[:].unsqueeze(3).broadcast_to(wide), ALU.mult).then_inc(p_ready, 1)
            for quarter in range(4):
                dve.wait_ge(p_turned, quarter + 1)
                dve.tensor_copy(pc_t[:, 2 * quarter:2 * quarter + 2, :].rearrange("n h s -> n (h s)"),
                                pt[quarter % 2][0:NCMP, :]).then_inc(p_half, 1)
            fold(7, len(halves))


def sparse_attention(nc, k, z, zt, pc_t, vc, gates, o_t):
    maps = []
    for h in range(HEADS):
        maps.append((h // 2, 4 + h // 2, h % 2, Z_MV + h * HEAD, None, h // 2, "only"))
    for h in range(HEADS):
        for br, part in ((1, "first"), (2, "last")):
            maps.append((8 + h // 2, 12 + br, h % 2, Z_KV + br * KV_BRANCH + KV_VALUE + (h % 2) * HEAD,
                         (br, h), 4 + h // 2, part))
    n_maps = len(maps)
    with Stage(nc, "attn") as st:
        sc = st.sb("sc", [P, 2, SC])
        pt = st.sb("pt", [P, 2, SC])
        nm = st.sb("nm", [P, 2, TT])
        sm = st.sb("sm", [P, 2, TT])
        ps = st.ps("ps", [P, 2, CW])
        pp = st.ps("pp", [P, 2, CW])
        po = st.ps("po", [P, 2, CW])
        scored, masked, neg_max, exped, probs, turned, pt_ready, attended, stored, dve_done = (
            st.sem(n) for n in ("scored", "masked", "neg_max", "exped", "probs", "turned", "pt_ready",
                                "attended", "stored", "dve_done"))
        block = st.block()
        parts = ((0, P), (P, SC))

        @block.tensor
        def _(pe):
            def scores(i):
                q, key, half, *_ = maps[i]
                rows = slice(half * HEAD, (half + 1) * HEAD)
                if i >= 2:
                    pe.wait_ge(masked, i - 1)
                for t, (lo, hi) in enumerate(parts):
                    last = pe.matmul(ps[:, i % 2, lo:hi], zt[rows, q, t * P:(t + 1) * P],
                                     zt[rows, key, 0:hi - lo], start=True, stop=True)
                last.then_inc(scored, 1)

            def turn_probs(i):
                pe.wait_ge(probs, i + 1)
                if i >= 2:
                    pe.wait_ge(pt_ready, i - 1)
                for c in range(3):
                    last = pe.transpose(pp[:, i % 2, c * P:(c + 1) * P], sc[:, i % 2, c * P:(c + 1) * P],
                                        k["ident"][:])
                last.then_inc(turned, 1)

            def values(i):
                _, _, half, vcol, gate, dest, part = maps[i]
                rows = slice(half * HEAD, (half + 1) * HEAD)
                pe.wait_ge(pt_ready, i + 1)
                if dest >= 2 and half == 0 and part != "last":
                    pe.wait_ge(stored, dest - 1)
                o = po[rows, dest % 2, :]
                first = part != "last"
                pe.matmul(o[:, 0:S], z[:, 0, vcol:vcol + HEAD], pt[:, i % 2, 0:S], start=first, stop=False)
                last = pe.matmul(o[:, P:S], z[:, 1, vcol:vcol + HEAD], pt[:, i % 2, S:SC], start=False,
                                 stop=(part == "only"))
                if part == "last":
                    last = pe.matmul(o[:, 0:S], vc[:, half, :], pc_t[:, gate[1], :], start=False, stop=True)
                last.then_inc(attended, 1)

            for i in range(n_maps + 2):
                if i < n_maps:
                    scores(i)
                if 1 <= i <= n_maps:
                    turn_probs(i - 1)
                if i >= 2:
                    values(i - 2)

        ends = [i for i, m in enumerate(maps) if m[2] == 1 and m[6] != "first"]

        @block.vector
        def _(dve):
            step = InOrder(dve, dve_done)

            def mask(i):
                dve.wait_ge(scored, i + 1)
                if i >= 2:
                    dve.wait_ge(turned, i - 1)
                s = sc[:, i % 2, :]
                dve.scalar_tensor_tensor(s, ps[:, i % 2, 0:SC], HEAD ** -0.5, k["causal"][:], ALU.mult,
                                         ALU.add).then_inc(masked, 1)
                dve.wait_ge(masked, i + 1)
                for t, (lo, hi) in enumerate(parts):
                    dve.tensor_reduce(nm[:, i % 2, t:t + 1], s[:, lo:hi], AX.X, ALU.max,
                                      negate=True).then_inc(neg_max, 1)

            def scale(i):
                dve.wait_ge(exped, 2 * i + 2)
                r = sm[:, i % 2, :]
                step(dve.reciprocal(r, r))
                if maps[i][4]:
                    br, h = maps[i][4]
                    step(dve.tensor_tensor(r, r, gates[:, :, br * HEADS + h], ALU.mult))
                for t, (lo, hi) in enumerate(parts):
                    last = dve.tensor_scalar(sc[:, i % 2, lo:hi], sc[:, i % 2, lo:hi], sm[:, i % 2, t:t + 1], None,
                                             ALU.mult)
                last.then_inc(probs, 1)

            for i in range(n_maps + 1):
                if i < n_maps:
                    mask(i)
                if i >= 1:
                    scale(i - 1)

        @block.scalar
        def _(act):
            def exp(i):
                for t, (lo, hi) in enumerate(parts):
                    act.wait_ge(neg_max, 2 * i + t + 1)
                    act.activation(sc[:, i % 2, lo:hi], sc[:, i % 2, lo:hi], ACT.Exp, bias=nm[:, i % 2, t:t + 1],
                                   accum_out=sm[:, i % 2, t:t + 1]).then_inc(exped, 1)

            def move_probs(i):
                act.wait_ge(turned, i + 1)
                if i >= 2:
                    act.wait_ge(attended, i - 1)
                act.copy(pt[:, i % 2, :], pp[:, i % 2, 0:SC]).then_inc(pt_ready, 1)

            def store(i):
                if i in ends:
                    n = ends.index(i)
                    act.wait_ge(attended, i + 1)
                    act.copy(o_t[:, n, :], po[:, n % 2, 0:S]).then_inc(stored, 1)

            for i in range(n_maps + 2):
                if i < n_maps:
                    exp(i)
                if 1 <= i <= n_maps:
                    move_probs(i - 1)
                if i >= 2:
                    store(i - 2)


def streamed_mlp(nc, k, name, columns, rows, kind, h_split, residual=None, kept=None, table=None, ada=None,
                 then=None):
    n_tiles, _, first = columns.shape
    halves = first // D
    lead = 3
    pairs = n_tiles // 2
    h_hi, h_lo = h_split
    with Stage(nc, name) as st:
        u = st.sb("u", [P, 2, first])
        u_hi, u_lo = (st.sb(n, [P, 2, first], F32R) for n in ("u_hi", "u_lo"))
        v = st.sb("v", [P, 2, D])
        v_hi, v_lo = (st.sb(n, [P, 2, D], F32R) for n in ("v_hi", "v_lo"))
        act_out = st.sb("act_out", [P, 2, S])
        coef = st.sb("coef", [P, S])
        c_hi, c_lo = (st.sb(n, [P, 2, S], F32R) for n in ("c_hi", "c_lo"))
        pa = st.ps("pa", [P, 2, CW])
        py = st.ps("py", [P, TT * 2, CW])
        u_loaded = [st.sem(f"u_loaded{i}") for i in range(2)]
        v_loaded = [st.sem(f"v_loaded{i}") for i in range(2)]
        u_hi_ready, u_split, v_hi_ready, v_split, rows_ready, acted, weighed, rounded, coef_ready, down_done, \
            kept_loaded, scaled, summed = (st.sem(n) for n in (
                "u_hi_ready", "u_split", "v_hi_ready", "v_split", "rows_ready", "acted", "weighed", "rounded",
                "coef_ready", "down_done", "kept_loaded", "scaled", "summed"))
        beside = Modulation(nc, k, st, ada[0], None, ada[1], first=2 * lead + 2) if ada else None
        x, gate = residual or (u[:], v[:, 0, :])
        tmp = v[:, 1, :].rearrange("p (a n) -> p a n", a=2)

        block = st.block()

        @block.sync
        def _(sp):
            def load(i, b, early=False):
                at = (lambda m: m[i]) if isinstance(i, int) else \
                    (lambda m: m[bass.ds(i, 1)].rearrange("a p n -> p (a n)"))
                if not early:
                    sp.wait_ge(u_split, i - 1)
                sp.dma_start(u[:, b, :], at(columns)).then_inc(u_loaded[b], 16)
                if not early:
                    sp.wait_ge(v_split, i - 1)
                sp.dma_start(v[:, b, :], at(rows)).then_inc(v_loaded[b], 16)

            for i in range(2 * lead):
                load(i, i % 2, early=(i < 2))
            for i in (2 * lead, 2 * lead + 1):
                load(i, i % 2)
                if ada:
                    beside.load(sp, i + 2, i % 2, early=True)
            with sp.Fori(lead + 1, pairs) as r:
                for b in range(2):
                    load(2 * r + b, b)
                    if ada:
                        beside.load(sp, 2 * r + (b + 2), b)
            if kept:
                sp.wait_ge(u_split, n_tiles)
                sp.dma_start(x, kept[0]).then_inc(kept_loaded, 16)
                sp.wait_ge(v_split, n_tiles)
                sp.dma_start(gate, kept[1]).then_inc(kept_loaded, 16)

        @block.tensor
        def _(pe):
            def up(i, b, early=False):
                pe.wait_ge(u_split, i + 1)
                if not early:
                    pe.wait_ge(coef_ready, i - 1)
                for half in range(halves):
                    for c in range(KT):
                        cols = slice(half * D + c * P, half * D + (c + 1) * P)
                        out = pa[:, b, half * S:(half + 1) * S]
                        pe.matmul(out, u_hi[:, b, cols], h_hi[:, c, :], start=(c == 0), stop=False)
                        pe.matmul(out, u_hi[:, b, cols], h_lo[:, c, :], start=False, stop=False)
                        last = pe.matmul(out, u_lo[:, b, cols], h_hi[:, c, :], start=False, stop=(c == KT - 1))
                last.then_inc(rows_ready, 1)

            def down(i, b, start=False, stop=False):
                pe.wait_ge(coef_ready, i + 1)
                pe.wait_ge(v_split, i + 1)
                for t in range(TT):
                    part = slice(t * P, (t + 1) * P)
                    for n in range(2):
                        cols = slice(n * CW, (n + 1) * CW)
                        pe.matmul(py[:, 2 * t + n, :], c_hi[:, b, part], v_hi[:, b, cols], start=start, stop=False)
                        pe.matmul(py[:, 2 * t + n, :], c_hi[:, b, part], v_lo[:, b, cols], start=False, stop=False)
                    for n in range(2):
                        cols = slice(n * CW, (n + 1) * CW)
                        last = pe.matmul(py[:, 2 * t + n, :], c_lo[:, b, part], v_hi[:, b, cols], start=False,
                                         stop=stop)
                last.then_inc(down_done, 1)

            up(0, 0, early=True)
            up(1, 1, early=True)
            down(0, 0, start=True)
            for i in range(2, 2 * lead):
                up(i, i % 2)
                down(i - 1, (i - 1) % 2)
            with pe.Fori(lead, pairs) as r:
                for b in range(2):
                    up(2 * r + b, b)
                    down(2 * r + (b - 1), 1 - b)
            down(n_tiles - 1, 1, stop=True)

        @block.scalar
        def _(act):
            func = ACT.Silu if kind == "swiglu" else ACT.Gelu

            def high_u(i, b, rnd, early=False):
                act.wait_ge(u_loaded[b], 16 * rnd + 16)
                if not early:
                    act.wait_ge(rows_ready, i - 1)
                act.copy(u_hi[:, b, :], u[:, b, :]).then_inc(u_hi_ready, 1)

            def high_v(i, b, rnd, early=False):
                act.wait_ge(v_loaded[b], 16 * rnd + 16)
                if not early:
                    act.wait_ge(down_done, i - 1)
                act.copy(v_hi[:, b, :], v[:, b, :]).then_inc(v_hi_ready, 1)

            def gate_tile(i, b, early=False):
                act.wait_ge(rows_ready, i + 1)
                if not early:
                    act.wait_ge(coef_ready, i - 1)
                act.activation(act_out[:, b, :], pa[:, b, 0:S], func).then_inc(acted, 1)

            high_u(0, 0, 0, early=True)
            high_u(1, 1, 0, early=True)
            high_v(0, 0, 0, early=True)
            for i in range(2 * lead):
                gate_tile(i, i % 2, early=(i < 2))
                high_u(i + 2, i % 2, i // 2 + 1)
                high_v(i + 1, (i + 1) % 2, (i + 1) // 2, early=(i < 1))
            with act.Fori(lead, pairs - 1) as r:
                for b in range(2):
                    gate_tile(2 * r + b, b)
                    high_u(2 * r + (b + 2), b, r + 1)
                    high_v(2 * r + (b + 1), 1 - b, r + b)
            gate_tile(n_tiles - 2, 0)
            high_v(n_tiles - 1, 1, pairs - 1)
            gate_tile(n_tiles - 1, 1)

        def low_u(engine, i, b):
            engine.wait_ge(u_hi_ready, i + 1)
            engine.tensor_tensor(u_lo[:, b, :], u[:, b, :], u_hi[:, b, :].bitcast(F32), ALU.subtract
                                 ).then_inc(u_split, 1)

        def low_v(engine, i, b):
            engine.wait_ge(v_hi_ready, i + 1)
            engine.tensor_tensor(v_lo[:, b, :], v[:, b, :], v_hi[:, b, :].bitcast(F32), ALU.subtract
                                 ).then_inc(v_split, 1)

        if ada:
            @block.gpsimd
            def _(pool):
                low_u(pool, 0, 0)
                with pool.Fori(0, pairs - 1) as r:
                    for b in range(2):
                        low_u(pool, 2 * r + (b + 1), 1 - b)
                        low_v(pool, 2 * r + b, b)
                low_u(pool, n_tiles - 1, 1)
                low_v(pool, n_tiles - 2, 0)
                low_v(pool, n_tiles - 1, 1)

        @block.vector
        def _(dve):
            def weigh(i, b, early=False):
                dve.wait_ge(acted, i + 1)
                if kind == "swiglu":
                    other = pa[:, b, S:2 * S]
                elif isinstance(i, int):
                    other = table[:, i, :]
                else:
                    other = table[:, bass.ds(i, 1), :].rearrange("p a s -> p (a s)")
                dve.tensor_tensor(coef[:], act_out[:, b, :], other, ALU.mult).then_inc(weighed, 1)
                dve.wait_ge(weighed, i + 1)
                if not early:
                    dve.wait_ge(down_done, i - 1)
                dve.tensor_copy(c_hi[:, b, :], coef[:]).then_inc(rounded, 1)
                dve.wait_ge(rounded, i + 1)
                dve.tensor_tensor(c_lo[:, b, :], coef[:], c_hi[:, b, :].bitcast(F32), ALU.subtract
                                  ).then_inc(coef_ready, 1)
                dve.wait_ge(coef_ready, i + 1)

            if not ada:
                low_u(dve, 0, 0)
                low_u(dve, 1, 1)
                low_v(dve, 0, 0)
            for i in range(2 * lead):
                weigh(i, i % 2, early=(i < 2))
                if not ada:
                    low_u(dve, i + 2, i % 2)
                    low_v(dve, i + 1, (i + 1) % 2)
            with dve.Fori(lead, pairs - 1) as r:
                for b in range(2):
                    weigh(2 * r + b, b)
                    if not ada:
                        low_u(dve, 2 * r + (b + 2), b)
                        low_v(dve, 2 * r + (b + 1), 1 - b)
                    if ada:
                        beside.fold(dve, 2 * r + (b + 2), b, (2 * r + (b - 2 * lead)) * KT, r - lead)
            for i in (n_tiles - 2, n_tiles - 1):
                weigh(i, i % 2)
                if not ada and i < n_tiles - 1:
                    low_v(dve, i + 1, 1)
                if ada:
                    beside.fold(dve, i + 2, i % 2, (i - 2 * lead) * KT, i // 2 - lead)
            dve.wait_ge(down_done, n_tiles)
            if kept:
                dve.wait_ge(kept_loaded, 32)
            for n in range(2 * TT):
                t, c = n // 2, (n % 2) * CW
                if n >= 2:
                    dve.wait_ge(summed, n - 1)
                dve.tensor_tensor(tmp[:, n % 2, :], py[:, n, :], gate[:, c:c + CW], ALU.mult).then_inc(scaled, 1)
                dve.wait_ge(scaled, n + 1)
                dve.tensor_tensor(x[:, t, c:c + CW], x[:, t, c:c + CW], tmp[:, n % 2, :], ALU.add).then_inc(summed, 1)
        if then:
            st.end_block()
            then(x, v)


def split_h(nc, name, h_t, hi, lo):
    with Stage(nc, name) as st:
        rounded, split = st.sem("rounded"), st.sem("split")
        block = st.block()

        @block.vector
        def _(dve):
            for c in range(0, KT, 2):
                dve.tensor_copy(hi[:, c:c + 2, :], h_t[:, c:c + 2, :]).then_inc(rounded, 1)
            for c in range(0, KT, 2):
                dve.wait_ge(rounded, c // 2 + 1)
                dve.tensor_tensor(lo[:, c:c + 2, :], h_t[:, c:c + 2, :], hi[:, c:c + 2, :].bitcast(F32), ALU.subtract
                                  ).then_inc(split, 1)
            dve.wait_ge(split, KT // 2)


def chunked(source, width, first=0):
    return [(source[j], first + j * WIDE, WIDE) for j in range(width // WIDE)]


def sparse_layer(nc, k, ins, mod, next_mod):
    x = k["x"]
    c = k["silu_c"][:, 0, :]
    with Stage(nc, "l0") as st:
        first_modulation(nc, k, "ada0", (ins["ada_w0"], ins["ada_b0"]), c, mod, 8)
        m = [mod[:, i * D:(i + 1) * D] for i in range(6)]
        with Stage(nc, "l0a") as sa:
            o_t = sa.sb("o_t", [P, KT, S])
            with Stage(nc, "l0b") as sb:
                z = sb.sb("z", [P, TT, SP_IN])
                h_t = sb.sb("h_t", [P, KT, S])
                normed(nc, k, "norm0", x, ins["attn_norm0"], m[0], m[1], h_t)
                whole = SP_IN // WIDE * WIDE
                project(nc, k, "proj0", h_t,
                        chunked(ins["sp_w_in"], whole) + [(ins["sp_w_in_tail"], whole, SP_IN - whole)],
                        out=z, ada=(ins["ada_w0"], [(c, mod, 12)], 8, 14))
                segs = [(Z_MQ, 8, ins["moba_q_norm"]), (Z_MK, 8, ins["moba_k_norm"]), (Z_NQ, 8, ins["nsa_q_norm"])]
                segs += [(Z_KV + br * KV_BRANCH, 2, ins["nsa_k_norm"][br]) for br in range(3)]
                head_norm_rope(nc, k, "rope0", z, segs)
                zt = sb.sb("zt", [P, 15, S])
                blocks = [Z_MQ + i * P for i in range(4)] + [Z_MK + i * P for i in range(4)]
                blocks += [Z_NQ + i * P for i in range(4)] + [Z_KV + br * KV_BRANCH for br in range(3)]
                turn(nc, k, "turn0", z, blocks, zt)
                pc_t = h_t[0:NCMP, :, :]
                vc = sb.sb("vc", [NCMP, 2, HEAD])
                gates = sb.sb("gates", [P, TT, 3 * HEADS])
                compress(nc, k, ins, z, zt[:, 8:12, :], pc_t, vc, gates,
                         ada=(ins["ada_w0"], [(c, mod, 12)], 14, 24))
                sparse_attention(nc, k, z, zt, pc_t, vc, gates, o_t)
            finish_modulation(nc, k, "ada0b", ins["ada_b0"], [(mod, 4, 12)])
            project(nc, k, "out0", o_t, chunked(ins["sp_w_out"], D), residual=(x, m[2]),
                    ada=(ins["ada_w1"], [(c, next_mod, 12)], 0, 8))
        feed_forward(nc, k, ins, 0, m, (ins["ada_w1"], [(c, next_mod, 12)]))
        finish_modulation(nc, k, "ada1b", ins["ada_b1"], [(next_mod, 0, 12)])


def feed_forward(nc, k, ins, layer, m, ada):
    hi, lo = k["h_hi"], k["h_lo"]
    with Stage(nc, f"ffh{layer}") as sh:
        h_t = sh.sb("h_t", [P, KT, S])
        normed(nc, k, f"fnorm{layer}", k["x"], ins[f"ffn_norm{layer}"], m[3], m[4], h_t)
        split_h(nc, f"fsplit{layer}", h_t, hi, lo)
    streamed_mlp(nc, k, f"ffn{layer}", ins[f"ffn_columns{layer}"], ins[f"ffn_rows{layer}"], "swiglu", (hi, lo),
                 residual=(k["x"][:], m[5]), ada=ada)


def head_norm(nc, k, name, o, gain, factor, gate=None):
    with Stage(nc, name) as st:
        sq = st.sb("sq", [P, TT, D])
        ss = st.sb("ss", [P, TT, HEADS])
        g = st.sb("g", [P, P])
        loaded, gated, mean_ready, root_ready, dve_done = (
            st.sem(n) for n in ("loaded", "gated", "mean_ready", "root_ready", "dve_done"))
        block = st.block()

        def by_head(v):
            return v.rearrange("p t (h d) -> p t h d", h=HEADS)

        @block.sync
        def _(sp):
            sp.dma_start(g[:], gain.partition_broadcast(P)).then_inc(loaded, 16)

        @block.scalar
        def _(act):
            if gate is not None:
                act.activation(gate, gate, ACT.Silu).then_inc(gated, 1)
            act.wait_ge(mean_ready, 1)
            act.activation(ss[:], ss[:], ACT.Sqrt).then_inc(root_ready, 1)

        @block.vector
        def _(dve):
            step = InOrder(dve, dve_done)
            step(dve.tensor_tensor(sq[:], o, o, ALU.mult))
            step(dve.tensor_reduce(ss[:], by_head(sq[:]), AX.X, ALU.add))
            dve.tensor_scalar(ss[:], ss[:], 1.0 / P, EPS, ALU.mult, ALU.add).then_inc(mean_ready, 1)
            dve.wait_ge(loaded, 16)
            step(dve.tensor_scalar(g[:], g[:], factor, None, ALU.mult))
            for t in range(TT):
                v = o[:, t, :].rearrange("p (h d) -> p h d", h=HEADS)
                step(dve.tensor_tensor(v, v, g[:].unsqueeze(1).broadcast_to([P, HEADS, P]), ALU.mult))
            if gate is not None:
                dve.wait_ge(gated, 1)
                step(dve.tensor_tensor(o, o, gate, ALU.mult))
            dve.wait_ge(root_ready, 1)
            step(dve.reciprocal(ss[:], ss[:]))
            step(dve.tensor_tensor(by_head(o), by_head(o), ss[:].unsqueeze(3).broadcast_to([P, TT, HEADS, P]),
                                   ALU.mult))


def diff_attention(nc, k, ins, z, zt, o):
    parts = ((0, P), (P, SC))
    with Stage(nc, "diff") as st:
        lp = st.sb("lp", [P, 4, HEAD])
        lam = st.sb("lam", [P, 2])
        neg_lam = st.sb("neg_lam", [P, 1])
        sc = st.sb("sc", [P, 2, 2, SC])
        pt = st.sb("pt", [P, 2, SC])
        nm = st.sb("nm", [P, 2, TT, 2])
        sm = st.sb("sm", [P, 2, TT, 2])
        ps = st.ps("ps", [P, 2, 2, CW])
        pp = st.ps("pp", [P, 2, CW])
        po = st.ps("po", [P, 2, CW])
        loaded, lam_sum, lam_exp, scored, masked, neg_max, exped, probs, turned, pt_ready, attended, stored, \
            dve_done = (st.sem(n) for n in (
                "loaded", "lam_sum", "lam_exp", "scored", "masked", "neg_max", "exped", "probs", "turned",
                "pt_ready", "attended", "stored", "dve_done"))
        block = st.block()

        @block.sync
        def _(sp):
            sp.dma_start(lp[:].rearrange("p a d -> p (a d)"), ins["diff_lambda"].partition_broadcast(P)
                         ).then_inc(loaded, 16)

        @block.tensor
        def _(pe):
            def scores(h):
                if h >= 2:
                    pe.wait_ge(masked, h - 1)
                for c in range(2):
                    rows = slice(c * HEAD, (c + 1) * HEAD)
                    for t, (lo, hi) in enumerate(parts):
                        last = pe.matmul(ps[:, h % 2, c, lo:hi], zt[rows, h, t * P:(t + 1) * P],
                                         zt[rows, 8 + h, 0:hi - lo], start=True, stop=True)
                last.then_inc(scored, 1)

            def turn_probs(h):
                pe.wait_ge(probs, h + 1)
                if h >= 2:
                    pe.wait_ge(pt_ready, h - 1)
                for c in range(3):
                    last = pe.transpose(pp[:, h % 2, c * P:(c + 1) * P], sc[:, h % 2, 0, c * P:(c + 1) * P],
                                        k["ident"][:])
                last.then_inc(turned, 1)

            def values(h):
                pe.wait_ge(pt_ready, h + 1)
                if h >= 2:
                    pe.wait_ge(stored, h - 1)
                v = [z[:, t, 2 * D + h * P:2 * D + (h + 1) * P] for t in range(TT)]
                pe.matmul(po[:, h % 2, 0:P], pt[:, h % 2, 0:P], v[0], start=True, stop=True)
                pe.matmul(po[:, h % 2, P:2 * P], pt[:, h % 2, P:2 * P], v[0], start=True, stop=False)
                pe.matmul(po[:, h % 2, P:2 * P], pt[:, h % 2, 2 * P:SC], v[1], start=False,
                          stop=True).then_inc(attended, 1)

            for h in range(HEADS + 2):
                if h < HEADS:
                    scores(h)
                if 1 <= h <= HEADS:
                    turn_probs(h - 1)
                if h >= 2:
                    values(h - 2)

        @block.vector
        def _(dve):
            step = InOrder(dve, dve_done)
            dve.wait_ge(loaded, 16)
            step(dve.tensor_tensor(lp[:, 0, :], lp[:, 0, :], lp[:, 1, :], ALU.mult))
            step(dve.tensor_tensor(lp[:, 2, :], lp[:, 2, :], lp[:, 3, :], ALU.mult))
            dve.tensor_reduce(lam[:, 0:1], lp[:, 0, :], AX.X, ALU.add).then_inc(lam_sum, 1)
            dve.tensor_reduce(lam[:, 1:2], lp[:, 2, :], AX.X, ALU.add).then_inc(lam_sum, 1)
            dve.wait_ge(lam_exp, 1)
            step(dve.tensor_tensor(neg_lam[:], lam[:, 1:2], lam[:, 0:1], ALU.subtract))
            step(dve.tensor_scalar(neg_lam[:], neg_lam[:], -DIFF_LAM_INIT, None, ALU.add))

            def mask(h):
                dve.wait_ge(scored, h + 1)
                if h >= 2:
                    dve.wait_ge(turned, h - 1)
                s = sc[:, h % 2]
                dve.scalar_tensor_tensor(s, ps[:, h % 2, :, 0:SC], HEAD ** -0.5,
                                         k["causal"][:].unsqueeze(1).broadcast_to([P, 2, SC]), ALU.mult,
                                         ALU.add).then_inc(masked, 1)
                dve.wait_ge(masked, h + 1)
                for t, (lo, hi) in enumerate(parts):
                    dve.tensor_reduce(nm[:, h % 2, t, :], s[:, :, lo:hi], AX.X, ALU.max,
                                      negate=True).then_inc(neg_max, 1)

            def combine(h):
                dve.wait_ge(exped, 4 * h + 4)
                r = sm[:, h % 2]
                step(dve.reciprocal(r, r))
                step(dve.tensor_scalar(r[:, :, 1], r[:, :, 1], neg_lam[:], None, ALU.mult))
                for t, (lo, hi) in enumerate(parts):
                    last = dve.tensor_scalar(sc[:, h % 2, 1, lo:hi], sc[:, h % 2, 1, lo:hi], sm[:, h % 2, t, 1:2],
                                             None, ALU.mult)
                step(last)
                for t, (lo, hi) in enumerate(parts):
                    last = dve.scalar_tensor_tensor(sc[:, h % 2, 0, lo:hi], sc[:, h % 2, 0, lo:hi],
                                                    sm[:, h % 2, t, 0:1], sc[:, h % 2, 1, lo:hi], ALU.mult, ALU.add)
                last.then_inc(probs, 1)

            for h in range(HEADS + 1):
                if h < HEADS:
                    mask(h)
                if h >= 1:
                    combine(h - 1)

        @block.scalar
        def _(act):
            act.wait_ge(lam_sum, 2)
            act.activation(lam[:], lam[:], ACT.Exp).then_inc(lam_exp, 1)

            def exp(h):
                for t, (lo, hi) in enumerate(parts):
                    act.wait_ge(neg_max, 2 * h + t + 1)
                    for c in range(2):
                        act.activation(sc[:, h % 2, c, lo:hi], sc[:, h % 2, c, lo:hi], ACT.Exp,
                                       bias=nm[:, h % 2, t, c:c + 1],
                                       accum_out=sm[:, h % 2, t, c:c + 1]).then_inc(exped, 1)

            def move_probs(h):
                act.wait_ge(turned, h + 1)
                if h >= 2:
                    act.wait_ge(attended, h - 1)
                act.copy(pt[:, h % 2, :], pp[:, h % 2, 0:SC]).then_inc(pt_ready, 1)

            def store(h):
                act.wait_ge(attended, h + 1)
                act.copy(o[:, :, h * P:(h + 1) * P],
                         po[:, h % 2, 0:2 * P].rearrange("p (t d) -> p t d", t=TT)).then_inc(stored, 1)

            for h in range(HEADS + 2):
                if h < HEADS:
                    exp(h)
                if 1 <= h <= HEADS:
                    move_probs(h - 1)
                if h >= 2:
                    store(h - 2)


def diff_layer(nc, k, ins, mod, next_mod, modc):
    x = k["x"]
    silu = k["silu_c"]
    ada = (ins["ada_w2"], [(silu[:, 1, :], next_mod, 12), (silu[:, 2, :], modc, 4)])
    with Stage(nc, "l1") as st:
        m = [mod[:, i * D:(i + 1) * D] for i in range(6)]
        h_t = st.sb("h_t", [P, KT, S])
        with Stage(nc, "l1b") as sb:
            z = sb.sb("z", [P, TT, 3 * D])
            normed(nc, k, "norm1", x, ins["attn_norm1"], m[0], m[1], h_t)
            project(nc, k, "proj1", h_t, chunked(ins["diff_w_in"], 3 * D), out=z, ada=(*ada, 0, 6))
            zt = sb.sb("zt", [P, 16, S])
            o = sb.sb("o", [P, TT, D])
            head_norm_rope(nc, k, "rope1", z, [(0, 16, ins["diff_q_norm"]), (D, 16, ins["diff_k_norm"])])
            turn(nc, k, "turn1", z, [i * P for i in range(16)], zt)
            diff_attention(nc, k, ins, z, zt, o)
            head_norm(nc, k, "onorm1", o[:], ins["diff_out_norm"], 1.0 - DIFF_LAM_INIT)
            turn(nc, k, "oturn1", o, [i * P for i in range(KT)], h_t)
        project(nc, k, "out1", h_t, chunked(ins["diff_w_out"], D), residual=(x, m[2]), ada=(*ada, 6, 8))
    feed_forward(nc, k, ins, 1, m, ada)
    finish_modulation(nc, k, "ada2b", ins["ada_b2"], [(next_mod, 0, 12), (modc, 0, 4)])


XC = 2 * S
DH = 2 * DN_HEADS
TILES = 2 * TT


def delta_qkv(nc, k, ins, h_t, q_t, k_t, v_t, y, w):
    with Stage(nc, "dnqkv") as st:
        ring = w.shape[1]
        h_hi, h_lo = (st.sb(n, [P, KT, XC], F32R) for n in ("h_hi", "h_lo"))
        w_hi, w_lo = (st.sb(n, [P, 2, KT * P], F32R) for n in ("w_hi", "w_lo"))
        taps = st.sb("taps", [P, 3 * KT, DN_CONV])
        psum = st.ps("psum", [P, 4, CW])
        slot_loaded = [st.sem(f"slot_loaded{i}") for i in range(ring)]
        taps_loaded, h_hi_ready, h_split, w_hi_ready, w_split, product, conved, silued, dve_done = (
            st.sem(n) for n in ("taps_loaded", "h_hi_ready", "h_split", "w_hi_ready", "w_split", "product", "conved",
                                "silued", "dve_done"))
        blocks = 3 * KT
        block = st.block()

        @block.sync
        def _(sp):
            for b in range(blocks):
                if b >= ring:
                    sp.wait_ge(w_split, b - ring + 1)
                sp.dma_start(w[:, b % ring, :], ins["dn_w_qkv"][b]).then_inc(slot_loaded[b % ring], 16)
                if b == 1:
                    sp.dma_start(taps[:], ins["dn_conv"]).then_inc(taps_loaded, 16)

        @block.gpsimd
        def _(pool):
            for b in range(blocks):
                pool.wait_ge(w_hi_ready, b + 1)
                pool.tensor_tensor(w_lo[:, b % 2, :], w[:, b % ring, :], w_hi[:, b % 2, :].bitcast(F32), ALU.subtract
                                   ).then_inc(w_split, 1)

        @block.tensor
        def _(pe):
            pe.wait_ge(h_split, KT)
            for b in range(blocks):
                n = S if b < KT else XC
                pe.wait_ge(w_split, b + 1)
                if b >= 4:
                    pe.wait_ge(conved, b - 3)
                bank = psum[:, b % 4, 0:n]
                for c in range(KT):
                    cols = slice(c * P, (c + 1) * P)
                    pe.matmul(bank, w_hi[:, b % 2, cols], h_hi[:, c, 0:n], start=(c == 0), stop=False)
                    pe.matmul(bank, w_hi[:, b % 2, cols], h_lo[:, c, 0:n], start=False, stop=False)
                    last = pe.matmul(bank, w_lo[:, b % 2, cols], h_hi[:, c, 0:n], start=False, stop=(c == KT - 1))
                last.then_inc(product, 1)

        @block.vector
        def _(dve):
            step = InOrder(dve, dve_done)
            for c in range(KT):
                dve.wait_ge(h_hi_ready, c + 1)
                dve.tensor_tensor(h_lo[:, c, :], h_t[:, c, :], h_hi[:, c, :].bitcast(F32), ALU.subtract
                                  ).then_inc(h_split, 1)
            dve.wait_ge(taps_loaded, 16)
            mid = DN_CONV // 2
            for b in range(blocks):
                dve.wait_ge(product, b + 1)
                if b >= 2:
                    dve.wait_ge(silued, b - 1)
                n = S if b < KT else XC
                step(dve.tensor_scalar(y[:, b % 2, 0:n], psum[:, b % 4, 0:n], taps[:, b, mid:mid + 1], None, ALU.mult))
                for tap in (0, 1, 3, 4):
                    s = tap - mid
                    for lo, hi, row in ((0, S, ROW), (S, XC, S)):
                        if hi > n:
                            continue
                        to = y[:, b % 2, lo:hi].rearrange("p (r w) -> p r w", w=row)[:, :, max(0, -s):row - max(0, s)]
                        of = psum[:, b % 4, lo:hi].rearrange("p (r w) -> p r w", w=row)[
                            :, :, max(0, s):row - max(0, -s)]
                        last = dve.scalar_tensor_tensor(to, of, taps[:, b, tap:tap + 1], to, ALU.mult, ALU.add)
                    if tap < 4:
                        step(last)
                last.then_inc(conved, 1)

        @block.scalar
        def _(act):
            def high_w(b):
                act.wait_ge(slot_loaded[b % ring], 16 * (b // ring + 1))
                if b >= 2:
                    act.wait_ge(product, b - 1)
                act.copy(w_hi[:, b % 2, :], w[:, b % ring, :]).then_inc(w_hi_ready, 1)

            for c in range(KT):
                act.copy(h_hi[:, c, :], h_t[:, c, :]).then_inc(h_hi_ready, 1)
            high_w(0)
            high_w(1)
            for b in range(blocks):
                kind, h = b // KT, b % KT
                n = S if b < KT else XC
                to = q_t[:, h, :] if kind == 0 else (k_t, v_t)[kind - 1][h // 4][:, h % 4, 0:n]
                if b + 2 < blocks:
                    high_w(b + 2)
                act.wait_ge(conved, b + 1)
                act.activation(to, y[:, b % 2, 0:n], ACT.Silu).then_inc(silued, 1)


def delta_unit(nc, k, q_t, k_t):
    jobs = [(q_t, h, S, P ** -0.5) for h in range(DN_HEADS)] + [(k_t, h, XC, 1.0) for h in range(DN_HEADS)]
    with Stage(nc, "dnunit") as st:
        H = DN_HEADS
        sq = st.sb("sq", [P, 2, XC])
        inv = st.sb("inv", [H, 2, XC])
        eps = st.sb("eps", [P, 1])
        column = st.sb("column", [P, H, H])
        row = st.sb("row", [H, H, P])
        sums = st.ps("sums", [P, 2, CW])
        wide = st.ps("wide", [P, 4, CW])
        made, squared, summed, rooted, inverted, spread, scaled = (st.sem(n) for n in (
            "made", "squared", "summed", "rooted", "inverted", "spread", "scaled"))
        block = st.block()

        @block.gpsimd
        def _(pool):
            step = InOrder(pool, made)
            step(pool.memset(eps[:], EPS))
            step(pool.memset(column[:], 1.0))
            step(pool.affine_select(out=column[:], in_=column[:], compare_op=ALU.is_equal, fill=0.0, base=0,
                                    pattern=[[1, H], [-1, H]], channel_multiplier=0))
            step(pool.memset(row[:], 1.0))
            step(pool.affine_select(out=row[:], in_=row[:], compare_op=ALU.is_equal, fill=0.0, base=0,
                                    pattern=[[-1, H], [0, P]], channel_multiplier=1))

        @block.scalar
        def _(act):
            def root(kind):
                n = jobs[kind * H][2]
                act.wait_ge(summed, (kind + 1) * H)
                act.activation(inv[:, kind, 0:n], sums[0:H, kind, 0:n], ACT.Sqrt, bias=eps[0:H, :]).then_inc(rooted, 1)

            act.wait_ge(made, 5)
            for i, (v, h, n, _) in enumerate(jobs):
                if i >= 2:
                    act.wait_ge(summed, i - 1)
                act.activation(sq[:, i % 2, 0:n], v[:, h, 0:n], ACT.Square).then_inc(squared, 1)
            root(0)
            root(1)

        @block.tensor
        def _(pe):
            pe.wait_ge(made, 5)
            for i, (_, h, n, _) in enumerate(jobs):
                pe.wait_ge(squared, i + 1)
                pe.matmul(sums[0:H, i // H, 0:n], column[:, h, :], sq[:, i % 2, 0:n], start=(h == 0),
                          stop=(h == H - 1)).then_inc(summed, 1)
            for i, (_, h, n, _) in enumerate(jobs):
                pe.wait_ge(inverted, i // H + 1)
                if i >= 4:
                    pe.wait_ge(scaled, i - 3)
                pe.matmul(wide[:, i % 4, 0:n], row[:, h, :], inv[:, i // H, 0:n], start=True,
                          stop=True).then_inc(spread, 1)

        @block.vector
        def _(dve):
            for kind in range(2):
                n = jobs[kind * H][2]
                dve.wait_ge(rooted, kind + 1)
                dve.reciprocal(inv[:, kind, 0:n], inv[:, kind, 0:n]).then_inc(inverted, 1)
            for i, (v, h, n, factor) in enumerate(jobs):
                dve.wait_ge(spread, i + 1)
                dve.scalar_tensor_tensor(v[:, h, 0:n], v[:, h, 0:n], factor, wide[:, i % 4, 0:n], ALU.mult,
                                         ALU.mult).then_inc(scaled, 1)


def delta_gates(nc, k, ins, h_t, dg):
    beta, g_sum, exp_g, exp_rest, exp_last, rows = (dg[n] for n in (
        "beta", "g_sum", "exp_g", "exp_rest", "exp_last", "rows"))
    wide = [P, TILES, DH]
    with Stage(nc, "dngate") as st:
        w = st.sb("w", [P, KT, 2 * DH])
        dt = st.sb("dt", [P, DH])
        la = st.sb("la", [P, DH])
        a = st.sb("a", wide)
        e = st.sb("e", wide)
        pba = st.ps("pba", [P, CW])
        pg = st.ps("pg", [P, CW])
        pl = st.ps("pl", [P, CW])
        pr = st.ps("pr", [P, 2, CW])
        loaded, product, neg_abs, exp_abs, one_plus, logged, g_ready, sums, turned, rest_ready, exps, dve_done = (
            st.sem(n) for n in ("loaded", "product", "neg_abs", "exp_abs", "one_plus", "logged", "g_ready",
                                "sums", "turned", "rest_ready", "exps", "dve_done"))
        block = st.block()

        @block.sync
        def _(sp):
            sp.dma_start(w[:].rearrange("p c n -> p (c n)"), ins["dn_w_ba"]).then_inc(loaded, 16)
            sp.dma_start(dt[:], ins["dn_dt_bias"].partition_broadcast(P)).then_inc(loaded, 16)
            sp.dma_start(la[:], ins["dn_a_log"].partition_broadcast(P)).then_inc(loaded, 16)

        @block.tensor
        def _(pe):
            pe.wait_ge(loaded, 48)
            for t in range(TILES):
                for c in range(KT):
                    last = pe.matmul(pba[:, t * 2 * DH:(t + 1) * 2 * DH], h_t[:, c, t * P:(t + 1) * P], w[:, c, :],
                                     start=(c == 0), stop=(c == KT - 1))
            last.then_inc(product, 1)
            pe.wait_ge(g_ready, 1)
            for t in range(TILES):
                for d in range(2):
                    at = t * DH + d * DN_HEADS
                    pe.matmul(pg[:, at:at + DN_HEADS], k["incl"][:, d, :], a[:, t, d * DN_HEADS:(d + 1) * DN_HEADS],
                              start=True, stop=True)
            pe.matmul(pl[:, 0:TILES * DH], k["ones"][:], a[:].rearrange("p t n -> p (t n)"), start=True,
                      stop=True).then_inc(sums, 1)
            pe.wait_ge(rest_ready, 1)
            for t in range(TILES):
                pe.transpose(pr[0:DH, t // 2, (t % 2) * S:(t % 2) * S + P], g_sum[:, t, :], k["ident"][:])
                last = pe.transpose(pr[0:DH, t // 2, (t % 2) * S + P:(t % 2 + 1) * S], beta[:, t, :], k["ident"][:])
            last.then_inc(turned, 1)

        @block.scalar
        def _(act):
            act.wait_ge(loaded, 48)
            act.activation(la[:], la[:], ACT.Exp).then_inc(exp_abs, 1)
            act.wait_ge(neg_abs, 2)
            act.activation(beta[:], beta[:], ACT.Exp, scale=-1.0).then_inc(exp_abs, 1)
            act.activation(e[:], e[:], ACT.Exp).then_inc(exp_abs, 1)
            act.wait_ge(one_plus, 1)
            act.activation(e[:], e[:], ACT.Ln).then_inc(logged, 1)
            act.wait_ge(rest_ready, 1)
            for v in (exp_g, exp_rest, exp_last):
                act.activation(v[:], v[:], ACT.Exp).then_inc(exps, 1)

        @block.vector
        def _(dve):
            step = InOrder(dve, dve_done)
            dve.wait_ge(product, 1)
            ba = pba[:, 0:TILES * 2 * DH].rearrange("p (t n) -> p t n", t=TILES)
            dve.tensor_copy(beta[:], ba[:, :, 0:DH]).then_inc(neg_abs, 1)
            step(dve.tensor_tensor(a[:], ba[:, :, DH:2 * DH], dt[:].unsqueeze(1).broadcast_to(wide), ALU.add))
            step(dve.tensor_scalar(e[:], a[:], -1.0, None, ALU.mult))
            dve.tensor_tensor(e[:], e[:], a[:], ALU.min).then_inc(neg_abs, 1)
            dve.wait_ge(exp_abs, 3)
            dve.tensor_scalar(e[:], e[:], 1.0, None, ALU.add).then_inc(one_plus, 1)
            step(dve.tensor_scalar(beta[:], beta[:], 1.0, None, ALU.add))
            step(dve.reciprocal(beta[:], beta[:]))
            step(dve.tensor_scalar(a[:], a[:], 0.0, None, ALU.max))
            dve.wait_ge(logged, 1)
            step(dve.tensor_tensor(a[:], a[:], e[:], ALU.add))
            dve.scalar_tensor_tensor(a[:], a[:], -1.0, la[:].unsqueeze(1).broadcast_to(wide), ALU.mult,
                                     ALU.mult).then_inc(g_ready, 1)
            dve.wait_ge(sums, 1)
            total = pl[:, 0:TILES * DH].rearrange("p (t n) -> p t n", t=TILES)
            so_far = pg[:, 0:TILES * DH].rearrange("p (t n) -> p t n", t=TILES)
            step(dve.tensor_copy(g_sum[:], so_far))
            step(dve.tensor_copy(exp_g[:], so_far))
            step(dve.tensor_copy(exp_last[:], total))
            dve.tensor_tensor(exp_rest[:], exp_last[:], g_sum[:], ALU.subtract).then_inc(rest_ready, 1)
            dve.wait_ge(turned, 1)
            dve.wait_ge(exps, 3)
            step(dve.tensor_copy(rows[:].rearrange("n (a b) s -> n a (b s)", a=2), pr[0:DH]))


def delta_matrices(nc, k, dg, q_t, k_t, at_m, qd):
    quads = [(t, g, d) for t in range(TILES) for g in range(2) for d in range(2)]
    n_jobs = len(quads)
    with Stage(nc, "dnmat") as st:
        dt = st.sb("dt", [P, 2, 4, P])
        pgram = st.ps("pgram", [P, 2, CW])
        pkq = st.ps("pkq", [P, 2, CW])
        prow = st.ps("prow", [P, 2, 4, S])
        sel = st.sb("sel", [DH, DH, P])
        betas = st.sb("betas", [P, 2, 4, P])
        sel_ready, grams, row_sums, beta_ready, differenced, diffs, decays, used, dve_done = (
            st.sem(n) for n in ("sel_ready", "grams", "row_sums", "beta_ready", "differenced", "diffs", "decays",
                                "used", "dve_done"))
        block = st.block()

        @block.gpsimd
        def _(pool):
            pool.memset(sel[:], 1.0).then_inc(sel_ready, 1)
            pool.wait_ge(sel_ready, 1)
            pool.affine_select(out=sel[:], in_=sel[:], compare_op=ALU.is_equal, fill=0.0, base=0,
                               pattern=[[-1, DH], [0, P]], channel_multiplier=1).then_inc(sel_ready, 1)

        @block.tensor
        def _(pe):
            pe.wait_ge(sel_ready, 2)
            for i, (t, g, d) in enumerate(quads):
                if i >= 2:
                    pe.wait_ge(differenced, i - 1)
                    pe.wait_ge(beta_ready, i - 1)
                for h in range(4):
                    last = pe.matmul(prow[:, i % 2, h, :], sel[:, d * DN_HEADS + g * 4 + h, :], dg["rows"][:, t, :],
                                     start=True, stop=True)
                last.then_inc(row_sums, 1)
                if d == 0:
                    pair = i // 2
                    if pair >= 2:
                        pe.wait_ge(used, i - 2)
                    for h in range(4):
                        key = k_t[:, g * 4 + h, t * P:(t + 1) * P]
                        last = pe.matmul(pgram[:, pair % 2, h * P:(h + 1) * P], key, key, start=True, stop=True)
                    if t < TT:
                        for h in range(4):
                            last = pe.matmul(pkq[:, pair % 2, h * P:(h + 1) * P],
                                             k_t[:, g * 4 + h, t * P:(t + 1) * P],
                                             q_t[:, g * 4 + h, t * P:(t + 1) * P], start=True, stop=True)
                    last.then_inc(grams, 1)

        @block.vector
        def _(dve):
            done = Counted(dve, dve_done)
            four = [P, 4, P]
            for i in range(n_jobs + 1):
                j = i - 1
                if i < n_jobs:
                    t, g, d = quads[i]
                    gs = dg["g_sum"][:, t, d * DN_HEADS + g * 4:d * DN_HEADS + g * 4 + 4]
                    dve.wait_ge(row_sums, i + 1)
                    if i >= 2:
                        dve.wait_ge(used, i - 1)
                    dve.tensor_tensor(dt[:, i % 2], prow[:, i % 2, :, 0:P], gs.unsqueeze(2).broadcast_to(four),
                                      ALU.subtract).then_inc(differenced, 1)
                if j >= 0:
                    jt, jg, jd = quads[j]
                    m = at_m[:, jt, jd, jg * 4:jg * 4 + 4, :]
                    bank = j // 2 % 2
                    dve.wait_ge(decays, j + 1)
                    dve.wait_ge(grams, j // 2 + 1)
                    decayed = done.at(dve.tensor_tensor(m, pgram[:, bank, :].rearrange("p (h s) -> p h s", h=4),
                                                        dt[:, j % 2], ALU.mult))
                if i < n_jobs:
                    dve.wait_ge(differenced, i + 1)
                    dve.tensor_tensor(dt[:, i % 2], dt[:, i % 2],
                                      k["decay_mask"][:, d, :].unsqueeze(1).broadcast_to(four),
                                      ALU.add).then_inc(diffs, 1)
                if j >= 0:
                    done.wait(decayed)
                    strict = done.at(dve.tensor_tensor(m, m, k["strict"][:, jd, :].unsqueeze(1).broadcast_to(four),
                                                       ALU.mult))
                    if jt < TT:
                        dve.tensor_tensor(qd[:, jt, jd, jg * 4:jg * 4 + 4, :],
                                          pkq[:, bank, :].rearrange("p (h s) -> p h s", h=4), dt[:, j % 2], ALU.mult)
                    done.wait(strict)
                    dve.wait_ge(beta_ready, j + 1)
                    dve.tensor_tensor(m, m, betas[:, j % 2], ALU.mult).then_inc(used, 1)

        @block.scalar
        def _(act):
            for i in range(n_jobs):
                act.wait_ge(differenced, i + 1)
                if i >= 2:
                    act.wait_ge(used, i - 1)
                act.copy(betas[:, i % 2], prow[:, i % 2, :, P:S]).then_inc(beta_ready, 1)
                act.wait_ge(diffs, i + 1)
                act.activation(dt[:, i % 2], dt[:, i % 2], ACT.Exp).then_inc(decays, 1)


def delta_inverse(nc, k, at_m):
    groups = [(t, d, g) for t in range(TILES) for d in range(2) for g in range(2)]
    levels = 6
    steps = [(pair, level, which) for pair in range(len(groups) // 2) for level in range(levels + 1)
             for which in range(2)]
    with Stage(nc, "dninv") as st:
        pw = st.sb("pw", [P, 2, 4, P])
        pwt = st.sb("pwt", [P, 2, 4, P])
        pp = st.ps("pp", [P, 2, CW])
        pt = st.ps("pt", [P, 2, CW])
        pi = st.ps("pi", [P, 2, CW])
        powers, power_ready, t_power_ready, product, inverse_ready = (
            st.sem(n) for n in ("powers", "power_ready", "t_power_ready", "product", "inverse_ready"))
        block = st.block()

        def inverse(pair, which):
            t, d, g = groups[2 * pair + which]
            return at_m[:, t, d, g * 4:g * 4 + 4, :]

        def t_powers_before(n):
            return sum(1 for _, level, _ in steps[:n] if level < levels)

        @block.tensor
        def _(pe):
            def power(n):
                pair, level, b = steps[n]
                m = inverse(pair, b)
                if n >= 2:
                    pe.wait_ge(power_ready, n - 1)
                    pe.wait_ge(t_power_ready, t_powers_before(n - 1))
                for h in range(4):
                    cols = slice(h * P, (h + 1) * P)
                    if level == 0:
                        last = pe.transpose(pp[:, b, cols], m[:, h, :], k["ident"][:])
                    else:
                        last = pe.matmul(pp[:, b, cols], pwt[:, b, h, :], pw[:, b, h, :], start=True, stop=True)
                    if 0 < level < levels:
                        last = pe.matmul(pt[:, b, cols], pw[:, b, h, :], pwt[:, b, h, :], start=True, stop=True)
                last.then_inc(powers, 1)

            def apply(n):
                pair, level, b = steps[n]
                if level == 0:
                    return
                m = inverse(pair, b)
                pe.wait_ge(power_ready, n + 1)
                pe.wait_ge(inverse_ready, n - 1)
                for h in range(4):
                    last = pe.matmul(pi[:, b, h * P:(h + 1) * P], pw[:, b, h, :], m[:, h, :], start=True, stop=True)
                last.then_inc(product, 1)

            for n in range(len(steps) + 1):
                if n < len(steps):
                    power(n)
                if n >= 1:
                    apply(n - 1)

        def products_before(n):
            return sum(1 for _, level, _ in steps[:n] if level)

        @block.scalar
        def _(act):
            for n, (pair, level, b) in enumerate(steps):
                act.wait_ge(powers, n + 1)
                if n >= 2:
                    act.wait_ge(product, products_before(n - 1)) if products_before(n - 1) else None
                act.copy(pw[:, b], pp[:, b, :].rearrange("p (h s) -> p h s", h=4)).then_inc(power_ready, 1)

        @block.vector
        def _(dve):
            def t_power(n):
                pair, level, b = steps[n]
                m = inverse(pair, b)
                if level == levels:
                    return
                dve.wait_ge(powers, n + 1)
                if level == 0:
                    dve.tensor_copy(pwt[:, b], m).then_inc(t_power_ready, 1)
                else:
                    dve.tensor_copy(pwt[:, b], pt[:, b, :].rearrange("p (h s) -> p h s", h=4)
                                    ).then_inc(t_power_ready, 1)

            def factor(n):
                pair, level, b = steps[n]
                m = inverse(pair, b)
                if level == 0:
                    dve.wait_ge(t_power_ready, t_powers_before(n + 1))
                    dve.scalar_tensor_tensor(m, m, -1.0, k["ident"][:].unsqueeze(1).broadcast_to([P, 4, P]), ALU.mult,
                                             ALU.add).then_inc(inverse_ready, 1)
                else:
                    dve.wait_ge(product, products_before(n + 1))
                    dve.wait_ge(inverse_ready, n - 1)
                    dve.tensor_tensor(m, m, pi[:, b, :].rearrange("p (h s) -> p h s", h=4), ALU.add
                                      ).then_inc(inverse_ready, 1)

            for n in range(len(steps) + 1):
                if n < len(steps):
                    t_power(n)
                if n >= 1:
                    factor(n - 1)


def delta_recurrence(nc, k, dg, q_t, k_t, k_tok, v_tok, inv_t, qd, o):
    order = {0: [2, 3, 0, 1], 1: [3, 2, 1, 0]}
    jobs = [(order[d][s], d, g) for s in range(TILES) for d in range(2) for g in range(2)]
    n_jobs = len(jobs)
    with Stage(nc, "dnrec") as st:
        state = st.sb("state", [P, 2, 2, 4, P])
        rhs = st.sb("rhs", [P, 2, 4, P])
        kd = st.sb("kd", [P, 2, 4, P])
        vn = st.sb("vn", [P, 2, 4, P])
        tmp = st.sb("tmp", [P, 4, P])
        pks = st.ps("pks", [P, 2, CW])
        pqs = st.ps("pqs", [P, CW])
        pvn = st.ps("pvn", [P, CW])
        psu = st.ps("psu", [P, 2, CW])
        poi = st.ps("poi", [P, 2, CW])
        zeroed, recalled, rhs_ready, q_used, kd_ready, v_new, vn_ready, updated, decayed, state_ready, out_done, \
            dve_done = (st.sem(n) for n in (
                "zeroed", "recalled", "rhs_ready", "q_used", "kd_ready", "v_new", "vn_ready", "updated", "decayed",
                "state_ready", "out_done", "dve_done"))
        block = st.block()

        def four(ap):
            return ap.rearrange("p (h s) -> p h s", h=4)

        def factor(what, i):
            t, d, g = jobs[i]
            v = dg[what][:, t, d * DN_HEADS + g * 4:d * DN_HEADS + g * 4 + 4]
            return v.unsqueeze(2).broadcast_to([P, 4, P])

        def outs(i):
            return sum(1 for t, _, _ in jobs[:i] if t < TT)

        @block.tensor
        def _(pe):
            def recall(i):
                t, d, g = jobs[i]
                if i == 0:
                    pe.wait_ge(zeroed, 2)
                if i >= 4:
                    pe.wait_ge(state_ready, i - 3)
                if i >= 2:
                    pe.wait_ge(rhs_ready, i - 1)
                for h in range(4):
                    last = pe.matmul(pks[:, i % 2, h * P:(h + 1) * P], k_t[:, g * 4 + h, t * P:(t + 1) * P],
                                     state[:, d, g, h, :], start=True, stop=True)
                if t < TT:
                    if outs(i) >= 1:
                        pe.wait_ge(q_used, outs(i))
                    for h in range(4):
                        last = pe.matmul(pqs[:, h * P:(h + 1) * P], q_t[:, g * 4 + h, t * P:(t + 1) * P],
                                         state[:, d, g, h, :], start=True, stop=True)
                last.then_inc(recalled, 1)

            def solve(i):
                t, d, g = jobs[i]
                pe.wait_ge(rhs_ready, i + 1)
                if i >= 1:
                    pe.wait_ge(vn_ready, i)
                for h in range(4):
                    last = pe.matmul(pvn[:, h * P:(h + 1) * P], inv_t[:, t, d, g * 4 + h, :],
                                     rhs[:, i % 2, h, :], start=True, stop=True)
                last.then_inc(v_new, 1)

            def update(i):
                t, d, g = jobs[i]
                pe.wait_ge(vn_ready, i + 1)
                pe.wait_ge(kd_ready, i + 1)
                if i >= 2:
                    pe.wait_ge(state_ready, i - 1)
                for h in range(4):
                    last = pe.matmul(psu[:, i % 2, h * P:(h + 1) * P], kd[:, i % 2, h, :], vn[:, i % 2, h, :],
                                     start=True, stop=True)
                if t < TT:
                    n = outs(i)
                    if n >= 2:
                        pe.wait_ge(out_done, n - 1)
                    for h in range(4):
                        last = pe.matmul(poi[:, n % 2, h * P:(h + 1) * P], qd[:, t, d, g * 4 + h, :],
                                         vn[:, i % 2, h, :], start=True, stop=True)
                last.then_inc(updated, 1)

            for i in range(n_jobs + 2):
                if i < n_jobs:
                    recall(i)
                if 1 <= i <= n_jobs:
                    solve(i - 1)
                if i >= 2:
                    update(i - 2)

        @block.gpsimd
        def _(pool):
            pool.memset(state[:], 0.0).then_inc(zeroed, 1)
            pool.memset(o, 0.0).then_inc(zeroed, 1)
            pool.wait_ge(zeroed, 2)
            for i, (t, d, g) in enumerate(jobs):
                if i >= 2:
                    pool.wait_ge(updated, i - 1)
                pool.tensor_tensor(kd[:, i % 2], k_tok[:, t, g * 4 * P:(g + 1) * 4 * P].rearrange(
                    "p (h s) -> p h s", h=4), factor("exp_rest", i), ALU.mult).then_inc(kd_ready, 1)
                pool.wait_ge(recalled, i + 1)
                if i >= 4:
                    pool.wait_ge(state_ready, i - 3)
                s = state[:, d, g]
                pool.tensor_tensor(s, s, factor("exp_last", i), ALU.mult).then_inc(decayed, 1)

        @block.scalar
        def _(act):
            for i in range(n_jobs):
                act.wait_ge(v_new, i + 1)
                if i >= 2:
                    act.wait_ge(updated, i - 1)
                act.copy(vn[:, i % 2], four(pvn[:])).then_inc(vn_ready, 1)

        @block.vector
        def _(dve):
            done = Counted(dve, dve_done)
            summed = 0

            def right_side(i):
                nonlocal summed
                t, d, g = jobs[i]
                cols = slice(g * 4 * P, (g + 1) * 4 * P)
                r = rhs[:, i % 2]
                dve.wait_ge(recalled, i + 1)
                if i >= 2:
                    dve.wait_ge(v_new, i - 1)
                scaled = done.at(dve.tensor_tensor(r, four(pks[:, i % 2, :]), factor("exp_g", i), ALU.mult))
                if t < TT:
                    done.wait(summed)
                    recall = dve.tensor_tensor(tmp[:], four(pqs[:]), factor("exp_g", i), ALU.mult)
                    recall.then_inc(q_used, 1)
                done.wait(scaled)
                taken = done.at(dve.tensor_tensor(r, four(v_tok[:, t, cols]), r, ALU.subtract))
                if t < TT:
                    dve.wait_ge(q_used, outs(i) + 1)
                    summed = done.at(dve.tensor_tensor(four(o[:, t, cols]), four(o[:, t, cols]), tmp[:], ALU.add))
                done.wait(taken)
                dve.tensor_tensor(r, r, factor("beta", i), ALU.mult).then_inc(rhs_ready, 1)

            def finish(i):
                nonlocal summed
                t, d, g = jobs[i]
                cols = slice(g * 4 * P, (g + 1) * 4 * P)
                s = state[:, d, g]
                dve.wait_ge(updated, i + 1)
                dve.wait_ge(decayed, i + 1)
                dve.tensor_tensor(s, s, four(psu[:, i % 2, :]), ALU.add).then_inc(state_ready, 1)
                if t < TT:
                    done.wait(summed)
                    last = dve.tensor_tensor(four(o[:, t, cols]), four(o[:, t, cols]), four(poi[:, outs(i) % 2, :]),
                                             ALU.add)
                    last.then_inc(out_done, 1)
                    dve.wait_ge(out_done, outs(i + 1))

            dve.wait_ge(zeroed, 2)
            for i in range(n_jobs + 2):
                if i < n_jobs:
                    right_side(i)
                if i >= 2:
                    finish(i - 2)


def turn_back(nc, k, name, v_t, out):
    with Stage(nc, name) as st:
        banks = 6
        psum = st.ps("psum", [P, banks, CW])
        turned, copied, moved = st.sem("turned"), st.sem("copied"), st.sem("moved")
        jobs = [(t, g) for t in range(TILES) for g in range(2)]
        block = st.block()

        @block.tensor
        def _(pe):
            for n, (t, g) in enumerate(jobs):
                if n >= banks:
                    prior = n - banks
                    pe.wait_ge(copied if prior % 2 == 0 else moved, prior // 2 + 1)
                for h in range(4):
                    last = pe.transpose(psum[:, n % banks, h * P:(h + 1) * P],
                                        v_t[g][:, h, t * P:(t + 1) * P], k["ident"][:])
                last.then_inc(turned, 1)

        @block.vector
        def _(dve):
            for n in range(0, len(jobs), 2):
                t, g = jobs[n]
                dve.wait_ge(turned, n + 1)
                dve.tensor_copy(out[:, t, g * CW:(g + 1) * CW], psum[:, n % banks, :]).then_inc(copied, 1)

        @block.scalar
        def _(act):
            for n in range(1, len(jobs), 2):
                t, g = jobs[n]
                act.wait_ge(turned, n + 1)
                act.copy(out[:, t, g * CW:(g + 1) * CW], psum[:, n % banks, :]).then_inc(moved, 1)


def delta_layer(nc, k, ins, mod, modc, free):
    x = k["x"]
    m = [mod[:, i * D:(i + 1) * D] for i in range(6)]
    with Stage(nc, "dn") as st:
        o = modc[:].rearrange("p (t d) -> p t d", t=TT)
        gate = mod[:, 0:2 * D].rearrange("p (t d) -> p t d", t=TT)
        with Stage(nc, "dna") as sa:
            q_t = free[:, TILES * D:6 * D].rearrange("p (h s) -> p h s", h=DN_HEADS)
            k_t = sa.sb("k_t", [P, DN_HEADS, XC])
            k_halves = [k_t[:, 0:4, :], k_t[:, 4:8, :]]
            v_tok = sa.sb("v_tok", [P, TILES, D])
            dg = {n: sa.sb(n, [P, TILES, DH]) for n in ("beta", "g_sum", "exp_g", "exp_rest", "exp_last")}
            dg["rows"] = sa.sb("rows", [DH, TILES, S])
            with Stage(nc, "dnb") as sb:
                h_t = sb.sb("h_t", [P, KT, XC])
                with Stage(nc, "dnc") as sc:
                    ctx = sc.sb("ctx", [P, TT, D])
                    loaded = sc.sem("loaded")
                    block = nc.Block()
                    with block as block:
                        @block.sync
                        def _(sp):
                            sp.dma_start(ctx[:], ins["ctx"].rearrange("(t p) d -> p t d", p=P)).then_inc(loaded, 16)
                            sp.wait_ge(loaded, 16)
                    normed(nc, k, "dnorm", x, ins["norm_g2"][0], m[0], m[1], h_t[:, :, 0:S])
                    normed(nc, k, "dcnorm", ctx, ins["norm_g2"][0], modc[:, 0:D], modc[:, D:2 * D], h_t[:, :, S:XC])
                v_t = [row.rearrange("p (h s) -> p h s", h=4) for row in (modc[:, 0:2 * D], mod[:, 0:2 * D])]
                delta_qkv(nc, k, ins, h_t, q_t, k_halves, v_t, v_tok[:, 0, :].rearrange("p (a n) -> p a n", a=2),
                          free[:, 0:3 * D].rearrange("p (a n) -> p a n", a=3))
                turn_back(nc, k, "dnv", v_t, v_tok)
                delta_unit(nc, k, q_t, k_t)
                project(nc, k, "dngp", h_t[:, :, 0:S], chunked(ins["dn_w_gate"], D), out=gate)
                delta_gates(nc, k, ins, h_t, dg)
            k_tok = free[:, 0:TILES * D].rearrange("p (t d) -> p t d", t=TILES)
            turn_back(nc, k, "dnk", k_halves, k_tok)
            at_m = sa.sb("at_m", [P, TILES, 2, DN_HEADS, P])
            qd = sa.sb("qd", [P, TT, 2, DN_HEADS, P])
            delta_matrices(nc, k, dg, q_t, k_t, at_m, qd)
            delta_inverse(nc, k, at_m)
            delta_recurrence(nc, k, dg, q_t, k_t, k_tok, v_tok, at_m, qd, o)
        h_t = st.sb("o_t", [P, KT, S])
        head_norm(nc, k, "dnon", o, ins["dn_norm_g"], 1.0, gate=gate)
        turn(nc, k, "dnot", o, [i * P for i in range(KT)], h_t)
        project(nc, k, "dnout", h_t, chunked(ins["dn_w_out"], D), residual=(x, m[2]))


def peer_scores(nc, k, ins, h_t, scores):
    with Stage(nc, "pq") as st:
        ring = 3
        per = WIDE // P
        blocks = 16
        n_chunks = blocks // per
        h_hi, h_lo = k["h_hi"], k["h_lo"]
        w = st.sb("w", [P, ring, KT * WIDE])
        w_hi, w_lo = (st.sb(n, [P, 2, KT * WIDE], F32R) for n in ("w_hi", "w_lo"))
        q_t = st.sb("q_t", [P, 16, S])
        keys = st.sb("keys", [P, 16, NKEYS])
        psum = st.ps("psum", [P, 4, CW])
        pscore = st.ps("pscore", [P, 2, CW])
        slot_loaded = [st.sem(f"slot_loaded{i}") for i in range(ring)]
        keys_loaded, h_hi_ready, h_split, w_hi_ready, w_split, product, q_ready, scored, stored = (
            st.sem(n) for n in ("keys_loaded", "h_hi_ready", "h_split", "w_hi_ready", "w_split", "product",
                                "q_ready", "scored", "stored"))
        block = st.block()

        @block.sync
        def _(sp):
            for j in range(n_chunks):
                if j >= ring:
                    sp.wait_ge(w_split, j - ring + 1)
                sp.dma_start(w[:, j % ring, :], ins["peer_w_q"][j]).then_inc(slot_loaded[j % ring], 16)
            sp.dma_start(keys[:], ins["peer_keys"]).then_inc(keys_loaded, 16)

        @block.vector
        def _(dve):
            for c in range(0, KT, 2):
                dve.wait_ge(h_hi_ready, c // 2 + 1)
                dve.tensor_tensor(h_lo[:, c:c + 2, :], h_t[:, c:c + 2, :], h_hi[:, c:c + 2, :].bitcast(F32),
                                  ALU.subtract).then_inc(h_split, 1)
            for j in range(n_chunks):
                dve.wait_ge(w_hi_ready, j + 1)
                dve.tensor_tensor(w_lo[:, j % 2, :], w[:, j % ring, :], w_hi[:, j % 2, :].bitcast(F32),
                                  ALU.subtract).then_inc(w_split, 1)

        @block.tensor
        def _(pe):
            pe.wait_ge(h_split, KT // 2)
            for b in range(blocks):
                j = b // per
                pe.wait_ge(w_split, j + 1)
                if b >= 4:
                    pe.wait_ge(q_ready, b - 3)
                bank = psum[:, b % 4, 0:S]
                for c in range(KT):
                    cols = slice(c * WIDE + b % per * P, c * WIDE + (b % per + 1) * P)
                    pe.matmul(bank, w_hi[:, j % 2, cols], h_hi[:, c, :], start=(c == 0), stop=False)
                    pe.matmul(bank, w_hi[:, j % 2, cols], h_lo[:, c, :], start=False, stop=False)
                    last = pe.matmul(bank, w_lo[:, j % 2, cols], h_hi[:, c, :], start=False, stop=(c == KT - 1))
                last.then_inc(product, 1)
            pe.wait_ge(keys_loaded, 16)
            pe.wait_ge(q_ready, 16)
            for n in range(8):
                t, quad = n // 4, n % 4
                if n >= 2:
                    pe.wait_ge(stored, n - 1)
                for b in range(4):
                    hp = quad * 4 + b
                    last = pe.matmul(pscore[:, n % 2, b * P:(b + 1) * P], q_t[:, hp, t * P:(t + 1) * P],
                                     keys[:, hp, :], start=True, stop=True)
                last.then_inc(scored, 1)

        @block.scalar
        def _(act):
            def high_w(j):
                act.wait_ge(slot_loaded[j % ring], 16 * (j // ring + 1))
                if j >= 2:
                    act.wait_ge(product, per * (j - 1))
                act.copy(w_hi[:, j % 2, :], w[:, j % ring, :]).then_inc(w_hi_ready, 1)

            for c in range(0, KT, 2):
                act.copy(h_hi[:, c:c + 2, :], h_t[:, c:c + 2, :]).then_inc(h_hi_ready, 1)
            high_w(0)
            for b in range(blocks):
                if b % per == 0 and b // per + 1 < n_chunks:
                    high_w(b // per + 1)
                act.wait_ge(product, b + 1)
                act.copy(q_t[:, b, :], psum[:, b % 4, 0:S]).then_inc(q_ready, 1)
            for n in range(8):
                t, quad = n // 4, n % 4
                act.wait_ge(scored, n + 1)
                act.copy(scores[:, t, quad * 4:quad * 4 + 4, :],
                         pscore[:, n % 2, :].rearrange("p (b s) -> p b s", b=4)).then_inc(stored, 1)


def peer_route(nc, k, scores, chosen):
    with Stage(nc, "route") as st:
        val = st.sb("val", [P, TT, 16, TOPK])
        idx = st.sb("idx", [P, TT, 16, TOPK], U32)
        idx_f = st.sb("idx_f", [P, TT, 16, TOPK])
        cand = st.sb("cand", [P, PHEADS, TOPK, TOPK])
        together = 4
        left = st.sb("left", [P, together, TOPK * TOPK])
        top = st.sb("top", [P, TT, PHEADS, TOPK])
        pos = st.sb("pos", [P, TT, PHEADS, TOPK], U32)
        ab = st.sb("ab", [P, 2, PHEADS * TOPK], U32)
        ab_f = st.sb("ab_f", [P, 2, PHEADS * TOPK])
        hot = st.sb("hot", [P, PHEADS, TOPK, TOPK])
        pick = st.sb("pick", [P, TT, 3, P])
        total = st.sb("total", [P, PHEADS])
        psum = st.ps("psum", [P, 2, CW])
        shifted, exped, picked, turned, dve_done = (
            st.sem(n) for n in ("shifted", "exped", "picked", "turned", "dve_done"))
        block = st.block()

        @block.vector
        def _(dve):
            done = Counted(dve, dve_done)

            def step(instruction):
                done.wait(done.at(instruction))

            def top16(lists):
                spare = [left[:, n, 0:values.shape[-1]] for n, (values, _, _) in enumerate(lists)]
                first = [done.at(dve.max(out_v[:, 0:8], values)) for values, out_v, _ in lists]
                rest = []
                for n, (values, out_v, _) in enumerate(lists):
                    done.wait(first[n])
                    rest.append(done.at(dve.match_replace(spare[n], out_v[:, 0:8], values, NEG)))
                second = []
                for n, (_, out_v, _) in enumerate(lists):
                    done.wait(rest[n])
                    second.append(done.at(dve.max(out_v[:, 8:16], spare[n])))
                for n, (values, out_v, out_i) in enumerate(lists):
                    done.at(dve.max_index(out_i[:, 0:8], out_v[:, 0:8], values))
                    done.wait(second[n])
                    done.at(dve.max_index(out_i[:, 8:16], out_v[:, 8:16], spare[n]))
                done.wait(done.n)

            for t in range(TT):
                for first in range(0, 16, together):
                    top16([(scores[:, t, hp, :], val[:, t, hp, :], idx[:, t, hp, :])
                           for hp in range(first, first + together)])
            step(dve.tensor_copy(idx_f[:], idx[:]))
            for t in range(TT):
                v = val[:, t].rearrange("p (h two) n -> p h two n", two=2)
                four_d = [P, PHEADS, TOPK, TOPK]
                step(dve.tensor_tensor(cand[:], v[:, :, 0, :].unsqueeze(3).broadcast_to(four_d),
                                       v[:, :, 1, :].unsqueeze(2).broadcast_to(four_d), ALU.add))
                for first in range(0, PHEADS, together):
                    top16([(cand[:, h].rearrange("p a b -> p (a b)"), top[:, t, h, :], pos[:, t, h, :])
                           for h in range(first, first + together)])
                flat = pos[:, t].rearrange("p h n -> p (h n)")
                step(dve.tensor_scalar(ab[:, 0, :], flat, 4, None, ALU.logical_shift_right))
                step(dve.tensor_scalar(ab[:, 1, :], flat, TOPK - 1, None, ALU.bitwise_and))
                step(dve.tensor_copy(ab_f[:], ab[:]))
                of = idx_f[:, t].rearrange("p (h two) n -> p h two n", two=2)
                for part in range(2):
                    step(dve.tensor_tensor(hot[:].rearrange("p h n a -> p (h n) a"),
                                           ab_f[:, part, :].unsqueeze(2).broadcast_to([P, P, TOPK]),
                                           k["iota"][:, 0:TOPK].unsqueeze(1).broadcast_to([P, P, TOPK]), ALU.is_equal))
                    step(dve.tensor_tensor(hot[:], hot[:], of[:, :, part, :].unsqueeze(2).broadcast_to(four_d), ALU.mult))
                    step(dve.tensor_reduce(pick[:, t, part, :], hot[:].rearrange("p h n a -> p (h n) a"), AX.X, ALU.add))
                gate = pick[:, t, 2, :].rearrange("p (h n) -> p h n", h=PHEADS)
                three = [P, PHEADS, TOPK]
                dve.tensor_tensor(gate, top[:, t], top[:, t, :, 0:1].broadcast_to(three), ALU.subtract).then_inc(shifted, 1)
                dve.wait_ge(exped, t + 1)
                step(dve.tensor_reduce(total[:], gate, AX.X, ALU.add))
                step(dve.reciprocal(total[:], total[:]))
                dve.tensor_tensor(gate, gate, total[:].unsqueeze(2).broadcast_to(three), ALU.mult).then_inc(picked, 1)
            for t in range(TT):
                dve.wait_ge(turned, t + 1)
                step(dve.tensor_copy(chosen[:, :, t * P:(t + 1) * P],
                                     psum[:, t, 0:3 * P].rearrange("p (c s) -> p c s", c=3)))

        @block.scalar
        def _(act):
            for t in range(TT):
                act.wait_ge(shifted, t + 1)
                act.activation(pick[:, t, 2, :], pick[:, t, 2, :], ACT.Exp).then_inc(exped, 1)

        @block.tensor
        def _(pe):
            for t in range(TT):
                pe.wait_ge(picked, t + 1)
                for c in range(3):
                    last = pe.transpose(psum[:, t, c * P:(c + 1) * P], pick[:, t, c, :], k["ident"][:])
                last.then_inc(turned, 1)


def peer_table(nc, k, chosen, table):
    per = 4
    quads = S // per
    with Stage(nc, "table") as st:
        first = st.sb("first", [P, 4, per, NKEYS])
        second = st.sb("second", [P, 4, per, NKEYS])
        psum = st.ps("psum", [P, 4, CW])
        hot, product, stored = (st.sem(n) for n in ("hot", "product", "stored"))
        block = st.block()

        @block.vector
        def _(dve):
            def one_hot(i, b, early=False):
                if not early:
                    dve.wait_ge(product, i - 3)
                wide = [P, per, NKEYS]
                key = chosen[:, 0, bass.ds(i * per, per)]
                dve.tensor_tensor(first[:, b], key.unsqueeze(2).broadcast_to(wide),
                                  k["iota"][:].unsqueeze(1).broadcast_to(wide), ALU.is_equal)
                for j in range(per):
                    key, gate = [chosen[:, c, bass.ds(i * per + j, 1)] for c in (1, 2)]
                    last = dve.tensor_scalar(second[:, b, j, :], k["iota"][:], key, gate, ALU.is_equal, ALU.mult)
                last.then_inc(hot, 1)

            for i in range(4):
                one_hot(i, i, early=True)
            with dve.Fori(1, quads // 4) as r:
                for b in range(4):
                    one_hot(r * 4 + b, b)

        @block.tensor
        def _(pe):
            def products(i, bank, early=False):
                pe.wait_ge(hot, i + 1)
                if not early:
                    pe.wait_ge(stored, i - 3)
                for j in range(per):
                    last = pe.matmul(psum[:, bank, j * P:(j + 1) * P], first[:, bank, j, :], second[:, bank, j, :],
                                     start=True, stop=True)
                last.then_inc(product, 1)

            for i in range(4):
                products(i, i, early=True)
            with pe.Fori(1, quads // 4) as r:
                for b in range(4):
                    products(r * 4 + b, b)

        @block.scalar
        def _(act):
            with act.Fori(0, quads // 4) as r:
                for b in range(4):
                    act.wait_ge(product, r * 4 + (b + 1))
                    act.copy(table[:, :, bass.ds((r * 4 + b) * per, per)].rearrange("p n t -> p t n"),
                             psum[:, b, :].rearrange("p (t n) -> p t n", t=per)).then_inc(stored, 1)


def final_norm(nc, ins, x, g, junk, out):
    with Stage(nc, "final") as st:
        ss = st.sb("ss", [P, TT])
        loaded, squared, mean_ready, root_ready, ready, stored, dve_done = (
            st.sem(n) for n in ("loaded", "squared", "mean_ready", "root_ready", "ready", "stored", "dve_done"))
        block = st.block()

        @block.sync
        def _(sp):
            sp.dma_start(g, ins["final_g"].partition_broadcast(P)).then_inc(loaded, 16)
            for t in range(TT):
                sp.wait_ge(ready, t + 1)
                sp.dma_start(out[t * P:(t + 1) * P, :], x[:, t, :]).then_inc(stored, 16)
            sp.wait_ge(stored, 16 * TT)

        @block.scalar
        def _(act):
            for t in range(TT):
                act.activation(junk, x[:, t, :], ACT.Square, accum_out=ss[:, t:t + 1]).then_inc(squared, 1)
                act.wait_ge(squared, t + 1)
            act.wait_ge(mean_ready, 1)
            act.activation(ss[:], ss[:], ACT.Sqrt).then_inc(root_ready, 1)

        @block.vector
        def _(dve):
            step = InOrder(dve, dve_done)
            dve.wait_ge(squared, TT)
            dve.tensor_scalar(ss[:], ss[:], 1.0 / D, EPS, ALU.mult, ALU.add).then_inc(mean_ready, 1)
            dve.wait_ge(root_ready, 1)
            step(dve.reciprocal(ss[:], ss[:]))
            dve.wait_ge(loaded, 16)
            for t in range(TT):
                dve.scalar_tensor_tensor(x[:, t, :], x[:, t, :], ss[:, t:t + 1], g, ALU.mult,
                                         ALU.mult).then_inc(ready, 1)


def keep(nc, copies):
    with Stage(nc, "keep") as st:
        stored = st.sem("stored")
        block = st.block()

        @block.sync
        def _(sp):
            for dram, tile in copies:
                sp.dma_start(dram, tile).then_inc(stored, 16)
            sp.wait_ge(stored, 16 * len(copies))




def program(nc, ins, out):
    x_kept = nc.dram_tensor("x_kept", (P, TT, D), F32, kind="Internal").ap()
    gate_kept = nc.dram_tensor("gate_kept", (P, D), F32, kind="Internal").ap()
    with Stage(nc, "all") as pst:
        k = {name: pst.sb(name, [P, P]) for name in ("ident", "ones", "iota")}
        h_hi, h_lo = (pst.sb(n, [P, KT, S], F32R) for n in ("h_hi", "h_lo"))
        k["h_hi"], k["h_lo"] = h_hi, h_lo
        chosen = pst.sb("chosen", [P, 3, S])
        with Stage(nc, "main") as ms:
            constants(nc, ms, ins, k)
            mods = [ms.sb(f"mod{i}", [P, 6 * D]) for i in range(2)]
            modc = ms.sb("modc", [P, 2 * D])
            sparse_layer(nc, k, ins, mods[0], mods[1])
            diff_layer(nc, k, ins, mods[1], mods[0], modc)
            mod = mods[0]
            delta_layer(nc, k, ins, mod, modc, mods[1])
            m = [mod[:, i * D:(i + 1) * D] for i in range(6)]
            h_t = modc[:].rearrange("p (c s) -> p c s", c=KT)
            normed(nc, k, "pnorm", k["x"], ins["norm_g2"][1], m[3], m[4], h_t)
            keep(nc, [(x_kept, k["x"][:]), (gate_kept, m[5])])
            with Stage(nc, "pr") as ps:
                scores = ps.sb("scores", [P, TT, 16, NKEYS])
                peer_scores(nc, k, ins, h_t, scores)
                peer_route(nc, k, scores, chosen)
        with Stage(nc, "peer") as st:
            table = st.sb("table", [P, NKEYS, S])
            peer_table(nc, k, chosen, table)
            streamed_mlp(nc, k, "experts", ins["peer_u"], ins["peer_v"], "peer", (h_hi, h_lo),
                         kept=(x_kept, gate_kept), table=table, then=lambda x, rest: final_norm(nc, ins, x, rest[:, 0, :], rest[:, 1, :], out))




def _column_tiles(w, width=WIDE):
    n = w.shape[1] // width
    return w.reshape(KT, P, n, width).transpose(2, 1, 0, 3).reshape(n, P, KT * width)


def _hidden_tiles(matrices):
    n = matrices[0].shape[1] // P
    return np.concatenate([m.reshape(KT, P, n, P).transpose(2, 1, 0, 3).reshape(n, P, KT * P) for m in matrices],
                          axis=2)


def _layout(a):
    a = {name: np.asarray(v) for name, v in a.items()}
    slots = np.array([b + 4 * g for b in range(4) for g in range(2)])
    w = a["sp_w_in"][0]
    nq = w[:, Z_NQ:Z_KV].reshape(D, HEADS, HEAD)[:, slots].reshape(D, -1)
    ng = w[:, Z_GATE:].reshape(D, 3, HEADS)[:, :, slots].reshape(D, -1)
    w = np.concatenate([w[:, :Z_NQ], nq, w[:, Z_KV:Z_GATE], ng], axis=1)
    whole = SP_IN // WIDE * WIDE
    out = {"x": a["x"][0], "positions": a["positions"].reshape(TT, P).T, "sp_w_in": _column_tiles(w[:, :whole]),
           "sp_w_in_tail": _column_tiles(w[:, whole:], SP_IN - whole)[0]}
    wo = a["sp_w_out"][0].reshape(2, HEADS, HEAD, D)
    wo = np.concatenate([wo[0], wo[1][slots]]).reshape(D, D)
    out["sp_w_out"] = _column_tiles(wo)
    for i in range(2):
        out[f"ada_w{i}"] = _column_tiles(a["ada_w"][i], CW // 2).reshape(24, P, KT, CW // 2)
        out[f"ada_b{i}"] = a["ada_b"][i]
        out[f"attn_norm{i}"] = a["attn_norm"][i]
        out[f"ffn_norm{i}"] = a["ffn_norm"][i]
        out[f"ffn_columns{i}"] = _hidden_tiles([a["ffn_w_gate"][i], a["ffn_w_up"][i]])
        out[f"ffn_rows{i}"] = a["ffn_w_down"][i].reshape(FFN_CHUNKS, P, D)
    out["c"] = a["c"].reshape(KT, P).T
    out["moba_q_norm"], out["moba_k_norm"] = a["moba_q_norm"][0], a["moba_k_norm"][0]
    out["nsa_q_norm"], out["nsa_k_norm"] = a["nsa_q_norm"][0], a["nsa_k_norm"][0]
    out["cmp_pos"] = a["nsa_cmp_pos"][0].transpose(2, 0, 1)
    out["cmp_w1"] = a["nsa_cmp_w1"][0].transpose(0, 2, 1, 3)
    out["cmp_w2"] = a["nsa_cmp_w2"][0].reshape(2, 2, P, HEAD).transpose(2, 0, 1, 3)
    out["diff_w_in"], out["diff_w_out"] = _column_tiles(a["diff_w_in"][0]), _column_tiles(a["diff_w_out"][0])
    out["diff_q_norm"], out["diff_k_norm"] = a["diff_q_norm"][0], a["diff_k_norm"][0]
    out["diff_lambda"], out["diff_out_norm"] = a["diff_lambda"][0].reshape(-1), a["diff_out_norm"][0]
    out["ada_w2"], out["ada_b2"] = _column_tiles(a["ada_w_2"][0], CW // 2).reshape(24, P, KT, CW // 2), a["ada_b_2"][0]
    out["c2"], out["c_ctx2"] = a["c_2"].reshape(KT, P).T, a["c_ctx_2"].reshape(KT, P).T
    out["ctx"], out["norm_g2"] = a["ctx_2"][0], a["norm_g_2"][0]
    dn = a["dn_w_in_2"][0]
    out["dn_w_qkv"] = _column_tiles(dn[:, :3 * D], P)
    out["dn_w_gate"] = _column_tiles(dn[:, 3 * D:4 * D])
    out["dn_w_ba"] = _column_tiles(dn[:, 4 * D:], 4 * DN_HEADS)[0]
    out["dn_conv"] = a["dn_conv_w_2"][0].reshape(DN_CONV, 3 * KT, P).transpose(2, 1, 0)
    out["dn_a_log"], out["dn_dt_bias"] = a["dn_a_log_2"][0].reshape(-1), a["dn_dt_bias_2"][0].reshape(-1)
    out["dn_norm_g"], out["dn_w_out"] = a["dn_norm_g_2"][0], _column_tiles(a["dn_w_out_2"][0])
    out["peer_w_q"] = _column_tiles(a["peer_w_q_2"][0])
    out["peer_keys"] = a["peer_keys_2"][0].reshape(16, NKEYS, P).transpose(2, 0, 1)
    out["peer_u"] = a["peer_u_2"][0].reshape(NKEYS, NKEYS, KT, P).transpose(1, 3, 2, 0).reshape(NKEYS, P, KT * P)
    out["peer_v"] = a["peer_v_2"][0].reshape(NKEYS, NKEYS, D).transpose(1, 0, 2)
    out["final_g"] = a["final_g_2"]
    return {name: np.ascontiguousarray(v) for name, v in out.items()}


def kernel(**inputs):
    import concourse.bacc as _bacc
    from concourse.bass_utils import run_bass_kernel_spmd as _run

    nc = _bacc.Bacc("TRN2", target_bir_lowering=False, num_devices=1)
    arrays, aps = {}, {}
    for name, a in _layout(inputs).items():
        arrays[f"in_{name}"] = a
        aps[name] = nc.dram_tensor(f"in_{name}", a.shape, mybir.dt.from_np(a.dtype), kind="ExternalInput").ap()
    out = nc.dram_tensor("out_x", (S, D), F32, kind="ExternalOutput").ap()
    program(nc, aps, out)
    r = _run(nc, [arrays], core_ids=[0])
    return r.results[0]["out_x"].reshape(1, S, D)
```
